# Optimizing a Trainium2 kernel written in Bass

```python
import math
import jax, jax.numpy as jnp
from jax import lax
import numpy as np

D_MODEL = 1024
BATCH = 1
SEQ = 1024
DEPTH = 1

GDN_HEADS = 8
GDN_HEAD_DIM = 128
GDN_WIDTH = GDN_HEADS * GDN_HEAD_DIM
GDN_CHUNK = 64
CONV_K = 5
DIL_GROUPS = ((128, 1), (512, 4), (2048, 16))
DIL_N_GROUPS = 3
DIL_HEADS_PER_GROUP = 4
DIL_HEADS = DIL_N_GROUPS * DIL_HEADS_PER_GROUP
DIL_HEAD_DIM = 128
DIL_WIDTH = DIL_HEADS * DIL_HEAD_DIM
DIL_OUT_WIDTH = DIL_HEADS_PER_GROUP * DIL_HEAD_DIM
DIL_BLOCK = 64
REL_BUCKETS = 32
REL_MAX_DIST = 1024
D_FF = 4 * D_MODEL
EPS = 1e-6
NEG = -1e30

C_QA = 0
C_KA = C_QA + GDN_WIDTH
C_VA = C_KA + GDN_WIDTH
C_ZA = C_VA + GDN_WIDTH
C_AF = C_ZA + GDN_WIDTH
C_AB = C_AF + GDN_HEADS
C_BF = C_AB + GDN_HEADS
C_BB = C_BF + GDN_HEADS
C_QB = C_BB + GDN_HEADS
C_KB = C_QB + DIL_WIDTH
C_VB = C_KB + DIL_WIDTH
C_GA = C_VB + DIL_WIDTH
C_GB = C_GA + D_MODEL
IN_COLS = C_GB + D_MODEL


def _rmsnorm(x, w):
    xf = x.astype(jnp.float32)
    y = xf * lax.rsqrt(jnp.mean(xf * xf, axis=-1, keepdims=True) + EPS) * w.astype(jnp.float32)
    return y.astype(x.dtype)

def _l2norm(x):
    return x * lax.rsqrt(jnp.sum(x * x, axis=-1, keepdims=True) + EPS)

def _t5_bucket(rel):
    nb = REL_BUCKETS // 2
    ret = (rel > 0).astype(np.int32) * nb
    n = np.abs(rel)
    max_exact = nb // 2
    large = max_exact + (np.log(np.maximum(n, 1) / max_exact) / math.log(REL_MAX_DIST / max_exact)
                         * (nb - max_exact)).astype(np.int32)
    large = np.minimum(large, nb - 1)
    return ret + np.where(n < max_exact, n, large).astype(np.int32)

def _chunk_gated_delta(q, k, v, g, beta):
    b, s, h, dk = q.shape
    dv = v.shape[-1]
    n = s // GDN_CHUNK

    def chunks(t):
        return jnp.moveaxis(t.reshape(b, n, GDN_CHUNK, h, -1), 3, 1)

    qc, kc, vc = chunks(q), chunks(k), chunks(v)
    gc = jnp.cumsum(chunks(g[..., None])[..., 0], axis=-1)
    bc = chunks(beta[..., None])
    tri = np.tril(np.ones((GDN_CHUNK, GDN_CHUNK), bool))
    strict = np.tril(np.ones((GDN_CHUNK, GDN_CHUNK), bool), -1)
    dd = gc[..., :, None] - gc[..., None, :]
    gam = jnp.where(tri, jnp.exp(jnp.where(tri, dd, 0.0)), 0.0)
    kb = kc * bc
    a_kk = jnp.where(strict, jnp.einsum('bhnic,bhnjc->bhnij', kb, kc) * gam, 0.0)
    eye = jnp.eye(GDN_CHUNK, dtype=a_kk.dtype)
    rhs = jnp.concatenate([vc * bc, kb * jnp.exp(gc)[..., None]], axis=-1)
    sol = lax.linalg.triangular_solve(a_kk + eye, rhs, left_side=True, lower=True,
                                      unit_diagonal=True)
    u, w = sol[..., :dv], sol[..., dv:]
    a_qk = jnp.einsum('bhnic,bhnjc->bhnij', qc, kc) * gam

    def step(state, inp):
        qn, kn, un, wn, gn, aqk = inp
        v_new = un - jnp.einsum('bhck,bhkv->bhcv', wn, state)
        o = (jnp.einsum('bhck,bhkv->bhcv', qn * jnp.exp(gn)[..., None], state)
             + jnp.einsum('bhij,bhjv->bhiv', aqk, v_new))
        g_last = gn[..., -1]
        state = (state * jnp.exp(g_last)[..., None, None]
                 + jnp.einsum('bhck,bhcv->bhkv', kn * jnp.exp(g_last[..., None] - gn)[..., None], v_new))
        return state, o

    xs = tuple(jnp.moveaxis(t, 2, 0) for t in (qc, kc, u, w, gc, a_qk))
    state0 = jnp.zeros((b, h, dk, dv), jnp.float32)
    _, o = lax.scan(step, state0, xs)
    o = jnp.moveaxis(o, 0, 2)
    return jnp.moveaxis(o, 1, 3).reshape(b, s, h, dv)

def _dilated_group(q, k, v, bias, dil, half):
    b, s, h, hd = q.shape
    blk = DIL_BLOCK
    L = s // dil
    nb = -(-L // blk)
    lp = nb * blk

    def res(t):
        return t.reshape(b, L, dil, h, hd).transpose(0, 2, 1, 3, 4)

    qr = jnp.pad(res(q), ((0, 0), (0, 0), (0, lp - L), (0, 0), (0, 0))).reshape(b, dil, nb, blk, h, hd)

    def win(t):
        tp = jnp.pad(res(t), ((0, 0), (0, 0), (blk, lp - L + blk), (0, 0), (0, 0)))
        tp = tp.reshape(b, dil, nb + 2, blk, h, hd)
        return jnp.concatenate([tp[:, :, :-2], tp[:, :, 1:-1], tp[:, :, 2:]], axis=3)

    kw, vw = win(k), win(v)
    off = np.arange(3 * blk)[None, :] - blk - np.arange(blk)[:, None]
    band = np.abs(off) <= half
    key_pos = np.arange(nb)[:, None] * blk - blk + np.arange(3 * blk)[None, :]
    key_ok = (key_pos >= 0) & (key_pos < L)
    mask = band[None] & key_ok[:, None, :]
    logits = (jnp.einsum('brnqhc,brnkhc->brnhqk', qr, kw) * (hd ** -0.5)
              + bias.astype(jnp.float32))
    logits = jnp.where(mask[:, None], logits, NEG)
    lse = jax.nn.logsumexp(logits, axis=-1)
    p = jnp.exp(logits - lse[..., None])
    o = jnp.einsum('brnhqk,brnkhc->brnqhc', p, vw).reshape(b, dil, lp, h, hd)[:, :, :L]
    o = o.transpose(0, 2, 1, 3, 4).reshape(b, s, h, hd)
    lse = lse.transpose(0, 1, 2, 4, 3).reshape(b, dil, lp, h)[:, :, :L]
    lse = lse.transpose(0, 2, 1, 3).reshape(b, s, h)
    return o, lse

def _gdn_decay(a, a_log, dt_bias):
    return -jnp.exp(a_log.astype(jnp.float32)) * jax.nn.softplus(a + dt_bias.astype(jnp.float32))

def first_inputs(seed: int = 0) -> dict:
    key = jax.random.key(seed)
    ks = jax.random.split(key, 24)
    f32 = jnp.float32

    def nrm(k, shape, scale):
        return jax.random.normal(k, shape, f32) * scale

    def gain(k, shape):
        return 1.0 + 0.05 * jax.random.normal(k, shape, f32)

    dt = jnp.exp(jax.random.uniform(ks[6], (2, DEPTH, GDN_HEADS), f32, math.log(1e-3), math.log(1e-1)))
    dt_bias = dt + jnp.log(-jnp.expm1(-dt))
    a_log = jnp.log(jax.random.uniform(ks[7], (2, DEPTH, GDN_HEADS), f32, 1.0, 16.0))
    return {
        "x": jax.random.normal(ks[0], (BATCH, SEQ, D_MODEL), f32),
        "rel_bias": nrm(ks[1], (REL_BUCKETS, DIL_HEADS), 0.5),
        "ln_mix_pre": gain(ks[2], (DEPTH, D_MODEL)),
        "w_in": nrm(ks[3], (DEPTH, D_MODEL, IN_COLS), D_MODEL ** -0.5),
        "conv_w": nrm(ks[4], (DEPTH, CONV_K, 3 * GDN_WIDTH), CONV_K ** -0.5),
        "a_log_f": a_log[0],
        "a_log_b": a_log[1],
        "dt_bias_f": dt_bias[0],
        "dt_bias_b": dt_bias[1],
        "norm_a": gain(ks[5], (DEPTH, GDN_HEAD_DIM)),
        "w_branch_a": nrm(ks[8], (DEPTH, GDN_WIDTH, D_MODEL), GDN_WIDTH ** -0.5),
        "w_branch_b": nrm(ks[9], (DEPTH, DIL_OUT_WIDTH, D_MODEL), DIL_OUT_WIDTH ** -0.5),
        "w_out": nrm(ks[10], (DEPTH, D_MODEL, D_MODEL), D_MODEL ** -0.5),
        "ln_mix_post": gain(ks[11], (DEPTH, D_MODEL)),
        "ln_mlp_pre": gain(ks[12], (DEPTH, D_MODEL)),
        "w_ff1": nrm(ks[13], (DEPTH, D_MODEL, D_FF), D_MODEL ** -0.5),
        "w_ff2": nrm(ks[14], (DEPTH, D_FF, D_MODEL), D_FF ** -0.5),
        "ln_mlp_post": gain(ks[15], (DEPTH, D_MODEL)),
    }

def first_block(x, rel_bias, ln_mix_pre, w_in, conv_w, a_log_f, a_log_b, dt_bias_f, dt_bias_b,
              norm_a, w_branch_a, w_branch_b, w_out, ln_mix_post, ln_mlp_pre, w_ff1, w_ff2,
              ln_mlp_post):
    b, s, _ = x.shape
    f32 = jnp.float32
    blk = DIL_BLOCK
    off = np.arange(3 * blk)[None, :] - blk - np.arange(blk)[:, None]
    group_bias = []
    for gi, (window, dil) in enumerate(DIL_GROUPS):
        bt = rel_bias[_t5_bucket(off * dil)]
        hs = slice(gi * DIL_HEADS_PER_GROUP, (gi + 1) * DIL_HEADS_PER_GROUP)
        group_bias.append(jnp.transpose(bt[:, :, hs], (2, 0, 1)))

    for l in range(DEPTH):
        h = _rmsnorm(x, ln_mix_pre[l])
        proj = jnp.einsum('bsd,dc->bsc', h, w_in[l]).astype(f32)

        qkv = lax.conv_general_dilated(
            proj[..., C_QA:C_ZA], conv_w[l].astype(f32)[:, None, :], window_strides=(1,),
            padding=[(CONV_K // 2, CONV_K // 2)], dimension_numbers=('NWC', 'WIO', 'NWC'),
            feature_group_count=3 * GDN_WIDTH)
        qkv = jax.nn.silu(qkv)
        qa = _l2norm(qkv[..., :GDN_WIDTH].reshape(b, s, GDN_HEADS, GDN_HEAD_DIM)) * (GDN_HEAD_DIM ** -0.5)
        ka = _l2norm(qkv[..., GDN_WIDTH:2 * GDN_WIDTH].reshape(b, s, GDN_HEADS, GDN_HEAD_DIM))
        va = qkv[..., 2 * GDN_WIDTH:].reshape(b, s, GDN_HEADS, GDN_HEAD_DIM)
        g_f = _gdn_decay(proj[..., C_AF:C_AB], a_log_f[l], dt_bias_f[l])
        g_b = _gdn_decay(proj[..., C_AB:C_BF], a_log_b[l], dt_bias_b[l])
        beta_f = jax.nn.sigmoid(proj[..., C_BF:C_BB])
        beta_b = jax.nn.sigmoid(proj[..., C_BB:C_QB])
        flip = lambda t: jnp.flip(t, axis=1)
        o_a = (_chunk_gated_delta(qa, ka, va, g_f, beta_f)
               + flip(_chunk_gated_delta(flip(qa), flip(ka), flip(va), flip(g_b), flip(beta_b))))
        z = proj[..., C_ZA:C_AF].reshape(b, s, GDN_HEADS, GDN_HEAD_DIM)
        o_a = _rmsnorm(o_a, norm_a[l]) * jax.nn.silu(z)
        o_a = o_a.reshape(b, s, GDN_WIDTH).astype(x.dtype)

        qb = proj[..., C_QB:C_KB].reshape(b, s, DIL_HEADS, DIL_HEAD_DIM)
        kb = proj[..., C_KB:C_VB].reshape(b, s, DIL_HEADS, DIL_HEAD_DIM)
        vb = proj[..., C_VB:C_GA].reshape(b, s, DIL_HEADS, DIL_HEAD_DIM)
        outs, lses = [], []
        for gi, (window, dil) in enumerate(DIL_GROUPS):
            hs = slice(gi * DIL_HEADS_PER_GROUP, (gi + 1) * DIL_HEADS_PER_GROUP)
            o_g, lse_g = _dilated_group(qb[:, :, hs], kb[:, :, hs], vb[:, :, hs], group_bias[gi],
                                        dil, window // (2 * dil))
            outs.append(o_g)
            lses.append(lse_g)
        wgt = jax.nn.softmax(jnp.stack(lses, axis=0), axis=0)
        o_b = jnp.sum(wgt[..., None] * jnp.stack(outs, axis=0), axis=0)
        o_b = o_b.reshape(b, s, DIL_OUT_WIDTH).astype(x.dtype)

        gate_a = jax.nn.sigmoid(proj[..., C_GA:C_GB]).astype(x.dtype)
        gate_b = jax.nn.sigmoid(proj[..., C_GB:IN_COLS]).astype(x.dtype)
        merged = (gate_a * jnp.einsum('bsc,cd->bsd', o_a, w_branch_a[l])
                  + gate_b * jnp.einsum('bsc,cd->bsd', o_b, w_branch_b[l]))
        y = jnp.einsum('bsd,de->bse', merged, w_out[l])
        x = x + _rmsnorm(y, ln_mix_post[l])

        h2 = _rmsnorm(x, ln_mlp_pre[l])
        f = jnp.square(jax.nn.relu(jnp.einsum('bsd,df->bsf', h2, w_ff1[l])))
        f = jnp.einsum('bsf,fd->bsd', f, w_ff2[l])
        x = x + _rmsnorm(f, ln_mlp_post[l])
    return x


CHUNK = 64
N_META = 16
D_MIX = D_MODEL
D_LRU = D_MIX // 2
D_ATT = D_MIX - D_LRU
N_ATT_HEADS = 4
ATT_VDIM = D_ATT // N_ATT_HEADS
ATT_QKDIM = ATT_VDIM // 2
D_QK = N_ATT_HEADS * 2 * ATT_QKDIM
ROT_DIM = ATT_QKDIM // 4
ROPE_THETA = 500000.0
N_LRU_BLOCKS = 8
LRU_BLOCK = D_LRU // N_LRU_BLOCKS
CONV_W = 4
LRU_C = 8.0
Q_BLOCK = 128
SUBLN_EPS = 1e-5
D_IN = 2 * D_QK + D_ATT + D_ATT + D_LRU + D_LRU


def rms_norm(x, w, eps):
    xf = x.astype(jnp.float32)
    y = xf * lax.rsqrt(jnp.mean(xf * xf, axis=-1, keepdims=True) + eps)
    return (y * w.astype(jnp.float32)).astype(x.dtype)

def rope_tables(T):
    pos = jnp.arange(T, dtype=jnp.float32)
    inv = jnp.power(ROPE_THETA, -jnp.arange(0, ROT_DIM, 2, dtype=jnp.float32) / ROT_DIM)
    ang = pos[:, None] * inv[None, :]
    return jnp.cos(ang), jnp.sin(ang)

def apply_partial_rope(x, cos, sin):
    xr = x[..., :ROT_DIM].astype(jnp.float32)
    x1, x2 = xr[..., : ROT_DIM // 2], xr[..., ROT_DIM // 2:]
    c = cos[None, :, None, :]
    s = sin[None, :, None, :]
    rot = jnp.concatenate([x1 * c - x2 * s, x2 * c + x1 * s], axis=-1)
    return jnp.concatenate([rot.astype(x.dtype), x[..., ROT_DIM:]], axis=-1)

def chunk_ids(T):
    p = jnp.arange(T)
    return jnp.where(p < N_META, 0, (p - N_META) // CHUNK + 1)

def chunk_end(p):
    if p < N_META:
        return N_META
    return N_META + ((p - N_META) // CHUNK + 1) * CHUNK

def diff_attention(q, k, v, lam, cid):
    T = q.shape[1]
    scale = ATT_QKDIM ** -0.5
    outs = []
    for s in range(0, T, Q_BLOCK):
        e = min(s + Q_BLOCK, T)
        kend = min(chunk_end(e - 1), T)
        qb, kb, vb = q[:, s:e], k[:, :kend], v[:, :kend]
        scores = jnp.einsum('bqhmd,bkhmd->bhmqk', qb, kb).astype(jnp.float32) * scale
        mask = cid[s:e, None] >= cid[None, :kend]
        scores = jnp.where(mask[None, None, None], scores, -jnp.inf)
        p = jax.nn.softmax(scores, axis=-1)
        w = p[:, :, 0] - lam * p[:, :, 1]
        outs.append(jnp.einsum('bhqk,bkhd->bqhd', w.astype(vb.dtype), vb))
    return jnp.concatenate(outs, axis=1)

def rg_lru(x, w_r, b_r, w_i, b_i, lru_L):
    B, T, C = x.shape
    xb = x.reshape(B, T, N_LRU_BLOCKS, LRU_BLOCK)
    r = jax.nn.sigmoid(jnp.einsum('btnc,ncd->btnd', xb, w_r).reshape(B, T, C) + b_r)
    i = jax.nn.sigmoid(jnp.einsum('btnc,ncd->btnd', xb, w_i).reshape(B, T, C) + b_i)
    log_a = -LRU_C * r.astype(jnp.float32) * jax.nn.softplus(-lru_L.astype(jnp.float32))
    a = jnp.exp(log_a)
    mult = jnp.sqrt(-jnp.expm1(2.0 * log_a))
    mult = mult.at[:, 0].set(1.0)
    b = mult * (i * x).astype(jnp.float32)

    def combine(left, right):
        a1, b1 = left
        a2, b2 = right
        return a1 * a2, a2 * b1 + b2

    _, h = lax.associative_scan(combine, (a, b), axis=1)
    return h.astype(x.dtype)

def hybrid_layer(h, norm_w, w_in, conv_w, conv_b, w_r, b_r, w_i, b_i, lru_L,
                 lq1, lk1, lq2, lk2, subln_w, w_out, lam_init, cos, sin, cid):
    B, T, _ = h.shape
    u = rms_norm(h, norm_w, EPS)
    proj = u @ w_in
    q, k, v, g_att, x_lru, g_lru = jnp.split(
        proj, [D_QK, 2 * D_QK, 2 * D_QK + D_ATT, 2 * D_QK + 2 * D_ATT,
               2 * D_QK + 2 * D_ATT + D_LRU], axis=-1)

    q = apply_partial_rope(q.reshape(B, T, 2 * N_ATT_HEADS, ATT_QKDIM), cos, sin)
    k = apply_partial_rope(k.reshape(B, T, 2 * N_ATT_HEADS, ATT_QKDIM), cos, sin)
    q = q.reshape(B, T, N_ATT_HEADS, 2, ATT_QKDIM)
    k = k.reshape(B, T, N_ATT_HEADS, 2, ATT_QKDIM)
    v = v.reshape(B, T, N_ATT_HEADS, ATT_VDIM)
    lam = (jnp.exp(jnp.sum(lq1.astype(jnp.float32) * lk1.astype(jnp.float32)))
           - jnp.exp(jnp.sum(lq2.astype(jnp.float32) * lk2.astype(jnp.float32)))
           + lam_init)
    o = diff_attention(q, k, v, lam, cid)
    o = rms_norm(o, subln_w, SUBLN_EPS) * (1.0 - lam_init)
    att_out = o.reshape(B, T, D_ATT) * jax.nn.silu(g_att)

    xc = lax.conv_general_dilated(
        x_lru, conv_w[:, None, :], window_strides=(1,), padding=[(CONV_W - 1, 0)],
        dimension_numbers=('NWC', 'WIO', 'NWC'), feature_group_count=D_LRU) + conv_b
    y = rg_lru(xc, w_r, b_r, w_i, b_i, lru_L)
    lru_out = y * jax.nn.silu(g_lru)

    mixed = jnp.concatenate([att_out, lru_out], axis=-1)
    return h + mixed @ w_out

def second_inputs(seed: int = 0) -> dict:
    key = jax.random.key(seed)
    ks = jax.random.split(key, 20)
    f32 = jnp.float32
    x = jax.random.normal(ks[0], (BATCH, SEQ, D_MODEL), f32)
    meta_tokens = jax.random.normal(ks[1], (N_META, D_MODEL), f32)
    norm_w = 1.0 + 0.02 * jax.random.normal(ks[2], (DEPTH, D_MODEL), f32)
    w_in = jax.random.normal(ks[3], (DEPTH, D_MODEL, D_IN), f32) * D_MODEL ** -0.5
    conv_w = jax.random.normal(ks[4], (DEPTH, CONV_W, D_LRU), f32) * CONV_W ** -0.5
    conv_b = 0.01 * jax.random.normal(ks[5], (DEPTH, D_LRU), f32)
    w_rgate = jax.random.normal(ks[6], (DEPTH, N_LRU_BLOCKS, LRU_BLOCK, LRU_BLOCK), f32) * LRU_BLOCK ** -0.5
    b_rgate = 0.01 * jax.random.normal(ks[7], (DEPTH, D_LRU), f32)
    w_igate = jax.random.normal(ks[8], (DEPTH, N_LRU_BLOCKS, LRU_BLOCK, LRU_BLOCK), f32) * LRU_BLOCK ** -0.5
    b_igate = 0.01 * jax.random.normal(ks[9], (DEPTH, D_LRU), f32)
    u = jax.random.uniform(ks[10], (DEPTH, D_LRU), f32, 0.9, 0.999)
    s = u ** (1.0 / LRU_C)
    lru_L = jnp.log(s) - jnp.log1p(-s)
    lambda_q1 = 0.1 * jax.random.normal(ks[11], (DEPTH, ATT_QKDIM), f32)
    lambda_k1 = 0.1 * jax.random.normal(ks[12], (DEPTH, ATT_QKDIM), f32)
    lambda_q2 = 0.1 * jax.random.normal(ks[13], (DEPTH, ATT_QKDIM), f32)
    lambda_k2 = 0.1 * jax.random.normal(ks[14], (DEPTH, ATT_QKDIM), f32)
    subln_w = 1.0 + 0.02 * jax.random.normal(ks[15], (DEPTH, ATT_VDIM), f32)
    w_out = jax.random.normal(ks[16], (DEPTH, D_MIX, D_MODEL), f32) * D_MIX ** -0.5
    final_norm_w = 1.0 + 0.02 * jax.random.normal(ks[17], (D_MODEL,), f32)
    return {"x": x, "meta_tokens": meta_tokens, "norm_w": norm_w, "w_in": w_in,
            "conv_w": conv_w, "conv_b": conv_b, "w_rgate": w_rgate, "b_rgate": b_rgate,
            "w_igate": w_igate, "b_igate": b_igate, "lru_L": lru_L,
            "lambda_q1": lambda_q1, "lambda_k1": lambda_k1, "lambda_q2": lambda_q2,
            "lambda_k2": lambda_k2, "subln_w": subln_w, "w_out": w_out,
            "final_norm_w": final_norm_w}

def second_block(x, meta_tokens, norm_w, w_in, conv_w, conv_b, w_rgate, b_rgate, w_igate,
              b_igate, lru_L, lambda_q1, lambda_k1, lambda_q2, lambda_k2, subln_w, w_out,
              final_norm_w):
    B = x.shape[0]
    meta = jnp.broadcast_to(meta_tokens[None].astype(x.dtype), (B, N_META, D_MODEL))
    h = jnp.concatenate([meta, x], axis=1)
    T = h.shape[1]
    cos, sin = rope_tables(T)
    cid = chunk_ids(T)
    for l in range(DEPTH):
        lam_init = 0.8 - 0.6 * math.exp(-0.3 * l)
        h = hybrid_layer(h, norm_w[l], w_in[l], conv_w[l], conv_b[l], w_rgate[l], b_rgate[l],
                         w_igate[l], b_igate[l], lru_L[l], lambda_q1[l], lambda_k1[l],
                         lambda_q2[l], lambda_k2[l], subln_w[l], w_out[l], lam_init,
                         cos, sin, cid)
    h = rms_norm(h, final_norm_w, EPS)
    return h[:, N_META:]


_first_inputs = second_inputs


def second_inputs(seed=0):
    import zlib

    import numpy as np

    out = dict(_first_inputs(seed))
    spreads = {}
    factors = {'norm_w': 3.711,
     'conv_b': 22.92,
     'b_rgate': 200.0,
     'b_igate': 200.0,
     'lambda_k1': 3.247,
     'lambda_q2': 3.223,
     'lambda_k2': 4.826,
     'subln_w': 75.694,
     'final_norm_w': 23.697}
    for name, (base, spread) in spreads.items():
        noise = np.random.default_rng([zlib.crc32(name.encode()), seed]).standard_normal(out[name].shape)
        drawn = base * np.exp(spread * noise) if base else spread * noise
        out[name] = __import__('jax').numpy.asarray(drawn.astype(out[name].dtype))
    for name, factor in factors.items():
        out[name] = (out[name] * factor).astype(out[name].dtype)
    return out


_narrow_inputs = second_inputs


def second_inputs(seed=0):

    out = dict(_narrow_inputs(seed))
    wider = {'b_rgate': 3.58, 'b_igate': 3.68, 'subln_w': 3.22, 'final_norm_w': 3.23}
    for name, times in wider.items():
        mean = out[name].mean()
        out[name] = (mean + times * (out[name] - mean)).astype(out[name].dtype)
    return out


def setup_inputs(seed=0):
    out = dict(first_inputs(seed))
    for name, value in second_inputs(seed + 1).items():
        if name != "x":
            out[name + "_2"] = value
    return out


def reference(
    x, rel_bias, ln_mix_pre, w_in, conv_w, a_log_f, a_log_b, dt_bias_f, dt_bias_b, norm_a,
    w_branch_a, w_branch_b, w_out, ln_mix_post, ln_mlp_pre, w_ff1, w_ff2, ln_mlp_post,
    meta_tokens_2, norm_w_2, w_in_2, conv_w_2, conv_b_2, w_rgate_2, b_rgate_2, w_igate_2,
    b_igate_2, lru_L_2, lambda_q1_2, lambda_k1_2, lambda_q2_2, lambda_k2_2, subln_w_2, w_out_2,
    final_norm_w_2,
):
    x = first_block(
        x, rel_bias, ln_mix_pre, w_in, conv_w, a_log_f, a_log_b, dt_bias_f, dt_bias_b, norm_a,
        w_branch_a, w_branch_b, w_out, ln_mix_post, ln_mlp_pre, w_ff1, w_ff2, ln_mlp_post,
    )
    return second_block(
        x, meta_tokens_2, norm_w_2, w_in_2, conv_w_2, conv_b_2, w_rgate_2, b_rgate_2, w_igate_2,
        b_igate_2, lru_L_2, lambda_q1_2, lambda_k1_2, lambda_q2_2, lambda_k2_2, subln_w_2,
        w_out_2, final_norm_w_2,
    )


_drawn_inputs = setup_inputs


def setup_inputs(seed=0):
    import zlib

    import numpy as np

    out = dict(_drawn_inputs(seed))
    spreads = {}
    factors = {}
    for name, (base, spread) in spreads.items():
        noise = np.random.default_rng([zlib.crc32(name.encode()), seed]).standard_normal(out[name].shape)
        drawn = base * np.exp(spread * noise) if base else spread * noise
        out[name] = __import__('jax').numpy.asarray(drawn.astype(out[name].dtype))
    for name, factor in factors.items():
        out[name] = (out[name] * factor).astype(out[name].dtype)
    return out
```

```python
from contextlib import ExitStack

import numpy as np
import concourse.bass as bass
from concourse import mybir

ALU = mybir.AluOpType
ACT = mybir.ActivationFunctionType
AX = mybir.AxisListType
F32 = mybir.dt.float32
U8 = mybir.dt.uint8

P = 128
S = 1024
KT = 8
H = 8
EPS = 1e-6
NEG = -1e30
BIG = 1e30
SLOT = 2048
STOP = 99

MASKS = [1, 2, 4, 8, 16, 32, 64]


class Program:

    def __init__(self, nc, ctx):
        self.nc, self.ctx = nc, ctx
        self.names = ["tensor", "vector", "scalar", "gpsimd", "sync"]
        self.queue = {e: [] for e in self.names}
        self.sem = {e: ctx.enter_context(nc.semaphore("s_" + e)) for e in self.names}
        self.count = {e: 0 for e in self.names}
        self.seen = {e: {} for e in self.names}

    def channel(self, name):
        self.sem[name] = self.ctx.enter_context(self.nc.semaphore("d_" + name))
        self.count[name] = 0
        return name

    def waits(self, eng, deps):
        need = {}
        for name, n in flat(deps):
            if n > self.seen[eng].get(name, 0):
                need[name] = max(n, need.get(name, 0))
        for name, n in need.items():
            self.seen[eng][name] = n
            self.queue[eng].append(("wait", self.sem[name], n))

    def op(self, eng, fn, *deps):
        self.waits(eng, deps)
        self.queue[eng].append(("do", fn, self.sem[eng], 1))
        self.count[eng] += 1
        return (eng, self.count[eng])

    def quiet(self, eng, fn, *deps):
        self.waits(eng, deps)
        self.queue[eng].append(("do", fn, None, 0))

    def dma(self, eng, chan, out, in_, *deps):
        self.waits(eng, deps)
        self.queue[eng].append(("do", lambda e: e.dma_start(out, in_), self.sem[chan], 16))
        self.count[chan] += 16
        return (chan, self.count[chan])

    def now(self, *engs):
        return [(e, self.count[e]) for e in engs if self.count[e]]

    def pe(self, fn, *deps):
        return self.op("tensor", fn, *deps)

    def dve(self, fn, *deps):
        return self.op("vector", fn, *deps)

    def act(self, fn, *deps):
        return self.op("scalar", fn, *deps)

    def pool(self, fn, *deps):
        return self.op("gpsimd", fn, *deps)

    def emit(self, block):
        def play(name):
            def body(eng):
                for item in self.queue[name]:
                    if item[0] == "wait":
                        eng.wait_ge(item[1], item[2])
                    else:
                        ins = item[1](eng)
                        if item[2] is not None:
                            ins.then_inc(item[2], item[3])
            return body

        block.tensor(play("tensor"))
        block.vector(play("vector"))
        block.scalar(play("scalar"))
        block.gpsimd(play("gpsimd"))
        block.sync(play("sync"))


def flat(deps):
    for d in deps:
        if d is None:
            continue
        if isinstance(d, tuple) and len(d) == 2 and isinstance(d[0], str):
            yield d
        else:
            yield from flat(d)


class Weights:

    def __init__(self, p, src, places):
        self.p, self.src = p, src
        self.places = [(ap, p.channel(f"w{i}")) for i, ap in enumerate(places)]
        self.next = 0
        self.ready = []
        for pl in list(self.places):
            self.load(pl)

    def load(self, place, *deps):
        if self.next < self.src.shape[0]:
            ap, chan = place
            t = self.p.dma("sync", chan, ap, self.src[self.next], *deps)
            self.ready.append((place, t))
            self.next += 1

    def add(self, ap, *deps):
        place = (ap, self.p.channel(f"w{len(self.places)}"))
        self.places.append(place)
        self.load(place, *deps)

    def get(self):
        return self.ready.pop(0)

    def release(self, place, *deps):
        self.load(place, *deps)


def interleave(*threads):
    live = [[g, n, 0] for g, n in threads]
    while live:
        t = min(live, key=lambda t: (t[2] + 1) / t[1])
        try:
            next(t[0])
            t[2] += 1
        except StopIteration:
            live.remove(t)


def bc(ap, *shape):
    return ap.to_broadcast(list(shape))


def program(nc, x, wst, wab, cwt, vecs, gate, relb, meta, lam, lruw, cst, onehot, rope, msk, out, dbg):
    with ExitStack() as ctx:
        ar = ctx.enter_context(nc.sbuf_tensor("ar", [P, 52640], F32))
        mk = ctx.enter_context(nc.sbuf_tensor("mk", [P, 14, 128], U8))
        ps = ctx.enter_context(nc.psum_tensor("ps", [P, 4096], F32))
        sc_o = nc.dram_tensor("sc_o", [8, P, 1024], F32, kind="Internal").ap()
        sc_b = nc.dram_tensor("sc_b", [3, 1024, 520], F32, kind="Internal").ap()
        sc_t = nc.dram_tensor("sc_t", [12, P * 384 + 256], F32, kind="Internal").ap()
        p = Program(nc, ctx)

        def A(off, *shape):
            n = int(np.prod(shape))
            v = ar[:, off:off + n]
            if len(shape) == 2:
                v = v.rearrange("p (a b) -> p a b", a=shape[0])
            if len(shape) == 3:
                v = v.rearrange("p (a b c) -> p a b c", a=shape[0], b=shape[1])
            return v

        def bank(i, n=512):
            return ps[:, 512 * i:512 * i + n]

        ld = p.channel("ld")
        hT = A(0, KT, S)
        W = Weights(p, wst, [A(8192 + SLOT * i, SLOT) for i in range(4)])

        C0 = 16384
        ident, Um, Lm, MxF, MxB, ones = [A(C0 + 128 * i, 128) for i in range(6)]
        gates0 = C0 + 768
        names = ["g", "beta", "nbeta", "gc", "egl", "dec", "bgc", "tmpg"]
        gt = {n: A(gates0 + 128 * i, 8, 16) for i, n in enumerate(names)}
        V0 = gates0 + 1024
        cw = A(V0, 24, 5)
        vc = A(V0 + 120, 48)
        small = A(V0 + 168, 88)
        t_c = p.dma("scalar", ld, A(C0, 768), cst)
        t_c = p.dma("scalar", ld, cw[:, :, :], cwt)
        t_c = p.dma("scalar", ld, vc, vecs)
        mkf = A(18432 + 12288, 14, 128)
        t_c = p.dma("scalar", ld, mkf, msk)
        LNPRE, NORMA, LNMLP, NW2, SUB, CB, BR, BI, LRUL = 0, 8, 9, 17, 25, 26, 30, 34, 38
        R = 18432
        wabt = A(R, 8, 32)
        t_c = p.dma("scalar", ld, wabt, wab)
        dtb = A(R + 256, 32)
        t_c = p.dma("scalar", ld, dtb, gate.partition_broadcast(P))
        xin = A(R + 1024, 8, 1024)
        xl_tok = []
        for i in range(8):
            c = p.channel(f"x{i}")
            xl_tok.append(p.dma("scalar", c, xin[:, i, :], x[0, 128 * i:128 * i + 128, :]))
        t_cw = p.dve(lambda e: e.tensor_scalar(A(V0, 120), A(V0, 120), 0.5, None, ALU.mult), t_c)

        t_mk = p.dve(lambda e: e.tensor_copy(mk[:, :, :], mkf), t_c)
        mh_t = small[:, 81:82]
        t_m = p.pool(lambda e: e.memset(mh_t, -0.5))

        def rstd(ss, n, scale, *deps, eps=EPS):
            t = p.dve(lambda e: e.tensor_scalar(ss, ss, scale, eps, ALU.mult, ALU.add), *deps)
            return p.pool(lambda e: e.tensor_tensor(ss, ss, bc(mh_t, P, n), ALU.pow), t, t_m)

        def normed_transposed(src, tok, stat, dst, wcol, banks, free, junk, junk_free):
            t = p.act(lambda e: e.activation(junk, src, ACT.Square, accum_out=stat), tok, junk_free)
            t = rstd(stat, 1, 1.0 / 1024, t)
            t = p.dve(lambda e: e.tensor_scalar(junk, src, stat, None, ALU.mult), t)
            toks = []
            for hf in range(2):
                b = bank(banks[hf])
                for j in range(4):
                    kt = 4 * hf + j
                    tp = p.pe(lambda e, kt=kt, j=j, b=b: e.transpose(b[:, 128 * j:128 * j + 128], junk[:, 128 * kt:128 * kt + 128], ident), t, t_c, free[hf])
                ev = None
                for j in range(4):
                    kt = 4 * hf + j
                    ev = p.act(lambda e, kt=kt, j=j, b=b: e.activation(dst[:, kt, :], b[:, 128 * j:128 * j + 128], ACT.Copy, scale=vc[:, wcol + kt:wcol + kt + 1]), tp)
                toks.append(ev)
            return toks, tp

        free = {b: None for b in range(8)}
        junks = [A(R + 1024 + 8192 + 1024 * i, 1024) for i in range(2)]
        jf = [None, None]
        t_h = None
        for i in range(8):
            b0 = 2 * (i % 4)
            toks, tp = normed_transposed(xin[:, i, :], xl_tok[i], small[:, i:i + 1],
                                         hT[:, :, 128 * i:128 * i + 128], LNPRE, (b0, b0 + 1),
                                         (free[b0], free[b0 + 1]), junks[i % 2], jf[i % 2])
            free[b0], free[b0 + 1] = toks
            jf[i % 2] = tp
            t_h = toks[1]

        pg = bank(0)
        for i in range(8):
            for kt in range(8):
                t = p.pe(lambda e, i=i, kt=kt: e.matmul(pg[:, 32 * i:32 * i + 32], hT[:, kt, 128 * i:128 * i + 128], wabt[:, kt, :], start=(kt == 0), stop=(kt == 7)), t_h, t_c)
        pgv = pg[:, 0:256].rearrange("p (c n) -> p c n", c=8)
        ga = gt["g"]
        tm = gt["tmpg"]

        def rows(off):
            return dtb[:, off:off + 16].rearrange("p (a n) -> p a n", a=1).to_broadcast([P, 8, 16])

        t = tga = p.dve(lambda e: e.tensor_tensor(ga, pgv[:, :, 0:16], rows(0), ALU.add), t, t_c)
        t2 = tabs = p.act(lambda e: e.activation(tm, ga, ACT.Abs), t)
        t2 = p.act(lambda e: e.activation(tm, tm, ACT.Exp, scale=-1.0), t2)
        t3 = p.act(lambda e: e.activation(dtb[:, 16:32], dtb[:, 16:32], ACT.Exp), t_c)
        t2 = p.act(lambda e: e.activation(tm, tm, ACT.Ln, bias=1.0), t2)
        t = p.dve(lambda e: e.tensor_scalar(ga, ga, 0.0, None, ALU.max), t, tabs)
        t = p.dve(lambda e: e.tensor_tensor(ga, ga, tm, ALU.add), t, t2)
        t = p.dve(lambda e: e.tensor_tensor(ga, ga, rows(16), ALU.mult), t, t3)
        t = p.dve(lambda e: e.tensor_scalar(ga, ga, -1.0, None, ALU.mult), t)
        be = gt["beta"]
        tb = p.act(lambda e: e.activation(be, pgv[:, :, 16:32], ACT.Exp, scale=-1.0), tga)
        tb = p.dve(lambda e: e.tensor_scalar(be, be, 1.0, None, ALU.add), tb)
        tb = p.dve(lambda e: e.reciprocal(be, be), tb)
        tb2 = p.dve(lambda e: e.tensor_scalar(gt["nbeta"], be, -1.0, None, ALU.mult), tb)
        pc = bank(1)
        tg = p.pe(lambda e: e.matmul(pc[:, 0:64], Um, ga[:, :, 0:8], start=True, stop=True), t, free[1])
        tg = p.pe(lambda e: e.matmul(pc[:, 64:128], Lm, ga[:, :, 8:16], start=True, stop=True), t)
        tg = p.pe(lambda e: e.matmul(pc[:, 128:256], ones, A(gates0, 128), start=True, stop=True), t)
        tk = p.dve(lambda e: e.tensor_copy(gt["gc"][:, :, 0:8], pc[:, 0:64].rearrange("p (c n) -> p c n", c=8)), tg)
        tk = p.dve(lambda e: e.tensor_copy(gt["gc"][:, :, 8:16], pc[:, 64:128].rearrange("p (c n) -> p c n", c=8)), tg)
        td = p.dve(lambda e: e.tensor_tensor(A(gates0 + 128 * 5, 128), pc[:, 128:256], A(gates0 + 128 * 3, 128), ALU.subtract), tk)
        t1 = p.act(lambda e: e.activation(gt["dec"], gt["dec"], ACT.Exp), td)
        t1 = p.act(lambda e: e.activation(A(gates0 + 128 * 4, 128), pc[:, 128:256], ACT.Exp), td)
        tegl = t1
        t1 = p.act(lambda e: e.activation(gt["bgc"], gt["gc"], ACT.Exp), tk)
        t_gate = [tegl, p.dve(lambda e: e.tensor_tensor(gt["bgc"], gt["bgc"], be, ALU.mult), t1, tb2)]

        raw = [A(R + 1028 * i, 1028) for i in range(2)]
        o = R + 2056
        tmp = [A(o + 1024 * i, 1024) for i in range(2)]
        o += 2048
        chq = [A(o + 1024 * i, 1024) for i in range(2)]
        o += 2048
        chk = [A(o + 1024 * i, 1024) for i in range(2)]
        o += 2048
        sqk = [A(o + 1024 * i, 1024) for i in range(2)]
        o += 2048
        sqv = [A(o + 1024 * i, 1024) for i in range(2)]
        o += 2048
        zt = [A(o + 1024 * i, 1024) for i in range(2)]
        o += 2048
        G0 = o
        Gb = [[{n: A(o + 4096 * q + 2048 * d + 512 * j, 512) for j, n in enumerate(("u", "WT", "aq", "qs"))}
               for d in range(2)] for q in range(2)]
        o += 8192
        OC0 = o
        oc = [A(o + 1024 * i, 1024) for i in range(2)]
        o += 2048
        Sb = o
        o += 1280
        iv = [{n: A(o + 3072 * d + 512 * j, 512) for j, n in enumerate(("gam", "A", "AT", "T", "TT", "Y"))}
              for d in range(2)]
        o += 6144
        ssq = A(o, 16)
        ssk = A(o + 16, 16)
        sso = A(o + 32, 16)
        assert o + 48 <= 52640

        p0 = p.now("tensor", "vector", "scalar", "gpsimd")
        tz = None
        for i in range(2):
            tz = p.pool(lambda e, i=i: e.memset(raw[i][:, 0:2], 0.0), p0)
            tz = p.pool(lambda e, i=i: e.memset(raw[i][:, 1026:1028], 0.0))
        tt = {"raw": [tz, tz], "tmp": [p0, p0], "bk": [p0, p0], "n": 0}
        free_q = [p0, p0]
        free_k = [p0, p0]
        free_sk = [p0, p0]
        free_v = [p0, p0]
        free_z = [p0, p0]
        ready = {}

        def gbank():
            b = tt["n"] % 2
            tt["n"] += 1
            return b, bank(b), tt["bk"][b]

        def proj(slot, tw, col, dst, rtok, scale=1.0):
            wv = slot.rearrange("p (k n) -> p k n", k=8)
            toks = []
            for hf in range(2):
                b, bk, fr = gbank()
                for kt in range(8):
                    tp = p.pe(lambda e, kt=kt, hf=hf, bk=bk: e.matmul(bk, wv[:, kt, col:col + 128], hT[:, kt, 512 * hf:512 * hf + 512], start=(kt == 0), stop=(kt == 7)), tw, fr, t_h)
                    if kt % 2 == 1:
                        yield
                ev = p.act(lambda e, hf=hf, bk=bk: e.activation(dst[:, 512 * hf:512 * hf + 512], bk, ACT.Copy, scale=scale), tp, rtok)
                tt["bk"][b] = ev
                toks.append(ev)
            proj.tok, proj.pe = toks[1], tp

        def flip(src, dst_fn, stok):
            for hf in range(2):
                b, bk, fr = gbank()
                for j in range(4):
                    c = 4 * hf + j
                    tp = p.pe(lambda e, c=c, j=j, bk=bk: e.transpose(bk[:, 128 * j:128 * j + 128], src[:, 128 * c:128 * c + 128], ident), stok, fr)
                flip.tok = dst_fn(hf, bk, tp)
                flip.pe = tp
                tt["bk"][b] = flip.tok
                yield

        def copy_to(dst, dfree):
            return lambda hf, bk, tp: p.act(lambda e: e.activation(dst[:, 512 * hf:512 * hf + 512], bk, ACT.Copy), tp, dfree)

        def conv(r, h, which, cidx, dst, dfree):
            t = proj.tok
            w = cw[:, cidx, :]
            tp = p.dve(lambda e: e.tensor_scalar(tmp[0], raw[r][:, 0:1024], w[:, 0:1], None, ALU.mult), t, tt["tmp"][0], t_cw)
            for j in range(1, 5):
                tp = p.dve(lambda e, j=j: e.scalar_tensor_tensor(out=tmp[0], in0=raw[r][:, j:j + 1024], scalar=w[:, j:j + 1], in1=tmp[0], op0=ALU.mult, op1=ALU.add), tp)
            tt["raw"][r] = tp
            ta = p.act(lambda e: e.activation(tmp[1], tmp[0], ACT.Tanh), tp, tt["tmp"][1])
            td = p.dve(lambda e: e.scalar_tensor_tensor(out=dst, in0=tmp[1], scalar=1.0, in1=tmp[0], op0=ALU.add, op1=ALU.mult), ta, dfree)
            tt["tmp"] = [td, td]
            return td

        def unit(seq, ss, stok, scale):
            for c in range(8):
                ta = p.act(lambda e, c=c: e.activation(tmp[1][:, 128 * c:128 * c + 128], seq[:, 128 * c:128 * c + 128], ACT.Square, accum_out=ss[:, c:c + 1]), stok, tt["tmp"][1])
            t = rstd(ss[:, 0:8], 8, 1.0, ta)
            if scale != 1.0:
                t = p.dve(lambda e: e.tensor_scalar(ss[:, 0:8], ss[:, 0:8], scale, None, ALU.mult), t)
            s3 = seq.rearrange("p (c n) -> p c n", c=8)
            tt["tmp"][1] = ta
            return p.dve(lambda e: e.tensor_tensor(s3, s3, ss[:, 0:8].rearrange("p (c n) -> p c n", n=1).to_broadcast([P, 8, 128]), ALU.mult), t)

        def prep0(h):
            q = h % 2
            place, tw = W.get()
            yield from proj(place[0], tw, 0, raw[0][:, 2:1026], tt["raw"][0])
            td = conv(0, h, "q", h, chq[q], free_q[q])
            yield from proj(place[0], tw, 128, raw[1][:, 2:1026], tt["raw"][1])
            W.release(place, proj.pe)
            yield from flip(chq[q], copy_to(tmp[0], tt["tmp"][0]), td)
            ts = unit(tmp[0], ssq, flip.tok, 128.0 ** -0.5)
            yield
            yield from flip(tmp[0], copy_to(chq[q], flip.pe), ts)
            ready["q", h] = flip.tok
            tt["tmp"][0] = flip.pe
            td = conv(1, h, "v", 16 + h, tmp[1], None)
            yield
            yield from flip(tmp[1], copy_to(sqv[q], free_v[q]), td)
            tt["tmp"][1] = flip.pe
            ready["v", h] = flip.tok

        def prep1(h):
            q = h % 2
            place, tw = W.get()
            yield from proj(place[0], tw, 0, raw[0][:, 2:1026], tt["raw"][0])
            td = conv(0, h, "k", 8 + h, chk[q], free_k[q])
            yield from flip(chk[q], copy_to(sqk[q], free_sk[q]), td)
            ts = unit(sqk[q], ssk, flip.tok, 1.0)
            yield from proj(place[0], tw, 128, zt[q], free_z[q], scale=0.5)
            W.release(place, proj.pe)
            yield from flip(sqk[q], copy_to(chk[q], flip.pe), ts)
            ready["k", h] = [flip.tok, ts]
            ta = p.act(lambda e: e.activation(tmp[1], zt[q], ACT.Tanh), proj.tok, tt["tmp"][1])
            td = p.dve(lambda e: e.scalar_tensor_tensor(out=zt[q], in0=tmp[1], scalar=1.0, in1=zt[q], op0=ALU.add, op1=ALU.mult), ta)
            tt["tmp"][1] = td
            ready["z", h] = td
            yield

        ivf = [{"gam": p0, "A": p0, "AT": p0, "T": p0, "TT": p0, "Y": p0, "b0": p0, "b1": p0} for d in range(2)]
        gfree = [[p0, p0], [p0, p0]]
        gready = {}

        def invert(h, part, d):
            c0 = 4 * (part if d == 0 else 1 - part)
            q = h % 2
            G = Gb[part][d]
            b = iv[d]
            f = ivf[d]
            gf = gfree[part][d]
            B0, B1 = bank(2 + 2 * d), bank(3 + 2 * d)
            tri, mx = (Um, MxF) if d == 0 else (Lm, MxB)
            cs = [(128 * c, 128 * j, gt, d * 8 + h, c) for j, c in enumerate(range(c0, c0 + 4))]

            def col(n, c):
                return gt[n][:, c, d * 8 + h:d * 8 + h + 1]

            def cols(n):
                return gt[n][:, c0:c0 + 4, d * 8 + h:d * 8 + h + 1].to_broadcast([P, 4, 128])

            def four(ap):
                return ap.rearrange("p (c n) -> p c n", c=4)

            def all4(ap):
                return ap.rearrange("p (c n) -> p c n", c=1).to_broadcast([P, 4, 128])

            def mm4(B, lhs, rhs, *deps):
                for j in range(4):
                    t = p.pe(lambda e, j=j: e.matmul(B[:, 128 * j:128 * j + 128], lhs(j), rhs(j), start=True, stop=True), *deps)
                return t

            def tr4(B, src, *deps):
                for j in range(4):
                    t = p.pe(lambda e, j=j: e.transpose(B[:, 128 * j:128 * j + 128], src[:, 128 * j:128 * j + 128], ident), *deps)
                return t

            def part4(ap):
                return lambda j: ap[:, 128 * j:128 * j + 128]

            kq = lambda j: chk[q][:, 128 * (c0 + j):128 * (c0 + j) + 128]
            qq = lambda j: chq[q][:, 128 * (c0 + j):128 * (c0 + j) + 128]
            tp = mm4(B0, lambda j: bc(col("g", c0 + j), P, 128), lambda j: tri, t_gate, f["b0"])
            tk = mm4(B1, kq, kq, ready["k", h], f["b1"])
            yield
            te = p.act(lambda e: e.activation(b["Y"], B0, ACT.Exp), tp, f["Y"])
            for j in range(4):
                tg = p.dve(lambda e, j=j: e.scalar_tensor_tensor(out=b["gam"][:, 128 * j:128 * j + 128], in0=B0[:, 128 * j:128 * j + 128], scalar=col("gc", c0 + j), in1=mx, op0=ALU.subtract, op1=ALU.max), te, f["gam"])
            tg = p.act(lambda e: e.activation(b["gam"], b["gam"], ACT.Exp, scale=-1.0), tg)
            tq = p.pool(lambda e: e.tensor_tensor(G["qs"], chq[q][:, 128 * c0:128 * c0 + 512], b["Y"], ALU.mult), te, gf, ready["q", h])
            yield
            tpq = mm4(B0, qq, kq, te, tg)
            for j in range(4):
                ta = p.dve(lambda e, j=j: e.scalar_tensor_tensor(out=b["A"][:, 128 * j:128 * j + 128], in0=B1[:, 128 * j:128 * j + 128], scalar=col("nbeta", c0 + j), in1=b["gam"][:, 128 * j:128 * j + 128], op0=ALU.mult, op1=ALU.mult), tg, tk, f["A"])
            ta2 = p.dve(lambda e: e.tensor_tensor(b["T"], B0, b["gam"], ALU.mult), tpq, f["T"])
            yield
            tr = tr4(B1, b["A"], ta)
            tra = tr4(B0, b["T"], ta2)
            yield
            tat = p.act(lambda e: e.activation(b["AT"], B1, ACT.Copy), tr, f["AT"])
            taq = p.act(lambda e: e.activation(G["aq"], B0, ACT.Copy), tra, gf)
            ti = p.pool(lambda e: e.tensor_copy(four(b["T"]), all4(ident)), tra)
            ti2 = p.pool(lambda e: e.tensor_copy(four(b["TT"]), all4(ident)), f["TT"])
            mi = lambda n, tr_: mk[:, 2 * n + (tr_ ^ d), :]
            tT = p.dve(lambda e: e.copy_predicated(four(b["T"]), all4(mi(0, 0)), four(b["A"])), ti, ta, t_mk)
            tTT = p.dve(lambda e: e.copy_predicated(four(b["TT"]), all4(mi(0, 1)), four(b["AT"])), ti2, tat)
            yield
            tv = p.pool(lambda e: e.tensor_tensor(four(b["gam"]), sqv[q][:, 128 * c0:128 * c0 + 512].rearrange("p (c n) -> p c n", c=4), cols("beta"), ALU.mult), ta2, ta, ready["v", h])
            tkb = p.pool(lambda e: e.tensor_tensor(four(b["A"]), sqk[q][:, 128 * c0:128 * c0 + 512].rearrange("p (c n) -> p c n", c=4), cols("bgc"), ALU.mult), tT, tr, ready["k", h])
            yfree = tq
            b0f, b1f = [taq], [tat]
            for n in range(1, 7):
                tp = mm4(B0, part4(b["AT"]), part4(b["T"]), tT, tat, b0f)
                yield
                ty = p.act(lambda e: e.activation(b["Y"], B0, ACT.Copy), tp, yfree)
                if n < 6:
                    tp1 = mm4(B1, part4(b["TT"]), part4(b["Y"]), ty, tTT, b1f)
                tp0 = mm4(B0, part4(b["Y"]), part4(b["TT"]), ty, tTT)
                yfree = tp0
                yield
                if n < 6:
                    tT = p.dve(lambda e, n=n: e.copy_predicated(four(b["T"]), all4(mi(n, 0)), four(B1)), tp1, tp)
                    b1f = [tT]
                tTT = p.dve(lambda e, n=n: e.copy_predicated(four(b["TT"]), all4(mi(n, 1)), four(B0)), tp0, tp1)
                b0f = [tTT]
            tu = mm4(B1, part4(b["TT"]), part4(b["gam"]), tTT, tv, b1f)
            tw = mm4(B0, part4(b["A"]), part4(b["TT"]), tkb, b0f)
            yield
            e1 = p.act(lambda e: e.activation(G["u"], B1, ACT.Copy), tu, gf)
            e0 = p.act(lambda e: e.activation(G["WT"], B0, ACT.Copy), tw, gf)
            f.update({"gam": tu, "A": tw, "AT": tp0, "T": tp, "TT": tw, "Y": tp0, "b0": e0, "b1": e1})
            gready[h, part, d] = [e0, e1, tq, taq]
            yield

        S2 = [ar[:, Sb + 256 * q:Sb + 256 * q + 256] for q in range(2)]
        V2 = ar[:, Sb + 512:Sb + 768]
        kd = [ar[:, Sb + 768 + 256 * q:Sb + 1024 + 256 * q] for q in range(2)]
        sf = {"S": p0, "v": p0, "A": p0, "O": p0, "kd": [p0, p0], "pe": p0, "n": 0}
        ofree = [p0, p0]
        odone = {}

        def pair(base, other):
            st = other - base
            return ar[:, base:base + 2 * st].rearrange("p (a b) -> p a b", a=2)[:, :, 0:128]

        def scan(h, part):
            q = h % 2
            f = sf
            B6, B7 = bank(6), bank(7)
            gr = [gready[h, part, 0], gready[h, part, 1]]
            G = Gb[part]
            if part == 0:
                f["S"] = p.pool(lambda e: e.memset(S2[f["n"] % 2], 0.0), f["S"], f["pe"])
            for n in range(4):
                So, Sn = S2[f["n"] % 2], S2[(f["n"] + 1) % 2]
                kk = kd[f["n"] % 2]
                cc = (4 * part + n, 7 - 4 * part - n)
                js = (n, 3 - n)
                sl = [slice(128 * j, 128 * j + 128) for j in js]
                for d in range(2):
                    tkd = p.pool(lambda e, d=d, kk=kk, c=cc[d]: e.tensor_scalar(kk[:, 128 * d:128 * d + 128], sqk[q][:, 128 * c:128 * c + 128], gt["dec"][:, c, d * 8 + h:d * 8 + h + 1], None, ALU.mult), f["kd"][f["n"] % 2], ready["k", h], t_gate)
                for d in range(2):
                    t1 = p.pe(lambda e, d=d, So=So, sl=sl: e.matmul(B6[:, 128 * d:128 * d + 128], G[d]["WT"][:, sl[d]], So[:, 128 * d:128 * d + 128], start=True, stop=True), f["S"], gr, f["A"])
                yield
                ub = pair(G0 + 4096 * part + 128 * js[0], G0 + 4096 * part + 2048 + 128 * js[1])
                V3 = V2.rearrange("p (a b) -> p a b", a=2)
                tv = p.dve(lambda e, ub=ub, V3=V3: e.tensor_tensor(V3, ub, B6[:, 0:256].rearrange("p (a b) -> p a b", a=2), ALU.subtract), t1, f["v"], gr)
                for d in range(2):
                    t4 = p.pe(lambda e, d=d, kk=kk: e.matmul(B6[:, 128 * d:128 * d + 128], kk[:, 128 * d:128 * d + 128], V2[:, 128 * d:128 * d + 128], start=True, stop=True), tkd, tv)
                f["kd"][f["n"] % 2] = t4
                for d in range(2):
                    r = d if part == 0 else 1 - d
                    p.quiet("tensor", lambda e, d=d, r=r, So=So, sl=sl: e.matmul(B7[:, 128 * r:128 * r + 128], G[d]["qs"][:, sl[d]], So[:, 128 * d:128 * d + 128], start=True, stop=False), f["O"])
                    t3 = p.pe(lambda e, d=d, r=r, sl=sl: e.matmul(B7[:, 128 * r:128 * r + 128], G[d]["aq"][:, sl[d]], V2[:, 128 * d:128 * d + 128], start=False, stop=True))
                yield
                for d in range(2):
                    egl = gt["egl"][:, cc[d], d * 8 + h:d * 8 + h + 1]
                    ts = p.dve(lambda e, d=d, egl=egl, So=So, Sn=Sn: e.scalar_tensor_tensor(out=Sn[:, 128 * d:128 * d + 128], in0=So[:, 128 * d:128 * d + 128], scalar=egl, in1=B6[:, 128 * d:128 * d + 128], op0=ALU.mult, op1=ALU.add), t4, f["pe"])
                lo, hi = min(cc), max(cc)
                od = pair(OC0 + 1024 * q + 128 * lo, OC0 + 1024 * q + 128 * hi)
                b3 = B7[:, 0:256].rearrange("p (a b) -> p a b", a=2)
                if part == 0:
                    to = p.act(lambda e, od=od, b3=b3: e.activation(od, b3, ACT.Copy), t3, ofree[q])
                else:
                    to = p.dve(lambda e, od=od, b3=b3: e.tensor_tensor(od, od, b3, ALU.add), t3, first[h])
                f.update({"S": ts, "v": t3, "A": ts, "O": to, "pe": t3})
                f["n"] += 1
                yield
            if part == 0:
                first[h] = to
            else:
                odone[h] = to
            gfree[part] = [[t3, tv], [t3, tv]]

        first = {}

        o_chan = [p.channel(f"o{i}") for i in range(2)]
        o_saved = []

        def finish_head(h):
            q = h % 2
            dn = odone[h]
            for c in range(8):
                ta = p.act(lambda e, c=c: e.activation(tmp[1][:, 128 * c:128 * c + 128], oc[q][:, 128 * c:128 * c + 128], ACT.Square, accum_out=sso[:, c:c + 1]), dn, tt["tmp"][1])
            t = rstd(sso[:, 0:8], 8, 1.0 / 128, ta)
            tt["tmp"][1] = ta
            o3 = oc[q].rearrange("p (c n) -> p c n", c=8)
            t = p.pool(lambda e: e.tensor_tensor(o3, o3, sso[:, 0:8].rearrange("p (c n) -> p c n", n=1).to_broadcast([P, 8, 128]), ALU.mult), t)
            yield

            def put(hf, bk, tp):
                z = zt[q][:, 512 * hf:512 * hf + 512]
                return p.dve(lambda e: e.scalar_tensor_tensor(out=z, in0=bk, scalar=vc[:, NORMA:NORMA + 1], in1=z, op0=ALU.mult, op1=ALU.mult), tp, ready["z", h])

            yield from flip(oc[q], put, t)
            ofree[q] = flip.pe
            t = p.dma("sync", o_chan[q], sc_o[h], zt[q], flip.tok)
            free_z[q] = t
            o_saved.append(t)

        def chain(*gens):
            for g in gens:
                yield from g

        for _ in chain(prep0(0), prep1(0)):
            pass
        for s in range(17):
            threads = []
            h, part = divmod(s, 2)
            if s < 16:
                threads += [(invert(h, part, 0), 18), (invert(h, part, 1), 18)]
            if s >= 1:
                hh, pp = divmod(s - 1, 2)
                threads.append((scan(hh, pp), 13))
            if s < 14:
                threads.append((prep0(h + 1), 22) if part == 0 else (prep1(h + 1), 22))
            interleave(*threads)
            if s < 16:
                if part == 1:
                    last = p.now("tensor", "gpsimd")
                    free_q[h % 2] = free_k[h % 2] = free_v[h % 2] = last
            if s >= 1 and part == 0:
                free_sk[(h - 1) % 2] = p.now("tensor", "gpsimd")
                for _ in finish_head(h - 1):
                    pass

        every = lambda: p.now("tensor", "vector", "scalar", "gpsimd")

        def done(src=None):
            if src is not None:
                t = p.dma("sync", ld, dbg[:, 0:src.shape[1]], src, every(), o_saved)
                p.waits("sync", [t])
            for c in p.count:
                if c not in p.names and p.count[c]:
                    p.waits("sync", [(c, p.count[c])])
            block = ctx.enter_context(nc.Block())
            p.emit(block)

        if STOP == 1:
            t = p.dma("sync", ld, A(R, 8192).rearrange("p (a n) -> p a n", a=8), sc_o.rearrange("a p n -> p a n"), every(), o_saved)
            p.waits("sync", [t])
            return done(A(R, 8192))

        p1 = every()
        o = R
        qp = [A(o + 8192 * i, 4, 1024) for i in range(2)]
        kp = [A(o + 8192 * i + 4096, 4, 1024) for i in range(2)]
        o += 16384
        Vt = A(o, 12, 512)
        o += 6144
        bias = [A(o, 4, 256), A(o + 1024, 4, 256), A(o + 2048, 4, 128)]
        o += 2560
        Lb = [A(o + 1024 * i, 1024) for i in range(2)]
        o += 2048
        PT = [A(o + 1024 * i, 1024) for i in range(2)]
        o += 2048
        Ob = [A(o + 520 * i, 520) for i in range(2)]
        o += 1040
        nm = [A(o + 4 * i, 4) for i in range(2)]
        o += 8
        oh = A(Vt_off := R + 16384, 3, 384)
        rb = A(Vt_off + 1152, 12)
        trow = [A(Vt_off + 1664 + 384 * i, 384) for i in range(2)]
        assert o <= 52640
        c_b = p.channel("bias")
        t_oh = p.dma("sync", c_b, oh, onehot, p1)
        t_oh = p.dma("sync", c_b, rb, relb, p1)
        c_t = [p.channel(f"t{i}") for i in range(2)]
        tfree = [p1, p1]
        bfree = p1
        for n in range(12):
            g = n // 4
            q = n % 2
            t = p.pe(lambda e, n=n, g=g: e.matmul(bank(7)[:, 0:384], bc(rb[0:33, n:n + 1], 33, 128), oh[0:33, g, :], start=True, stop=True), t_oh, bfree)
            t = p.act(lambda e, q=q: e.activation(trow[q], bank(7)[:, 0:384], ACT.Copy), t, tfree[q])
            bfree = t
            tfree[q] = p.dma("sync", c_t[q], sc_t[n][0:P * 384].rearrange("(a b) -> a b", a=P), trow[q], t)
        t_bias = None
        for n in range(12):
            g, hh = divmod(n, 4)
            if g < 2:
                src = sc_t[n][127:127 + 128 * 383].rearrange("(a b) -> a b", b=383)[:, 0:256]
                t_bias = p.dma("sync", c_b, bias[g][:, hh, :], src, tfree, p1)
            else:
                src = sc_t[n][191:191 + 128 * 383].rearrange("(a b) -> a b", b=383)[:, 0:128]
                t_bias = p.dma("sync", c_b, bias[2][:, hh, :], src, tfree, p1)
        bias_pe = p.now("tensor", "scalar")
        t_bias = [t_bias]

        DIL = (1, 4, 8)
        tt["bk"] = [p1, p1]
        qkfree = [p1, p1]
        qk_tok = {}

        def qk_proj(g):
            dil = DIL[g]
            L = S // dil
            for which, dstt, scale in ((0, qp[g % 2], 128.0 ** -0.5), (1, kp[g % 2], 1.0)):
                for sl in range(2):
                    place, tw = W.get()
                    wv = place[0].rearrange("p (k n) -> p k n", k=8)
                    for ct in range(2):
                        hd = 2 * sl + ct
                        for hf in range(2):
                            b, bk, fr = gbank()
                            for kt in range(8):
                                tp = p.pe(lambda e, kt=kt, hf=hf, bk=bk, ct=ct, wv=wv: e.matmul(bk, wv[:, kt, 128 * ct:128 * ct + 128], hT[:, kt, 512 * hf:512 * hf + 512], start=(kt == 0), stop=(kt == 7)), tw, fr)
                                if kt % 4 == 3:
                                    yield
                            n = 512 // dil
                            dv = dstt[:, hd, :].rearrange("p (r l) -> p l r", r=dil)[:, n * hf:n * hf + n, :]
                            sv = bk.rearrange("p (l r) -> p l r", r=dil)
                            ev = p.act(lambda e, dv=dv, sv=sv, scale=scale: e.activation(dv, sv, ACT.Copy, scale=scale), tp, qkfree[g % 2])
                            tt["bk"][b] = ev
                    W.release(place, tp)
            qk_tok[g] = ev

        vfree = [bias_pe, tfree]
        v_tok = {}

        def chunks(g):
            if g == 0:
                return [(0, 64)] + [(64 + 128 * i, 128) for i in range(7)] + [(960, 64)]
            if g == 1:
                return [(r * 256 + a, n) for r in range(4) for a, n in ((0, 64), (64, 128), (192, 64))]
            return [(128 * i, 128) for i in range(8)]

        def v_proj(g):
            dil = DIL[g]
            L = S // dil
            pl = [W.get(), W.get()]
            for i, (a, n) in enumerate(chunks(g)):
                b, bk, fr = gbank()
                for sl in range(2):
                    wv = pl[sl][0][0].rearrange("p (k n) -> p k n", k=8)
                    for kt in range(8):
                        r, l = divmod(a, L)
                        lh = hT[:, kt, r + dil * l:r + dil * l + dil * (n - 1) + 1:dil]
                        tp = p.pe(lambda e, kt=kt, bk=bk, sl=sl, wv=wv, lh=lh, n=n: e.matmul(bk[0:n, 256 * sl:256 * sl + 256], lh, wv[:, kt, :], start=(kt == 0), stop=(kt == 7)), pl[sl][1], fr)
                    yield
                ev = p.act(lambda e, bk=bk, i=i, n=n: e.activation(Vt[0:n, i, :], bk[0:n, :], ACT.Copy), tp, vfree)
                tt["bk"][b] = ev
            for sl in range(2):
                W.release(pl[sl][0], tp)
            v_tok[g] = ev

        def tiles(g):
            if g == 2:
                return [(128 * i, 128 * i, 128, 0, [(i, 0, 128)]) for i in range(8)]
            L = S // DIL[g]
            res = []
            ch = chunks(g)
            at = {a: (i, n) for i, (a, n) in enumerate(ch)}
            for r in range(DIL[g]):
                for i in range(L // 128):
                    q0 = 128 * i
                    k0, k1 = max(q0 - 64, 0), min(q0 + 192, L)
                    parts, k = [], k0
                    while k < k1:
                        ci, n = at[r * L + k]
                        parts.append((ci, k - k0, n))
                        k += n
                    res.append((r * L + q0, r * L + k0, k1 - k0, k0 - (q0 - 64), parts))
            return res

        af = {"S": p1, "T": p1, "U": p1, "L": [p1, p1], "PT": [p1, p1], "O": [p1, p1], "n": 0}
        c_ob = [p.channel(f"ob{i}") for i in range(2)]
        ob_saved = []

        def attend(g):
            dil = DIL[g]
            L = S // dil
            todo = tiles(g)
            kept = {}

            def logits(i):
                qo, ko, nk, bo, parts = todo[i]
                x_ = af["n"] % 2
                af["n"] += 1
                SP = ps[:, 1024:2048].rearrange("p (h n) -> p h n", h=4)
                for hh in range(4):
                    tp = p.pe(lambda e, hh=hh: e.matmul(SP[:, hh, 0:nk], qp[g % 2][:, hh, qo:qo + 128], kp[g % 2][:, hh, ko:ko + nk], start=True, stop=True), qk_tok[g], af["S"])
                L3 = Lb[x_].rearrange("p (h n) -> p h n", h=4)[:, :, 0:nk]
                t = p.dve(lambda e: e.tensor_tensor(L3, SP[:, :, 0:nk], bias[g][:, :, bo:bo + nk], ALU.add), tp, t_bias, af["L"][x_])
                af["S"] = t
                O = Ob[x_]
                t = p.dve(lambda e: e.tensor_reduce(O[:, 512:516], L3, AX.X, ALU.max), t, af["O"][x_])
                t = p.dve(lambda e: e.tensor_scalar(nm[x_], O[:, 512:516], -1.0, None, ALU.mult), t)
                for hh in range(4):
                    te = p.act(lambda e, hh=hh: e.activation(L3[:, hh, :], L3[:, hh, :], ACT.Exp, bias=nm[x_][:, hh:hh + 1], accum_out=O[:, 516 + hh:517 + hh]), t)
                kept[i] = (x_, L3, te)

            def values(i):
                qo, ko, nk, bo, parts = todo[i]
                x_, L3, te = kept.pop(i)
                T3 = ps[:, 2048:3072].rearrange("p (j n) -> p j n", j=8)
                np_ = len(parts)
                where = {}
                for hh in range(4):
                    for j, (ci, c0, n) in enumerate(parts):
                        where[hh, j] = 2 * hh + j if np_ <= 2 else None
                t = None
                for hh in range(4):
                    for j, (ci, c0, n) in enumerate(parts):
                        tp = p.pe(lambda e, hh=hh, j=j, c0=c0, n=n: e.transpose(T3[0:n, 2 * hh + j, :], L3[:, hh, c0:c0 + n], ident), te, af["T"])
                yield
                PT3 = PT[x_].rearrange("p (j n) -> p j n", j=8)
                t = []
                if all(n == 128 for _, _, n in parts) and np_ == 2:
                    t.append(p.act(lambda e: e.activation(PT3[:, 0:4, :], T3[:, 0:4, :], ACT.Copy), tp, af["PT"][x_]))
                    t.append(p.dve(lambda e: e.tensor_copy(PT3[:, 4:8, :], T3[:, 4:8, :]), tp, af["PT"][x_]))
                else:
                    for j, (ci, c0, n) in enumerate(parts):
                        ov = PT[x_].rearrange("p (h j n) -> p h j n", h=4, j=2)[0:n, :, j, :]
                        iv_ = ps[0:n, 2048:3072].rearrange("p (h j n) -> p h j n", h=4, j=2)[:, :, j, :]
                        if j == 0:
                            t.append(p.act(lambda e, ov=ov, iv_=iv_: e.activation(ov, iv_, ACT.Copy), tp, af["PT"][x_]))
                        else:
                            t.append(p.dve(lambda e, ov=ov, iv_=iv_: e.tensor_copy(ov, iv_), tp, t[0], af["PT"][x_]))
                af["T"] = t
                af["L"][x_] = tp
                yield
                UP = bank(6)
                for hh in range(4):
                    for j, (ci, c0, n) in enumerate(parts):
                        tp = p.pe(lambda e, hh=hh, j=j, ci=ci, n=n: e.matmul(UP[:, 128 * hh:128 * hh + 128], PT3[0:n, 2 * hh + j, :], Vt[0:n, ci, 128 * hh:128 * hh + 128], start=(j == 0), stop=(j == np_ - 1)), t, v_tok[g], af["U"])
                af["PT"][x_] = tp
                O = Ob[x_]
                t = p.act(lambda e: e.activation(O[:, 0:512], UP, ACT.Copy), tp, af["O"][x_])
                af["U"] = t
                r, l = divmod(qo, L)
                s0 = r + dil * l
                t = p.dma("sync", c_ob[x_], sc_b[g][s0:s0 + dil * 127 + 1:dil, :], O, t, te)
                af["O"][x_] = t
                ob_saved.append(t)
                yield

            logits(0)
            yield
            for i in range(len(todo)):
                if i + 1 < len(todo):
                    logits(i + 1)
                yield
                yield from values(i)
            qkfree[g % 2] = p.now("tensor")
            vfree[0] = p.now("tensor")
            vfree[1] = None

        for _ in chain(qk_proj(0), v_proj(0)):
            pass
        interleave((attend(0), 33), (qk_proj(1), 32))
        for _ in v_proj(1):
            pass
        interleave((attend(1), 33), (qk_proj(2), 32))
        for _ in v_proj(2):
            pass

        def combine_loads():
            for g in range(3):
                t = p.dma("sync", c_cb, CBt[g], sc_b[g].rearrange("(i p) n -> p i n", p=P), ob_saved, p2)
            return t

        for _ in attend(2):
            pass
        p2 = every()
        c_cb = p.channel("cb")
        c_oa = p.channel("oa")
        oT = A(R, 8, 1024)
        obT = A(R + 8192, 4, 1024)
        mT = A(R + 12288, 8, 1024)
        CB0 = R + 20480
        CBt = [A(CB0 + 4160 * i, 8, 520) for i in range(3)]
        gtmp = [A(CB0 + 12480 + 512 * i, 512) for i in range(2)]
        M4 = A(CB0 + 12480 + 1024, 8, 4)
        D4 = A(CB0 + 12480 + 1056, 8, 4)
        X4 = A(CB0 + 12480 + 1088, 8, 4)
        assert CB0 + 12480 + 1120 <= 52640
        t_oa = p.dma("sync", c_oa, oT, sc_o.rearrange("a p n -> p a n"), o_saved, p2)
        t_cb = combine_loads()
        obt_tok = []

        def combine():
            m = [CBt[g][:, :, 512:516] for g in range(3)]
            z = [CBt[g][:, :, 516:520] for g in range(3)]
            t = p.dve(lambda e: e.tensor_tensor(M4, m[0], m[1], ALU.max), t_cb)
            t = p.dve(lambda e: e.tensor_tensor(M4, M4, m[2], ALU.max), t)
            for g in range(3):
                t1 = p.dve(lambda e, g=g: e.tensor_tensor(m[g], m[g], M4, ALU.subtract), t)
                t1 = p.act(lambda e, g=g: e.activation(m[g], m[g], ACT.Exp), t1)
                t1 = p.dve(lambda e, g=g: e.tensor_tensor(z[g], z[g], m[g], ALU.mult), t1)
            t = p.dve(lambda e: e.tensor_tensor(D4, z[0], z[1], ALU.add), t1)
            t = p.dve(lambda e: e.tensor_tensor(D4, D4, z[2], ALU.add), t)
            t = p.dve(lambda e: e.reciprocal(D4, D4), t)
            yield
            for g in range(3):
                t1 = p.dve(lambda e, g=g: e.tensor_tensor(m[g], m[g], D4, ALU.mult), t)
            for i in range(8):
                u = [CBt[g][:, i, 0:512].rearrange("p (h n) -> p h n", h=4) for g in range(3)]
                sc = [m[g][:, i, :].rearrange("p (h n) -> p h n", n=1).to_broadcast([P, 4, 128]) for g in range(3)]
                ts = [p.dve(lambda e, g=g, u=u, sc=sc: e.tensor_tensor(u[g], u[g], sc[g], ALU.mult), t1) for g in range(2)]
                ts.append(p.pool(lambda e, u=u, sc=sc: e.tensor_tensor(u[2], u[2], sc[2], ALU.mult), t1))
                t2 = p.dve(lambda e, u=u: e.tensor_tensor(u[0], u[0], u[1], ALU.add), ts[1])
                t2 = p.dve(lambda e, u=u: e.tensor_tensor(u[0], u[0], u[2], ALU.add), t2, ts[2])
                yield
                bk = bank(7)
                for j in range(4):
                    tp = p.pe(lambda e, i=i, j=j: e.transpose(bk[:, 128 * j:128 * j + 128], CBt[0][:, i, 128 * j:128 * j + 128], ident), t2, fb[0])
                fb[0] = p.act(lambda e, i=i: e.activation(obT[:, :, 128 * i:128 * i + 128], bk.rearrange("p (j n) -> p j n", j=4), ACT.Copy), tp)
                yield
            obt_tok.append(fb[0])

        fb = [p2]
        nb = {"n": 0, "free": [p2] * 4, "g": [p2, p2]}
        mt_tok = []

        def branch(second):
            src, nk, stok = (obT, 4, obt_tok) if second else (oT, 8, [t_oa])
            for cb in range(4):
                gw, t_gw = W.get()
                bw, t_bw = W.get()
                gv = gw[0].rearrange("p (k n) -> p k n", k=8)
                bv = bw[0].rearrange("p (k n) -> p k n", k=8)
                for ct in range(2):
                    for hf in range(2):
                        s0, s1 = nb["n"] % 4, (nb["n"] + 1) % 4
                        nb["n"] += 2
                        x_ = (nb["n"] // 2) % 2
                        b0, b1 = bank(s0), bank(s1)
                        hs = slice(512 * hf, 512 * hf + 512)
                        for kt in range(8):
                            tg = p.pe(lambda e, kt=kt, b0=b0, gv=gv, ct=ct, hs=hs: e.matmul(b0, gv[:, kt, 128 * ct:128 * ct + 128], hT[:, kt, hs], start=(kt == 0), stop=(kt == 7)), t_gw, nb["free"][s0])
                        yield
                        for kt in range(nk):
                            tb = p.pe(lambda e, kt=kt, b1=b1, bv=bv, ct=ct, hs=hs: e.matmul(b1, bv[:, kt, 128 * ct:128 * ct + 128], src[:, kt, hs], start=(kt == 0), stop=(kt == nk - 1)), t_bw, nb["free"][s1], stok)
                        yield
                        g_ = gtmp[x_]
                        t = p.act(lambda e, b0=b0, g_=g_: e.activation(g_, b0, ACT.Tanh, scale=0.5), tg, nb["g"][x_])
                        nb["free"][s0] = t
                        t = p.dve(lambda e, g_=g_: e.tensor_scalar(g_, g_, 0.5, 0.5, ALU.mult, ALU.add), t)
                        dst = mT[:, 2 * cb + ct, hs]
                        if not second:
                            t = p.dve(lambda e, g_=g_, b1=b1, dst=dst: e.tensor_tensor(dst, g_, b1, ALU.mult), t, tb)
                            nb["free"][s1] = t
                        else:
                            t = p.dve(lambda e, g_=g_, b1=b1: e.tensor_tensor(g_, g_, b1, ALU.mult), t, tb)
                            nb["free"][s1] = t
                            t = p.dve(lambda e, g_=g_, dst=dst: e.tensor_tensor(dst, dst, g_, ALU.add), t)
                        nb["g"][x_] = t
                W.release(gw, tg)
                W.release(bw, tb)
            mt_tok.append(t)

        interleave((branch(False), 32), (combine(), 18))
        if STOP == 2:
            return done(ar[:, R + 8192:R + 20480])
        for _ in branch(True):
            pass
        if STOP == 3:
            return done(ar[:, R + 12288:R + 20480])

        x1 = A(R, 8, 1024)
        YT = [A(R + 8192 + 1024 * i, 1024) for i in range(2)]
        lrow = A(R + 10240, 1024)
        JK = A(R + 11264, 1024)
        XS = 39488
        p3 = every()
        for i in range(2):
            W.add(A(XS + SLOT * i, SLOT), p3)
        c_row = p.channel("row")
        t_row = p.dma("sync", c_row, lrow, lam["lnpost"].partition_broadcast(P), p3)
        t_x = [p.dma("sync", p.channel(f"xx{i}"), x1[:, i, :], x[0, 128 * i:128 * i + 128, :], p3) for i in range(8)]
        st4 = A(V0 + 168, 80)
        yb = {"free": [p3] * 4, "n": 0, "y": [p3, p3], "jk": p3, "tb": [p3, p3]}

        def out_rows(lhs, pl, i, deps):
            x_ = i % 2
            for cb in range(4):
                s_ = yb["n"] % 4
                yb["n"] += 1
                bk = bank(s_)
                wv = pl[cb][0][0].rearrange("p (k n) -> p k n", k=8)
                for kt in range(8):
                    tp = p.pe(lambda e, kt=kt, bk=bk, wv=wv: e.matmul(bk[:, 0:256], lhs[:, kt, 128 * i:128 * i + 128], wv[:, kt, :], start=(kt == 0), stop=(kt == 7)), pl[cb][1], deps, yb["free"][s_])
                if i == 7:
                    W.release(pl[cb][0], tp)
                ev = p.act(lambda e, cb=cb, bk=bk: e.activation(YT[x_][:, 256 * cb:256 * cb + 256], bk[:, 0:256], ACT.Copy), tp, yb["y"][x_])
                yb["free"][s_] = ev
            return ev

        def residual(i, src, tok, scol, *deps):
            st = st4[:, scol:scol + 1]
            t = p.act(lambda e: e.activation(JK, src, ACT.Square, accum_out=st), tok, yb["jk"])
            yb["jk"] = t
            t = rstd(st, 1, 1.0 / 1024, t)
            t = p.dve(lambda e: e.scalar_tensor_tensor(out=src, in0=src, scalar=st, in1=lrow, op0=ALU.mult, op1=ALU.mult), t, t_row)
            t = p.dve(lambda e: e.tensor_tensor(x1[:, i, :], x1[:, i, :], src, ALU.add), t, *deps)
            return t

        pl = [W.get() for _ in range(4)]
        h2T = A(0, 8, 1024)
        h2_tok = None
        pend = None

        def tail4(i, t):
            toks, tp = normed_transposed(x1[:, i, :], t, st4[:, 8 + i:9 + i], h2T[:, :, 128 * i:128 * i + 128], LNMLP, (4, 5), tuple(yb["tb"]), JK, yb["jk"])
            yb["tb"] = toks
            yb["jk"] = tp
            return toks[1]

        for i in range(8):
            ev = out_rows(mT, pl, i, p3)
            if pend is not None:
                h2_tok = tail4(*pend)
            t = residual(i, YT[i % 2], ev, i, t_x[i])
            yb["y"][i % 2] = t
            pend = (i, t)
        h2_tok = tail4(*pend)
        if STOP == 4:
            return done(ar[:, R:R + 8192])

        fT = [A(30720 + 4096 * i, 4, 1024) for i in range(2)]
        acc = A(43584, 8, 1024)
        p4 = every()
        t_row = p.dma("sync", c_row, lrow, lam["lnmlppost"].partition_broadcast(P), p4)
        fb_ = {"free": [p4] * 8, "n": 0, "f": [p4, p4], "acc": {}}
        f_tok = {}

        def ff1(c):
            q = c % 2
            for sl in range(2):
                place, tw = W.get()
                wv = place[0].rearrange("p (k n) -> p k n", k=8)
                for ct in range(2):
                    for hf in range(2):
                        s_ = fb_["n"] % 4
                        fb_["n"] += 1
                        bk = bank(s_)
                        hs = slice(512 * hf, 512 * hf + 512)
                        for kt in range(8):
                            tp = p.pe(lambda e, kt=kt, bk=bk, wv=wv, ct=ct, hs=hs: e.matmul(bk, wv[:, kt, 128 * ct:128 * ct + 128], h2T[:, kt, hs], start=(kt == 0), stop=(kt == 7)), tw, fb_["free"][s_])
                        dst = fT[q][:, 2 * sl + ct, hs]
                        t = p.act(lambda e, bk=bk, dst=dst: e.activation(dst, bk, ACT.Relu), tp, fb_["f"][q])
                        fb_["free"][s_] = t
                        f_tok[c] = p.act(lambda e, dst=dst: e.activation(dst, dst, ACT.Square), t)
                        yield
                W.release(place, tp)

        def ff2(c):
            q = c % 2
            pl = [W.get(), W.get()]
            wv = [x_[0][0].rearrange("p (k n) -> p k n", k=2) for x_ in pl]
            for i in range(8):
                for hf in range(2):
                    s_ = 4 + fb_["n2"] % 4
                    fb_["n2"] += 1
                    bk = bank(s_)
                    hs = slice(512 * hf, 512 * hf + 512)
                    for kt in range(4):
                        tp = p.pe(lambda e, kt=kt, bk=bk, i=i, hs=hs: e.matmul(bk, fT[q][:, kt, 128 * i:128 * i + 128], wv[kt // 2][:, kt % 2, hs], start=(kt == 0), stop=(kt == 3)), pl[0][1], pl[1][1], fb_["free"][s_], f_tok[c])
                    dst = acc[:, i, hs]
                    if c == 0:
                        t = p.dve(lambda e, bk=bk, dst=dst: e.tensor_copy(dst, bk), tp, p4)
                    else:
                        t = p.dve(lambda e, bk=bk, dst=dst: e.tensor_tensor(dst, dst, bk, ALU.add), tp, fb_["acc"][i, hf])
                    fb_["free"][s_] = t
                    fb_["acc"][i, hf] = t
                    if c == 7 and hf == 1:
                        mlp_done(i, t)
                    yield
            for x_ in pl:
                W.release(x_[0], tp)
            fb_["f"][q] = tp

        x2_tok = {}

        def mlp_done(i, t):
            t = residual(i, acc[:, i, :], t, 16 + i)
            x2_tok[i] = t

        fb_["n2"] = 0
        for _ in ff1(0):
            pass
        for c in range(8):
            if c < 7:
                interleave((ff1(c + 1), 8), (ff2(c), 16))
            else:
                for _ in ff2(c):
                    pass
        if STOP == 5:
            return done(ar[:, R:R + 8192])

        p5 = every()
        Q0 = 26624
        uT = A(0, 8, 1024)
        mix = A(43584, 8, 1024)
        uTm = A(51776, 8, 16)
        c2 = p.channel("c2")
        mt = A(Q0, 1024)
        mj = A(Q0 + 1024, 1024)
        t_mt = p.dma("sync", c2, mt[0:16, :], meta, p5)
        LW = 51904
        sm = st4[0:16, 24:25]
        t = p.act(lambda e: e.activation(mj[0:16, :], mt[0:16, :], ACT.Square, accum_out=sm), t_mt)
        t = p.dve(lambda e: e.tensor_scalar(sm, sm, 1.0 / 1024, EPS, ALU.mult, ALU.add), t)
        t = p.pool(lambda e: e.tensor_tensor(sm, sm, mh_t[0:16, :], ALU.pow), t)
        t = p.dve(lambda e: e.tensor_scalar(mj[0:16, :], mt[0:16, :], sm, None, ALU.mult), t)
        for kt in range(8):
            tp = p.pe(lambda e, kt=kt: e.transpose(bank(6)[:, 16 * kt:16 * kt + 16], mj[0:16, 128 * kt:128 * kt + 128], ident[0:16, 0:16]), t, p5)
        for kt in range(8):
            t_um = p.act(lambda e, kt=kt: e.activation(uTm[:, kt, :], bank(6)[:, 16 * kt:16 * kt + 16], ACT.Copy, scale=vc[:, NW2 + kt:NW2 + kt + 1]), tp)
        JK2 = [A(Q0 + 3072 + 1024 * i, 1024) for i in range(2)]
        jf = [p5, p5]
        tbf = [[p5, p5], [p5, p5]]
        for i in range(8):
            x_ = i % 2
            toks, tp = normed_transposed(x1[:, i, :], x2_tok[i], st4[:, 32 + i:33 + i], uT[:, :, 128 * i:128 * i + 128], NW2, (2 * x_, 2 * x_ + 1), tuple(tbf[x_]), JK2[x_], jf[x_])
            tbf[x_] = toks
            jf[x_] = tp
        t_u = toks[1]

        bt = {"n": 0, "free": [every()] * 8}

        def nbank(lo, n):
            s_ = lo + bt["n"] % n
            bt["n"] += 1
            return s_, bank(s_)

        def gemm_c(nslots, with_meta, each):
            for sl in range(nslots):
                place, tw = W.get()
                wv = place[0].rearrange("p (k n) -> p k n", k=8)
                for ct in range(2):
                    pieces = [(uT, 0, 512, 16), (uT, 512, 512, 528)]
                    if with_meta:
                        pieces.insert(0, (uTm, 0, 16, 0))
                    for src, c0, n, pos in pieces:
                        s_, bk = nbank(0, 4)
                        for kt in range(8):
                            tp = p.pe(lambda e, kt=kt, bk=bk, wv=wv, ct=ct, src=src, c0=c0, n=n: e.matmul(bk[:, 0:n], wv[:, kt, 128 * ct:128 * ct + 128], src[:, kt, c0:c0 + n], start=(kt == 0), stop=(kt == 7)), tw, t_u, t_um, bt["free"][s_])
                        bt["free"][s_] = each(2 * sl + ct, pos, n, bk, tp)
                W.release(place, tp)

        T = 1040
        lwt = A(Q0 + 12544 - 1024, 8, 128)
        p6 = every()
        tz = p.pool(lambda e: e.memset(lwt, 0.0), p6)
        for g in range(2):
            for n in range(8):
                hlf = n % 2
                t_lw = p.dma("sync", c2, lwt[64 * hlf:64 * hlf + 64, 4 * g + n // 2, 64 * hlf:64 * hlf + 64], lruw[g, n], tz)
        c8 = st4[:, 40:44]
        c8b = st4[:, 44:48]
        Lc = vc[:, LRUL:LRUL + 4]
        t = p.act(lambda e: e.activation(c8b, Lc, ACT.Abs))
        t = p.act(lambda e: e.activation(c8b, c8b, ACT.Exp, scale=-1.0), t)
        t = p.act(lambda e: e.activation(c8b, c8b, ACT.Ln, bias=1.0), t)
        t = p.dve(lambda e: e.tensor_scalar(c8, Lc, -1.0, 0.0, ALU.mult, ALU.max), t)
        t = p.dve(lambda e: e.tensor_tensor(c8, c8, c8b, ALU.add), t)
        t = p.dve(lambda e: e.tensor_scalar(c8, c8, -8.0, None, ALU.mult), t)
        hb = st4[:, 48:56]
        t = p.dve(lambda e: e.tensor_scalar(hb[:, 0:4], vc[:, BR:BR + 4], -1.0, None, ALU.mult), t)
        t = p.dve(lambda e: e.tensor_scalar(hb[:, 4:8], vc[:, BI:BI + 4], 0.5, None, ALU.mult), t)
        t_c8 = t
        wc = 42
        LB = [[A(Q0 + 5220 * i + 1044 * j, 1044) for j in range(5)] for i in range(2)]
        lfree = [p6, p6]
        xl_t = {}

        def each_x(ct, pos, n, bk, tp):
            xl = LB[ct % 2][0]
            t = p.act(lambda e: e.activation(xl[:, 3 + pos:3 + pos + n], bk[:, 0:n], ACT.Copy), tp, lfree[ct % 2])
            xl_t[ct] = t
            if pos == 528:
                if ct > 0:
                    lru(ct - 1)
            return t

        lru_out = {}

        def lru(ct):
            xl, xc, r_, i_, a_ = LB[ct % 2]
            tz = p.pool(lambda e: e.memset(xl[:, 0:3], 0.0), lfree[ct % 2])
            cw2 = lam_cw[:, ct, :]
            t = p.dve(lambda e: e.tensor_scalar(xc[:, 0:T], xl[:, 0:T], cw2[:, 0:1], vc[:, CB + ct:CB + ct + 1], ALU.mult, ALU.add), xl_t[ct], tz, lfree[ct % 2], t_cw2)
            for j in range(1, 4):
                t = p.dve(lambda e, j=j: e.scalar_tensor_tensor(out=xc[:, 0:T], in0=xl[:, j:j + T], scalar=cw2[:, j:j + 1], in1=xc[:, 0:T], op0=ALU.mult, op1=ALU.add), t)
            ev = []
            for g, dst in ((0, r_), (1, i_)):
                for c0, n in ((0, 512), (512, 512), (1024, 16)):
                    s_ = 4 + bt["n4"] % 4
                    bt["n4"] += 1
                    bk = bank(s_)
                    tp = p.pe(lambda e, g=g, c0=c0, n=n, bk=bk: e.matmul(bk[:, 0:n], lwt[:, 4 * g + ct, :], xc[:, c0:c0 + n], start=True, stop=True), t, t_lw, bt["free"][s_])
                    tv = p.act(lambda e, g=g, c0=c0, n=n, bk=bk, dst=dst: e.activation(dst[:, c0:c0 + n], bk[:, 0:n], ACT.Exp if g == 0 else ACT.Tanh, scale=-1.0 if g == 0 else 0.5, bias=hb[:, 4 * g + ct:4 * g + ct + 1]), tp, lfree[ct % 2], t_c8)
                    bt["free"][s_] = tv
            R_, I_, Aa, Xc, Xl = r_[:, 0:T], i_[:, 0:T], a_[:, 0:T], xc[:, 0:T], xl[:, 0:T]
            t1 = p.dve(lambda e: e.tensor_scalar(R_, R_, 1.0, None, ALU.add), tv)
            t1 = p.dve(lambda e: e.reciprocal(R_, R_), t1)
            ta = p.act(lambda e: e.activation(Aa, R_, ACT.Exp, scale=c8[:, ct:ct + 1]), t1, lfree[ct % 2])
            t1 = p.dve(lambda e: e.tensor_scalar(R_, R_, c8[:, ct:ct + 1], None, ALU.mult), ta)
            th = p.act(lambda e: e.activation(R_, R_, ACT.Tanh), t1)
            t2 = p.dve(lambda e: e.tensor_tensor(Xl, Aa, Aa, ALU.mult), ta)
            t2 = p.dve(lambda e: e.scalar_tensor_tensor(out=Xl, in0=Xl, scalar=1.0, in1=R_, op0=ALU.add, op1=ALU.mult), t2, th)
            tm_ = p.act(lambda e: e.activation(Xl, Xl, ACT.Sqrt, scale=-1.0), t2)
            t3 = p.dve(lambda e: e.tensor_scalar(I_, I_, 0.5, 0.5, ALU.mult, ALU.add), tv)
            t3 = p.dve(lambda e: e.tensor_tensor(I_, I_, Xc, ALU.mult), t3)
            t4 = p.dve(lambda e: e.memset(Xl[:, 0:1], 1.0), tm_)
            t3 = p.dve(lambda e: e.tensor_tensor(I_, I_, Xl, ALU.mult), t3, t4)
            t3 = p.dve(lambda e: e.tensor_tensor_scan(R_, Aa, I_, 0.0, ALU.mult, ALU.add), t3, th)
            t3 = p.dve(lambda e: e.tensor_copy(mix[:, 4 + ct, :], r_[:, 16:T]), t3, p5)
            lfree[ct % 2] = t3
            lru_out[ct] = t3

        bt["n4"] = 0
        lam_cw = A(LW, 4, 4)
        t_cw2 = p.dma("sync", p.channel("cw2"), lam_cw, lam["cw2"], p6)
        GT = [A(Q0 + 12544 - 1024 - 1064 + 532 * i, 532)[:, 0:512] for i in range(2)]
        gfr = [p6, p6]

        def each_g(base):
            def f(ct, pos, n, bk, tp):
                x_ = (pos // 512) % 2
                hs = slice(pos - 16, pos - 16 + n)
                ta = p.act(lambda e: e.activation(GT[x_], bk, ACT.Tanh, scale=0.5), tp, gfr[x_])
                t = p.dve(lambda e: e.scalar_tensor_tensor(out=GT[x_], in0=GT[x_], scalar=1.0, in1=bk, op0=ALU.add, op1=ALU.mult), ta)
                dst = mix[:, base + ct, hs]
                if base == 4:
                    t2 = p.dve(lambda e: e.scalar_tensor_tensor(out=dst, in0=GT[x_], scalar=0.5, in1=dst, op0=ALU.mult, op1=ALU.mult), t, lru_out[ct])
                else:
                    t2 = p.dve(lambda e: e.tensor_scalar(dst, GT[x_], 0.5, None, ALU.mult), t)
                gfr[x_] = t2
                return t
            return f

        gemm_c(2, True, each_x)
        lru(3)
        gemm_c(2, False, each_g(0))
        gemm_c(2, False, each_g(4))
        if STOP == 6:
            return done(ar[:, 43584:43584 + 8192])

        p7 = every()
        qT = A(Q0, 4, 1024)
        kT = A(Q0 + 4096, 4, 1040)
        vO = Q0 + 8256
        cosT, sinT = A(vO, 1040), A(vO + 1040, 1040)
        rp = [A(vO + 2080 + 512 * i, 512) for i in range(2)]
        permT = A(vO + 3104, 128)
        lqk = A(vO + 3232, 256)
        c3 = p.channel("c3")
        t_r = p.dma("sync", c3, cosT, rope[0], p7)
        t_r = p.dma("sync", c3, sinT, rope[1], p7)
        t_r = p.dma("sync", c3, permT, rope[2][:, 0:128], p7)
        t_lq = p.dma("sync", p.channel("lq"), lqk, lam["lqk"].partition_broadcast(P), p7)
        lm = st4[:, 56:64]
        t = p.dve(lambda e: e.tensor_tensor(lqk[:, 0:64], lqk[:, 0:64], lqk[:, 64:128], ALU.mult), t_lq, t_r)
        t = p.dve(lambda e: e.tensor_tensor(lqk[:, 128:192], lqk[:, 128:192], lqk[:, 192:256], ALU.mult), t)
        t = p.dve(lambda e: e.tensor_reduce(lm[:, 0:1], lqk[:, 0:64], AX.X, ALU.add), t)
        t = p.dve(lambda e: e.tensor_reduce(lm[:, 1:2], lqk[:, 128:192], AX.X, ALU.add), t)
        t = p.act(lambda e: e.activation(lm[:, 0:2], lm[:, 0:2], ACT.Exp), t)
        t = p.dve(lambda e: e.tensor_tensor(lm[:, 2:3], lm[:, 1:2], lm[:, 0:1], ALU.subtract), t)
        LAM_INIT = float(0.8 - 0.6 * np.exp(0.0))
        t = p.dve(lambda e: e.tensor_scalar(lm[:, 2:3], lm[:, 2:3], LAM_INIT, None, ALU.subtract), t)
        t_lm = t
        rfree = [p7, p7]
        rk = {"n": 0}
        rt = {}

        def each_r(dst, key, shift):
            def f(ct, pos, n, bk, tp):
                x_ = rk["n"] % 2
                rk["n"] += 1
                tc = p.act(lambda e: e.activation(rp[x_][:, 0:n], bk[:, 0:n], ACT.Copy), tp, rfree[x_], p7)
                s_ = 4 + bt["n4"] % 4
                bt["n4"] += 1
                b2 = bank(s_)
                t2 = p.pe(lambda e: e.matmul(b2[:, 0:n], permT, rp[x_][:, 0:n], start=True, stop=True), tc, t_r, bt["free"][s_])
                d = dst[:, ct, pos - shift:pos - shift + n]
                t3 = p.dve(lambda e: e.tensor_tensor(d, b2[:, 0:n], sinT[:, pos:pos + n], ALU.mult), t2, p7, t_r)
                bt["free"][s_] = t3
                t4 = p.dve(lambda e: e.tensor_tensor(rp[x_][:, 0:n], rp[x_][:, 0:n], cosT[:, pos:pos + n], ALU.mult), t2)
                t5 = p.dve(lambda e: e.tensor_tensor(d, d, rp[x_][:, 0:n], ALU.add), t4)
                rfree[x_] = t5
                rt[key] = t5
                return tc
            return f

        gemm_c(2, True, each_r(kT, "k", 0))
        gemm_c(2, False, each_r(qT, "q", 16))
        p8 = every()
        vv = A(vO, 9, 512)
        pl = [W.get(), W.get()]
        for i in range(9):
            s_, bk = nbank(0, 4)
            n = 16 if i == 0 else 128
            for sl in range(2):
                wv = pl[sl][0][0].rearrange("p (k n) -> p k n", k=8)
                for kt in range(8):
                    lh = uTm[:, kt, :] if i == 0 else uT[:, kt, 128 * (i - 1):128 * i]
                    tp = p.pe(lambda e, kt=kt, bk=bk, sl=sl, wv=wv, lh=lh, n=n: e.matmul(bk[0:n, 256 * sl:256 * sl + 256], lh, wv[:, kt, :], start=(kt == 0), stop=(kt == 7)), pl[sl][1], bt["free"][s_])
            t_v = p.act(lambda e, i=i, n=n, bk=bk: e.activation(vv[0:n, i, :], bk[0:n, :], ACT.Copy), tp, p8)
            bt["free"][s_] = t_v
        for sl in range(2):
            W.release(pl[sl][0], tp)

        p9 = every()
        Eb = [[A(1040 * (2 * i + m), 1040) for m in range(2)] for i in range(2)]
        WTb = [A(4160 + 1152 * i, 9, 128) for i in range(2)]
        o2 = [A(6464 + 128 * i, 128) for i in range(2)]
        negr = A(6720, 128)
        oner = A(6848, 64)
        st2 = A(6912, 8)
        jk2 = A(6920, 128)
        tn = p.pool(lambda e: e.memset(negr[0:1, 0:64], NEG), p9)
        tn = p.pool(lambda e: e.memset(negr[0:1, 64:128], 0.0))
        tn = p.pool(lambda e: e.memset(oner[0:1, :], 1.0))
        stat = [A(7060 + 16 * i, 16) for i in range(2)]
        fz = {"E": [p9, p9], "W": [p9, p9], "SP": [p9, p9], "T": p9, "U": p9, "o": [p9, p9], "st": [p9, p9], "OT": p9}
        items = [(hh, i) for i in range(8) for hh in range(4)]
        kept = {}

        def scores(n):
            hh, i = items[n]
            x_ = n % 2
            nk = 16 + 128 * (i + 1)
            st = stat[x_]
            for m in range(2):
                SPm = ps[:, 1536 * m:1536 * m + nk]
                rows_ = slice(64 * m, 64 * m + 64)
                k0 = 0
                while k0 < nk:
                    w_ = min(512, nk - k0)
                    lo = nk - 64
                    cut = [(k0, w_)] if k0 + w_ <= lo or k0 >= lo else [(k0, lo - k0), (lo, k0 + w_ - lo)]
                    for a_, b_ in cut:
                        last = a_ + b_ > lo
                        t = p.pe(lambda e, a_=a_, b_=b_, last=last, SPm=SPm, rows_=rows_: e.matmul(SPm[:, a_:a_ + b_], qT[rows_, hh, 128 * i:128 * i + 128], kT[rows_, hh, a_:a_ + b_], start=True, stop=not last), rt["k"], rt["q"], fz["SP"][m])
                        if last:
                            s0 = max(lo, a_)
                            w2 = a_ + b_ - s0
                            t = p.pe(lambda e, s0=s0, w2=w2, SPm=SPm: e.matmul(SPm[:, s0:s0 + w2], negr[0:1, :], oner[0:1, 0:w2], start=False, stop=True), tn)
                    k0 += w_
                tm_ = p.dve(lambda e, m=m, SPm=SPm: e.tensor_reduce(st[:, m:m + 1], SPm, AX.X, ALU.max), t, fz["st"][x_])
                tm_ = p.dve(lambda e, m=m: e.tensor_scalar(st[:, m:m + 1], st[:, m:m + 1], -0.125, None, ALU.mult), tm_)
                te = p.act(lambda e, m=m, SPm=SPm: e.activation(Eb[x_][m][:, 0:nk], SPm, ACT.Exp, scale=0.125, bias=st[:, m:m + 1], accum_out=st[:, 2 + m:3 + m]), tm_, fz["E"][x_])
                fz["SP"][m] = te
            t = p.dve(lambda e: e.reciprocal(st[:, 4:6], st[:, 2:4]), te)
            t = p.dve(lambda e: e.tensor_scalar(st[:, 5:6], st[:, 5:6], lm[:, 2:3], None, ALU.mult), t, t_lm)
            t = p.dve(lambda e: e.tensor_scalar(Eb[x_][1][:, 0:nk], Eb[x_][1][:, 0:nk], st[:, 5:6], None, ALU.mult), t)
            t = p.dve(lambda e: e.scalar_tensor_tensor(out=Eb[x_][0][:, 0:nk], in0=Eb[x_][0][:, 0:nk], scalar=st[:, 4:5], in1=Eb[x_][1][:, 0:nk], op0=ALU.mult, op1=ALU.add), t)
            kept[n] = (x_, nk, t)

        o_tok = {}

        def mixv(n):
            hh, i = items[n]
            x_, nk, te = kept.pop(n)
            E = Eb[x_][0]
            blocks = [(0, 16, 0)] + [(16 + 128 * j, 128, j + 1) for j in range(i + 1)]
            TB = bank(6)
            evs = []
            todo = [blocks[0:1]] + [blocks[a_:a_ + 4] for a_ in range(1, len(blocks), 4)]
            for grp in todo:
                n_ = grp[0][1]
                for j, (c0, nn, bi) in enumerate(grp):
                    tp = p.pe(lambda e, j=j, c0=c0, nn=nn: e.transpose(TB[0:nn, 128 * j:128 * j + 128], E[:, c0:c0 + nn], ident), te, fz["T"])
                g_ = len(grp)
                b0 = grp[0][2]
                fz["T"] = p.act(lambda e, g_=g_, b0=b0, n_=n_: e.activation(WTb[x_][0:n_, b0:b0 + g_, :], TB[0:n_, 0:128 * g_].rearrange("p (g n) -> p g n", g=g_), ACT.Copy), tp, fz["W"][x_])
            fz["E"][x_] = tp
            U = bank(7)[:, 0:128]
            for j, (c0, nn, bi) in enumerate(blocks):
                tp = p.pe(lambda e, j=j, nn=nn, bi=bi: e.matmul(U, WTb[x_][0:nn, bi, :], vv[0:nn, bi, 128 * hh:128 * hh + 128], start=(j == 0), stop=(j == len(blocks) - 1)), fz["T"], fz["U"], fz["OT"], t_v)
            fz["W"][x_] = tp
            st = stat[x_]
            t = p.act(lambda e: e.activation(o2[x_], U, ACT.Copy), tp, fz["o"][x_])
            t1 = p.act(lambda e: e.activation(jk2, o2[x_], ACT.Square, accum_out=st[:, 6:7]), t)
            t2 = p.dve(lambda e: e.tensor_scalar(st[:, 6:7], st[:, 6:7], 1.0 / 128, 1e-5, ALU.mult, ALU.add), t1)
            t2 = p.pool(lambda e: e.tensor_tensor(st[:, 6:7], st[:, 6:7], mh_t, ALU.pow), t2)
            t2 = p.dve(lambda e: e.tensor_scalar(o2[x_], o2[x_], st[:, 6:7], 1.0 - LAM_INIT, ALU.mult, ALU.mult), t2)
            fz["st"][x_] = t2
            fz["U"] = t
            kept["o", n] = (x_, t2)

        def turn(n):
            hh, i = items[n]
            x_, t2 = kept.pop(("o", n))
            OT = bank(7)[:, 256:384]
            tp = p.pe(lambda e: e.transpose(OT, o2[x_], ident), t2, fz["OT"])
            fz["o"][x_] = tp
            dst = mix[:, hh, 128 * i:128 * i + 128]
            t = p.dve(lambda e: e.scalar_tensor_tensor(out=dst, in0=OT, scalar=vc[:, SUB:SUB + 1], in1=dst, op0=ALU.mult, op1=ALU.mult), tp)
            fz["OT"] = t
            o_tok[0] = t

        scores(0)
        for n in range(len(items)):
            if n + 1 < len(items):
                scores(n + 1)
            if n >= 1:
                turn(n - 1)
            mixv(n)
        turn(len(items) - 1)
        if STOP == 7:
            return done(ar[:, 43584:43584 + 8192])

        p10 = every()
        YT[0], YT[1] = A(Q0, 1024), A(Q0 + 1024, 1024)
        FR = A(Q0 + 2048, 1024)
        JF = [A(Q0 + 3072 + 1024 * i, 1024) for i in range(2)]
        t_fr = p.dma("sync", c_row, FR, lam["fnorm"].partition_broadcast(P), p10)
        pl = [W.get() for _ in range(4)]
        yb = {"free": [p10] * 4, "n": 0, "y": [p10, p10], "jk": p10}
        c_out = [p.channel(f"out{i}") for i in range(2)]
        jf = p10
        for i in range(8):
            x_ = i % 2
            for cb in range(4):
                s_ = yb["n"] % 4
                yb["n"] += 1
                bk = bank(s_)
                wv = pl[cb][0][0].rearrange("p (k n) -> p k n", k=8)
                for kt in range(8):
                    tp = p.pe(lambda e, kt=kt, bk=bk, wv=wv, i=i: e.matmul(bk[:, 0:256], mix[:, kt, 128 * i:128 * i + 128], wv[:, kt, :], start=(kt == 0), stop=(kt == 7)), pl[cb][1], p10, yb["free"][s_])
                ev = p.dve(lambda e, cb=cb, bk=bk, i=i, x_=x_: e.tensor_tensor(YT[x_][:, 256 * cb:256 * cb + 256], bk[:, 0:256], x1[:, i, 256 * cb:256 * cb + 256], ALU.add), tp, yb["y"][x_])
                yb["free"][s_] = ev
            st = st4[:, 64 + i:65 + i]
            t = p.act(lambda e, x_=x_, st=st: e.activation(JF[x_], YT[x_], ACT.Square, accum_out=st), ev)
            t = rstd(st, 1, 1.0 / 1024, t)
            t = p.dve(lambda e, x_=x_, st=st: e.scalar_tensor_tensor(out=YT[x_], in0=YT[x_], scalar=st, in1=FR, op0=ALU.mult, op1=ALU.mult), t, t_fr)
            yb["y"][x_] = p.dma("sync", c_out[x_], out[0, 128 * i:128 * i + 128, :], YT[x_], t)
        done()


def constants():
    f = np.float32
    i = np.arange(128)
    cst = np.zeros((128, 6, 128), f)
    cst[:, 0] = np.eye(128)
    cst[:, 1] = i[:, None] <= i[None, :]
    cst[:, 2] = i[:, None] >= i[None, :]
    cst[:, 3] = np.where(i[:, None] >= i[None, :], 0, BIG)
    cst[:, 4] = np.where(i[:, None] <= i[None, :], 0, BIG)
    cst[:, 5] = 1
    msk = np.zeros((128, 14, 128), np.float32)
    for n, b in enumerate(MASKS):
        m = (i[:, None] // (2 * b) == i[None, :] // (2 * b)) & ((i[:, None] // b) % 2 == 1) & ((i[None, :] // b) % 2 == 0)
        msk[:, 2 * n] = m
        msk[:, 2 * n + 1] = m.T
    oh = np.zeros((128, 3, 384), f)
    off = np.arange(384) - 191
    for g, dil in enumerate((1, 4, 8)):
        rel = off * dil
        n = np.abs(rel)
        large = 8 + (np.log(np.maximum(n, 1) / 8) / np.log(1024 / 8) * 8).astype(np.int32)
        bucket = (rel > 0) * 16 + np.where(n < 8, n, np.minimum(large, 15))
        ok = (np.abs(off) <= 64) if g < 2 else (off % 2 == 0) & (np.abs(off) <= 128)
        oh[bucket[ok], g, np.arange(384)[ok]] = 1
        oh[32, g, ~ok] = 1
    pos = np.arange(1040, dtype=f)
    inv = np.power(f(500000.0), -np.arange(0, 16, 2, dtype=f) / f(16)).astype(f)
    ang = pos[:, None] * inv[None, :]
    rope = np.zeros((3, 128, 1040), f)
    rope[0] = 1
    for b in range(2):
        for d in range(8):
            rope[0, 64 * b + d] = rope[0, 64 * b + 8 + d] = np.cos(ang[:, d])
            rope[1, 64 * b + d] = rope[1, 64 * b + 8 + d] = np.sin(ang[:, d])
            rope[2, 64 * b + 8 + d, 64 * b + d] = -1
            rope[2, 64 * b + d, 64 * b + 8 + d] = 1
    return cst.reshape(128, 768), msk, oh, rope


def stream(inp):
    w_in = inp["w_in"][0]

    def cols(w, *starts):
        n = 256 // len(starts)
        a = np.concatenate([w[:, s:s + n] for s in starts], axis=1)
        k = a.shape[0] // 128
        a = a.reshape(k, 128, 256).transpose(1, 0, 2).reshape(128, -1)
        if a.shape[1] < SLOT:
            a = np.concatenate([a, np.zeros((128, SLOT - a.shape[1]), a.dtype)], axis=1)
        return a

    s = []
    for h in range(8):
        s.append(cols(w_in, 128 * h, 2048 + 128 * h))
        s.append(cols(w_in, 1024 + 128 * h, 3072 + 128 * h))
    qb, kb, vb = 4128, 4128 + 1536, 4128 + 3072
    for g in range(3):
        for base in (qb, kb, vb):
            for j in range(2):
                s.append(cols(w_in, base + 512 * g + 256 * j))
    ga = vb + 1536
    gb = ga + 1024
    for g0, w in ((ga, inp["w_branch_a"][0]), (gb, inp["w_branch_b"][0])):
        for j in range(4):
            s.append(cols(w_in, g0 + 256 * j))
            s.append(cols(w, 256 * j))
    for j in range(4):
        s.append(cols(inp["w_out"][0], 256 * j))
    w2 = inp["w_ff2"][0].reshape(16, 2, 128, 1024).transpose(0, 2, 1, 3).reshape(16, 128, 2048)
    f1 = [[cols(inp["w_ff1"][0], 512 * c + 256 * j) for j in range(2)] for c in range(8)]
    f2 = [[w2[2 * c], w2[2 * c + 1]] for c in range(8)]
    s += f1[0]
    FF = ff_order()
    for kind, c, j in FF:
        s.append(f1[c][j] if kind == 1 else f2[c][j])
    wi = inp["w_in_2"][0]
    for base in (2048, 1536, 2560, 512, 0, 1024):
        for j in range(2):
            s.append(cols(wi, base + 256 * j))
    for j in range(4):
        s.append(cols(inp["w_out_2"][0], 256 * j))
    return np.ascontiguousarray(np.stack(s))


def ff_order():
    order = []
    for c in range(8):
        if c < 7:
            a = (yield_order(1, c + 1), 8)
            b = (yield_order(2, c), 16)
            live = [[*a, 0], [*b, 0]]
            while live:
                t = min(live, key=lambda t: (t[2] + 1) / t[1])
                try:
                    order += next(t[0])
                    t[2] += 1
                except StopIteration:
                    live.remove(t)
        else:
            order += [(2, 7, 0), (2, 7, 1)]
    return order


def yield_order(kind, c):
    if kind == 1:
        for sl in range(2):
            for n in range(4):
                yield [(1, c, sl)] if n == 0 else []
    else:
        for n in range(16):
            yield [(2, c, 0), (2, c, 1)] if n == 0 else []


def kernel(**inputs):
    import concourse.bacc as _bacc
    from concourse.bass_utils import run_bass_kernel_spmd as _run

    inp = {k: np.asarray(v) for k, v in inputs.items()}
    nc = _bacc.Bacc("TRN2", target_bir_lowering=False, num_devices=1)
    arrays = {}

    def put(name, a):
        a = np.ascontiguousarray(a)
        arrays[name] = a
        return nc.dram_tensor(name, a.shape, mybir.dt.from_np(a.dtype), kind="ExternalInput").ap()

    def col(v):
        return v.reshape(-1, 128).T

    cst, msk, oh, rope = constants()
    w_in = inp["w_in"][0]
    wab = w_in[:, 4096:4128].reshape(8, 128, 32).transpose(1, 0, 2)
    cwt = inp["conv_w"][0].reshape(5, 24, 128).transpose(2, 1, 0)
    vecs = np.concatenate([
        col(inp["ln_mix_pre"][0]), col(inp["norm_a"][0]), col(inp["ln_mlp_pre"][0]), col(inp["norm_w_2"][0]),
        col(inp["subln_w_2"][0]), col(inp["conv_b_2"][0]), col(inp["b_rgate_2"][0]), col(inp["b_igate_2"][0]),
        col(inp["lru_L_2"][0])], axis=1)
    vecs = np.concatenate([vecs, np.zeros((128, 48 - vecs.shape[1]), vecs.dtype)], axis=1)
    gate = np.concatenate([inp["dt_bias_f"][0], inp["dt_bias_b"][0], inp["a_log_f"][0], inp["a_log_b"][0]])
    relb = np.concatenate([inp["rel_bias"], np.full((1, 12), NEG, np.float32), np.zeros((95, 12), np.float32)])
    lruw = np.stack([inp["w_rgate_2"][0], inp["w_igate_2"][0]])
    lqk = np.concatenate([inp["lambda_q1_2"][0], inp["lambda_k1_2"][0], inp["lambda_q2_2"][0], inp["lambda_k2_2"][0]])
    lam = {
        "lnpost": put("lnpost", inp["ln_mix_post"][0]), "lnmlppost": put("lnmlppost", inp["ln_mlp_post"][0]),
        "fnorm": put("fnorm", inp["final_norm_w_2"]), "lqk": put("lqk", lqk),
        "cw2": put("cw2", inp["conv_w_2"][0].reshape(4, 4, 128).transpose(2, 1, 0)),
    }
    out = nc.dram_tensor("out", (1, 1024, 1024), F32, kind="ExternalOutput").ap()
    dbg = nc.dram_tensor("dbg", (128, 12288), F32, kind="ExternalOutput").ap() if STOP < 99 else None
    program(nc, put("x", inp["x"]), put("wst", stream(inp)), put("wab", wab), put("cwt", cwt), put("vecs", vecs),
            put("gate", gate), put("relb", relb), put("meta", inp["meta_tokens_2"]), lam, put("lruw", lruw),
            put("cst", cst), put("onehot", oh), put("rope", rope), put("msk", msk), out, dbg)
    r = _run(nc, [arrays], core_ids=[0])
    return r.results[0]["out"]
```

```python
from contextlib import ExitStack

import numpy as np
import concourse.bass as bass
from concourse import mybir

ALU = mybir.AluOpType
ACT = mybir.ActivationFunctionType
AX = mybir.AxisListType
F32 = mybir.dt.float32
F32R = mybir.dt.float32r
U8 = mybir.dt.uint8

P = 128
S = 1024
KT = 8
H = 8
EPS = 1e-6
NEG = -1e30
BIG = 1e30
SLOT = 2048
STOP = 99
SP = [(0.112, 0.363), (0.022, 0.973), (0.088, 1.048), (0.103, 0.964), (0.155, 1.097)]

MASKS = [1, 2, 4, 8, 16, 32, 64]


class Program:

    def __init__(self, nc, ctx):
        self.nc, self.ctx = nc, ctx
        self.names = ["tensor", "vector", "scalar", "gpsimd", "sync"]
        self.queue = {e: [] for e in self.names}
        self.sem = {e: ctx.enter_context(nc.semaphore("s_" + e)) for e in self.names}
        self.count = {e: 0 for e in self.names}
        self.seen = {e: {} for e in self.names}

    def channel(self, name):
        self.sem[name] = self.ctx.enter_context(self.nc.semaphore("d_" + name))
        self.count[name] = 0
        return name

    def waits(self, eng, deps):
        need = {}
        for name, n in flat(deps):
            if n > self.seen[eng].get(name, 0):
                need[name] = max(n, need.get(name, 0))
        for name, n in need.items():
            self.seen[eng][name] = n
            self.queue[eng].append(("wait", self.sem[name], n))

    def op(self, eng, fn, *deps):
        self.waits(eng, deps)
        self.queue[eng].append(("do", fn, self.sem[eng], 1))
        self.count[eng] += 1
        return (eng, self.count[eng])

    def quiet(self, eng, fn, *deps):
        self.waits(eng, deps)
        self.queue[eng].append(("do", fn, None, 0))

    def dma(self, eng, chan, out, in_, *deps):
        self.waits(eng, deps)
        self.queue[eng].append(("do", lambda e: e.dma_start(out, in_), self.sem[chan], 16))
        self.count[chan] += 16
        return (chan, self.count[chan])

    def now(self, *engs):
        return [(e, self.count[e]) for e in engs if self.count[e]]

    def pe(self, fn, *deps):
        return self.op("tensor", fn, *deps)

    def dve(self, fn, *deps):
        return self.op("vector", fn, *deps)

    def act(self, fn, *deps):
        return self.op("scalar", fn, *deps)

    def pool(self, fn, *deps):
        return self.op("gpsimd", fn, *deps)

    def emit(self, block):
        def play(name):
            def body(eng):
                for item in self.queue[name]:
                    if item[0] == "wait":
                        eng.wait_ge(item[1], item[2])
                    else:
                        ins = item[1](eng)
                        if item[2] is not None:
                            ins.then_inc(item[2], item[3])
            return body

        block.tensor(play("tensor"))
        block.vector(play("vector"))
        block.scalar(play("scalar"))
        block.gpsimd(play("gpsimd"))
        block.sync(play("sync"))


def flat(deps):
    for d in deps:
        if d is None:
            continue
        if isinstance(d, tuple) and len(d) == 2 and isinstance(d[0], str):
            yield d
        else:
            yield from flat(d)


class Weights:

    def __init__(self, p, src, places):
        self.p, self.src = p, src
        self.places = [(ap, p.channel(f"w{i}")) for i, ap in enumerate(places)]
        self.next = 0
        self.keep = len(places)
        self.ready = []
        for pl in list(self.places):
            self.load(pl)

    def load(self, place, *deps):
        if self.next < self.src.shape[0]:
            ap, chan = place
            t = self.p.dma("sync", chan, ap, self.src[self.next], *deps)
            self.ready.append((place, t))
            self.next += 1

    def add(self, ap, *deps):
        place = (ap, self.p.channel(f"w{len(self.places)}"))
        self.places.append(place)
        self.load(place, *deps)

    def get(self):
        return self.ready.pop(0)

    def release(self, place, *deps):
        if self.places.index(place) < self.keep:
            self.load(place, *deps)


class Split:

    def __init__(self, p, w, sets, free):
        self.p, self.w, self.sets = p, w, sets
        self.free = [free] * len(sets)
        self.n = 0
        self.ready = []

    def ahead(self):
        k = self.n % len(self.sets)
        self.n += 1
        hi, lo = self.sets[k]
        place, t = self.w.get()
        raw = place[0]
        th = self.p.act(lambda e: e.activation(hi, raw, ACT.Copy), t, self.free[k])
        tl = self.p.dve(lambda e: e.tensor_tensor(lo, raw, hi.bitcast(F32), ALU.subtract), th, self.free[k], t)
        self.w.release(place, tl)
        self.ready.append((hi, lo, k, tl))

    def get(self, more=True):
        if not self.ready:
            self.ahead()
        if more:
            self.ahead()
        return self.ready.pop(0)

    def done(self, k, tok):
        self.free[k] = tok


def interleave(*threads):
    live = [[g, n, 0, *(span or (0.0, 1.0))] for g, n, *span in threads]
    while live:
        t = min(live, key=lambda t: t[3] + (t[4] - t[3]) * (t[2] + 1) / t[1])
        try:
            next(t[0])
            t[2] += 1
        except StopIteration:
            live.remove(t)


def bc(ap, *shape):
    return ap.to_broadcast(list(shape))


def program(nc, x, wst, wab, cwt, vecs, gate, relb, meta, lam, lruw, cst, onehot, rope, msk, out, dbg):
    with ExitStack() as ctx:
        wins = {}
        for off, n in ([(0, 8192), (39488, 8192), (51776, 128), (51904, 128)] + [(1024 * i, 1024) for i in range(8)]
                       + [(39488 + 1024 * i, 1024) for i in range(8)] + [(SLOT * i, SLOT) for i in (6, 7, 13, 14, 15, 16, 17, 18)]
                       + [(30720 + SLOT * i, SLOT) for i in range(4)] + [(47680, SLOT), (49728, SLOT)]):
            if (off, n) not in wins:
                with ExitStack() as c2:
                    if off:
                        c2.enter_context(nc.sbuf_tensor(f"b{off}_{n}", [P, off], F32))
                    wins[off, n] = c2.enter_context(nc.sbuf_tensor(f"r{off}_{n}", [P, n], F32R))
        ar = ctx.enter_context(nc.sbuf_tensor("ar", [P, 52640], F32))
        mk = ctx.enter_context(nc.sbuf_tensor("mk", [P, 14, 128], U8))
        ps = ctx.enter_context(nc.psum_tensor("ps", [P, 4096], F32))
        sc_o = nc.dram_tensor("sc_o", [8, P, 1024], F32, kind="Internal").ap()
        sc_b = nc.dram_tensor("sc_b", [3, 1024, 520], F32, kind="Internal").ap()
        sc_x = nc.dram_tensor("sc_x", [2, 1024, 1024], F32, kind="Internal").ap()
        sc_t = nc.dram_tensor("sc_t", [12, P * 384 + 256], F32, kind="Internal").ap()
        p = Program(nc, ctx)

        def view(v, shape):
            if len(shape) == 2:
                v = v.rearrange("p (a b) -> p a b", a=shape[0])
            if len(shape) == 3:
                v = v.rearrange("p (a b c) -> p a b c", a=shape[0], b=shape[1])
            return v

        def A(off, *shape):
            return view(ar[:, off:off + int(np.prod(shape))], shape)

        def R_(off, *shape):
            return view(wins[off, int(np.prod(shape))][:, :], shape)

        def bank(i, n=512):
            return ps[:, 512 * i:512 * i + n]

        ld = p.channel("ld")
        hT = A(0, KT, S)
        W = Weights(p, wst, [A(8192 + SLOT * i, SLOT) for i in range(4)])

        C0 = 16384
        ident, Um, Lm, MxF, MxB, ones = [A(C0 + 128 * i, 128) for i in range(6)]
        gates0 = C0 + 768
        names = ["g", "beta", "nbeta", "gc", "egl", "dec", "bgc", "tmpg"]
        gt = {n: A(gates0 + 128 * i, 8, 16) for i, n in enumerate(names)}
        V0 = gates0 + 1024
        cw = A(V0, 24, 5)
        vc = A(V0 + 120, 48)
        small = A(V0 + 168, 88)
        t_c = p.dma("scalar", ld, A(C0, 768), cst)
        t_c = p.dma("scalar", ld, cw[:, :, :], cwt)
        t_c = p.dma("scalar", ld, vc, vecs)
        mkf = A(18432 + 12288, 14, 128)
        t_c = p.dma("scalar", ld, mkf, msk)
        LNPRE, NORMA, LNMLP, NW2, SUB, CB, BR, BI, LRUL = 0, 8, 9, 17, 25, 26, 30, 34, 38
        R = 18432
        wabt = A(50560, 8, 32)
        t_c = p.dma("scalar", ld, wabt, wab)
        dtb = A(50816, 32)
        t_c = p.dma("scalar", ld, dtb, gate.partition_broadcast(P))
        xin = A(R + 1024, 8, 1024)
        xl_tok = []
        for i in range(8):
            c = p.channel(f"x{i}")
            xl_tok.append(p.dma("scalar", c, xin[:, i, :], x[0, 128 * i:128 * i + 128, :]))
        t_cw = p.dve(lambda e: e.tensor_scalar(A(V0, 120), A(V0, 120), 0.5, None, ALU.mult), t_c)

        t_mk = p.dve(lambda e: e.tensor_copy(mk[:, :, :], mkf), t_c)
        mh_t = small[:, 81:82]
        t_m = p.pool(lambda e: e.memset(mh_t, -0.5))

        def rstd(ss, n, scale, *deps, eps=EPS):
            t = p.dve(lambda e: e.tensor_scalar(ss, ss, scale, eps, ALU.mult, ALU.add), *deps)
            return p.pool(lambda e: e.tensor_tensor(ss, ss, bc(mh_t, P, n), ALU.pow), t, t_m)

        def transposed(src, t, dst, wcol, banks, free):
            toks = []
            for hf in range(2):
                b = bank(banks[hf])
                for j in range(4):
                    kt = 4 * hf + j
                    tp = p.pe(lambda e, kt=kt, j=j, b=b: e.transpose(b[:, 128 * j:128 * j + 128], src[:, 128 * kt:128 * kt + 128], ident), t, t_c, free[hf])
                ev = None
                for j in range(4):
                    kt = 4 * hf + j
                    if hf == 0:
                        ev = p.act(lambda e, kt=kt, j=j, b=b: e.activation(dst[:, kt, :], b[:, 128 * j:128 * j + 128], ACT.Copy, scale=vc[:, wcol + kt:wcol + kt + 1]), tp)
                    else:
                        ev = p.dve(lambda e, kt=kt, j=j, b=b: e.tensor_scalar(dst[:, kt, :], b[:, 128 * j:128 * j + 128], vc[:, wcol + kt:wcol + kt + 1], None, ALU.mult), tp)
                toks.append(ev)
            return toks, tp

        def mm3(o, l, r, first, last, *deps):
            p.quiet("tensor", lambda e: e.matmul(o, l[0], r[0], start=first, stop=False), *deps)
            p.quiet("tensor", lambda e: e.matmul(o, l[0], r[1], start=False, stop=False))
            return p.pe(lambda e: e.matmul(o, l[1], r[0], start=False, stop=last))

        def normed(src, tok, stat, row, trow, junk, junk_free, n=P):
            t = p.act(lambda e: e.activation(junk, src, ACT.Square, accum_out=stat), tok, junk_free)
            t = p.dve(lambda e: e.tensor_scalar(stat, stat, 1.0 / 1024, EPS, ALU.mult, ALU.add), t)
            t = p.pool(lambda e: e.tensor_tensor(stat, stat, mh_t[0:n, :], ALU.pow), t, t_m)
            return p.dve(lambda e: e.scalar_tensor_tensor(out=junk, in0=src, scalar=stat, in1=row, op0=ALU.mult, op1=ALU.mult), t, trow)

        def split_transposed(junk, t, hi, lo, banks, free, n=P):
            toks = []
            for hf in range(2):
                b = bank(banks[hf])
                for j in range(4):
                    kt = 4 * hf + j
                    tp = p.pe(lambda e, kt=kt, j=j, b=b: e.transpose(b[:, n * j:n * j + n], junk[:, 128 * kt:128 * kt + 128], ident[0:n, 0:n]), t, t_c, free[hf])
                b3 = b[:, 0:4 * n].rearrange("p (j n) -> p j n", j=4)
                h_, l_ = hi[:, 4 * hf:4 * hf + 4, :], lo[:, 4 * hf:4 * hf + 4, :]
                ev = p.act(lambda e, b3=b3, h_=h_: e.activation(h_, b3, ACT.Copy), tp)
                ev = p.dve(lambda e, b3=b3, h_=h_, l_=l_: e.tensor_tensor(l_, b3, h_.bitcast(F32), ALU.subtract), ev)
                toks.append(ev)
            return toks, tp

        free = {b: None for b in range(8)}
        junks = [A(R + 1024 + 8192 + 1024 * i, 1024) for i in range(2)]
        jf = [None, None]
        sq = []
        for i in range(8):
            t = p.act(lambda e, i=i: e.activation(junks[i % 2], xin[:, i, :], ACT.Square, accum_out=small[:, i:i + 1]), xl_tok[i], sq[i - 2] if i > 1 else None)
            sq.append(t)
            if i % 2 == 1:
                c = slice(i - 1, i + 1)
                t = rstd(small[:, c], 2, 1.0 / 1024, t)
                for k in (i - 1, i):
                    t2 = p.dve(lambda e, k=k: e.tensor_scalar(xin[:, k, :], xin[:, k, :], small[:, k:k + 1], None, ALU.mult), t, sq[k])
                    jf.append(t2)
        for i in range(8):
            b0 = 2 * (i % 4)
            toks, tp = transposed(xin[:, i, :], jf[2 + i], hT[:, :, 128 * i:128 * i + 128], LNPRE, (b0, b0 + 1), (free[b0], free[b0 + 1]))
            free[b0], free[b0 + 1] = toks
            t_h = toks
        t_h = list(t_h)

        t_gate = []

        def gates():
            pg = bank(4)
            for i in range(8):
                for kt in range(8):
                    t = p.pe(lambda e, i=i, kt=kt: e.matmul(pg[:, 32 * i:32 * i + 32], hT[:, kt, 128 * i:128 * i + 128], wabt[:, kt, :], start=(kt == 0), stop=(kt == 7)), t_h, t_c, p0)
                yield
            pgv = pg[:, 0:256].rearrange("p (c n) -> p c n", c=8)
            ga = gt["g"]
            tm = gt["tmpg"]

            def rows(off):
                return dtb[:, off:off + 16].rearrange("p (a n) -> p a n", a=1).to_broadcast([P, 8, 16])

            t = tga = p.dve(lambda e: e.tensor_tensor(ga, pgv[:, :, 0:16], rows(0), ALU.add), t, t_c)
            t2 = tabs = p.act(lambda e: e.activation(tm, ga, ACT.Abs), t)
            t2 = p.act(lambda e: e.activation(tm, tm, ACT.Exp, scale=-1.0), t2)
            t3 = p.act(lambda e: e.activation(dtb[:, 16:32], dtb[:, 16:32], ACT.Exp), t_c)
            t2 = p.act(lambda e: e.activation(tm, tm, ACT.Ln, bias=1.0), t2)
            t = p.dve(lambda e: e.tensor_scalar(ga, ga, 0.0, None, ALU.max), t, tabs)
            t = p.dve(lambda e: e.tensor_tensor(ga, ga, tm, ALU.add), t, t2)
            t = p.dve(lambda e: e.tensor_tensor(ga, ga, rows(16), ALU.mult), t, t3)
            t = p.dve(lambda e: e.tensor_scalar(ga, ga, -1.0, None, ALU.mult), t)
            yield
            be = gt["beta"]
            tb = p.act(lambda e: e.activation(be, pgv[:, :, 16:32], ACT.Exp, scale=-1.0), tga)
            tb = p.dve(lambda e: e.tensor_scalar(be, be, 1.0, None, ALU.add), tb)
            tb = p.dve(lambda e: e.reciprocal(be, be), tb)
            tb2 = p.dve(lambda e: e.tensor_scalar(gt["nbeta"], be, -1.0, None, ALU.mult), tb)
            yield
            pc = bank(5)
            tg = p.pe(lambda e: e.matmul(pc[:, 0:64], Um, ga[:, :, 0:8], start=True, stop=True), t, p0)
            tg = p.pe(lambda e: e.matmul(pc[:, 64:128], Lm, ga[:, :, 8:16], start=True, stop=True), t)
            tg = p.pe(lambda e: e.matmul(pc[:, 128:256], ones, A(gates0, 128), start=True, stop=True), t)
            yield
            tk = p.dve(lambda e: e.tensor_copy(gt["gc"][:, :, 0:8], pc[:, 0:64].rearrange("p (c n) -> p c n", c=8)), tg)
            tk = p.dve(lambda e: e.tensor_copy(gt["gc"][:, :, 8:16], pc[:, 64:128].rearrange("p (c n) -> p c n", c=8)), tg)
            td = p.dve(lambda e: e.tensor_tensor(A(gates0 + 128 * 5, 128), pc[:, 128:256], A(gates0 + 128 * 3, 128), ALU.subtract), tk)
            t1 = p.act(lambda e: e.activation(gt["dec"], gt["dec"], ACT.Exp), td)
            t1 = p.act(lambda e: e.activation(A(gates0 + 128 * 4, 128), pc[:, 128:256], ACT.Exp), td)
            tegl = t1
            t1 = p.act(lambda e: e.activation(gt["bgc"], gt["gc"], ACT.Exp), tk)
            t_gate.extend([tegl, p.dve(lambda e: e.tensor_tensor(gt["bgc"], gt["bgc"], be, ALU.mult), t1, tb2)])
            yield

        raw = [A(R + 1028 * i, 1028) for i in range(2)]
        o = R + 2056
        tmp = [A(o + 1024 * i, 1024) for i in range(2)]
        o += 2048
        chq = [A(o + 1024 * i, 1024) for i in range(2)]
        o += 2048
        chk = [A(o + 1024 * i, 1024) for i in range(2)]
        o += 2048
        sqk = [A(o + 1024 * i, 1024) for i in range(2)]
        o += 2048
        sqv = [A(o + 1024 * i, 1024) for i in range(2)]
        o += 2048
        zt = [A(o + 1024 * i, 1024) for i in range(2)]
        o += 2048
        G0 = o
        Gb = [[{n: A(o + 4096 * q + 2048 * d + 512 * j, 512) for j, n in enumerate(("u", "WT", "aq", "qs"))}
               for d in range(2)] for q in range(2)]
        o += 8192
        OC0 = o
        oc = [A(o + 1024 * i, 1024) for i in range(2)]
        o += 2048
        Sb = o
        o += 1280
        iv = [{n: A(o + 3072 * d + 512 * j, 512) for j, n in enumerate(("gam", "A", "AT", "T", "TT", "Y"))}
              for d in range(2)]
        o += 6144
        ssq = A(o, 16)
        ssk = A(o + 16, 16)
        sso = A(o + 32, 16)
        assert o + 48 <= 52640

        p0 = p.now("tensor", "vector", "scalar", "gpsimd")
        tz = None
        for i in range(2):
            tz = p.pool(lambda e, i=i: e.memset(raw[i][:, 0:2], 0.0), p0)
            tz = p.pool(lambda e, i=i: e.memset(raw[i][:, 1026:1028], 0.0))
        tt = {"raw": [tz, tz], "tmp": [p0, p0], "bk": [p0, p0], "n": 0, "open": None}
        free_q = [p0, p0]
        free_k = [p0, p0]
        free_sk = [p0, p0]
        free_v = [p0, p0]
        free_z = [p0, p0]
        ready = {}

        def gbank():
            b = tt["n"] % 2
            if b == tt["open"]:
                b = 1 - b
            tt["n"] = b + 1
            return b, bank(b), tt["bk"][b]

        def proj(slot, tw, col, dst, rtok, scale=1.0):
            wv = slot.rearrange("p (k n) -> p k n", k=8)
            toks = []
            for hf in range(2):
                b, bk, fr = gbank()
                tt["open"] = b
                for kt in range(8):
                    tp = p.pe(lambda e, kt=kt, hf=hf, bk=bk: e.matmul(bk, wv[:, kt, col:col + 128], hT[:, kt, 512 * hf:512 * hf + 512], start=(kt == 0), stop=(kt == 7)), tw, fr, t_h)
                    if kt % 2 == 1:
                        yield
                ev = p.act(lambda e, hf=hf, bk=bk: e.activation(dst[:, 512 * hf:512 * hf + 512], bk, ACT.Copy, scale=scale), tp, rtok)
                tt["bk"][b] = ev
                tt["open"] = None
                toks.append(ev)
            proj.tok, proj.pe = toks[1], tp

        def flip(src, dst_fn, stok):
            for hf in range(2):
                b, bk, fr = gbank()
                for j in range(4):
                    c = 4 * hf + j
                    tp = p.pe(lambda e, c=c, j=j, bk=bk: e.transpose(bk[:, 128 * j:128 * j + 128], src[:, 128 * c:128 * c + 128], ident), stok, fr)
                flip.tok = dst_fn(hf, bk, tp)
                flip.pe = tp
                tt["bk"][b] = flip.tok
                yield

        def copy_to(dst, dfree):
            return lambda hf, bk, tp: p.act(lambda e: e.activation(dst[:, 512 * hf:512 * hf + 512], bk, ACT.Copy), tp, dfree)

        def conv(r, h, which, cidx, dst, dfree):
            t = proj.tok
            w = cw[:, cidx, :]
            tp = p.dve(lambda e: e.tensor_scalar(tmp[0], raw[r][:, 0:1024], w[:, 0:1], None, ALU.mult), t, tt["tmp"][0], t_cw)
            yield
            for j in range(1, 5):
                tp = p.dve(lambda e, j=j: e.scalar_tensor_tensor(out=tmp[0], in0=raw[r][:, j:j + 1024], scalar=w[:, j:j + 1], in1=tmp[0], op0=ALU.mult, op1=ALU.add), tp)
                yield
            tt["raw"][r] = tp
            ta = p.act(lambda e: e.activation(tmp[1], tmp[0], ACT.Tanh), tp, tt["tmp"][1])
            td = p.dve(lambda e: e.scalar_tensor_tensor(out=dst, in0=tmp[1], scalar=1.0, in1=tmp[0], op0=ALU.add, op1=ALU.mult), ta, dfree)
            tt["tmp"] = [td, td]
            conv.tok = td
            yield

        def unit(seq, ss, stok, scale):
            for c in range(8):
                if c % 2 == 0:
                    yield
                ta = p.act(lambda e, c=c: e.activation(tmp[1][:, 128 * c:128 * c + 128], seq[:, 128 * c:128 * c + 128], ACT.Square, accum_out=ss[:, c:c + 1]), stok, tt["tmp"][1])
            t = rstd(ss[:, 0:8], 8, 1.0, ta)
            if scale != 1.0:
                t = p.dve(lambda e: e.tensor_scalar(ss[:, 0:8], ss[:, 0:8], scale, None, ALU.mult), t)
            s3 = seq.rearrange("p (c n) -> p c n", c=8)
            tt["tmp"][1] = ta
            unit.tok = p.dve(lambda e: e.tensor_tensor(s3, s3, ss[:, 0:8].rearrange("p (c n) -> p c n", n=1).to_broadcast([P, 8, 128]), ALU.mult), t)

        def prep0(h):
            q = h % 2
            place, tw = W.get()
            yield from proj(place[0], tw, 0, raw[0][:, 2:1026], tt["raw"][0])
            yield from conv(0, h, "q", h, chq[q], free_q[q])
            td = conv.tok
            yield from proj(place[0], tw, 128, raw[1][:, 2:1026], tt["raw"][1])
            W.release(place, proj.pe)
            yield from flip(chq[q], copy_to(tmp[0], tt["tmp"][0]), td)
            yield from unit(tmp[0], ssq, flip.tok, 128.0 ** -0.5)
            ts = unit.tok
            yield
            yield from flip(tmp[0], copy_to(chq[q], flip.pe), ts)
            ready["q", h] = flip.tok
            tt["tmp"][0] = flip.pe
            yield from conv(1, h, "v", 16 + h, tmp[1], None)
            td = conv.tok
            yield
            yield from flip(tmp[1], copy_to(sqv[q], free_v[q]), td)
            tt["tmp"][1] = flip.pe
            ready["v", h] = flip.tok

        def prep1(h):
            q = h % 2
            place, tw = W.get()
            yield from proj(place[0], tw, 0, raw[0][:, 2:1026], tt["raw"][0])
            yield from conv(0, h, "k", 8 + h, chk[q], free_k[q])
            td = conv.tok
            yield from flip(chk[q], copy_to(sqk[q], free_sk[q]), td)
            yield from unit(sqk[q], ssk, flip.tok, 1.0)
            ts = unit.tok
            assert h < 2 or ("fin", h - 2) in ready
            yield from proj(place[0], tw, 128, zt[q], free_z[q], scale=0.5)
            W.release(place, proj.pe)
            yield from flip(sqk[q], copy_to(chk[q], flip.pe), ts)
            ready["k", h] = [flip.tok, ts]
            ta = p.act(lambda e: e.activation(tmp[1], zt[q], ACT.Tanh), proj.tok, tt["tmp"][1])
            td = p.dve(lambda e: e.scalar_tensor_tensor(out=zt[q], in0=tmp[1], scalar=1.0, in1=zt[q], op0=ALU.add, op1=ALU.mult), ta)
            tt["tmp"][1] = td
            ready["z", h] = td
            yield

        ivf = [{"gam": p0, "A": p0, "AT": p0, "T": p0, "TT": p0, "Y": p0, "b0": p0, "b1": p0} for d in range(2)]
        gfree = [[p0, p0], [p0, p0]]
        gready = {}

        def invert(h, part, d):
            c0 = 4 * (part if d == 0 else 1 - part)
            q = h % 2
            G = Gb[part][d]
            b = iv[d]
            f = ivf[d]
            gf = gfree[part][d]
            B0, B1 = bank(2 + 2 * d), bank(3 + 2 * d)
            tri, mx = (Um, MxF) if d == 0 else (Lm, MxB)
            cs = [(128 * c, 128 * j, gt, d * 8 + h, c) for j, c in enumerate(range(c0, c0 + 4))]

            def col(n, c):
                return gt[n][:, c, d * 8 + h:d * 8 + h + 1]

            def cols(n):
                return gt[n][:, c0:c0 + 4, d * 8 + h:d * 8 + h + 1].to_broadcast([P, 4, 128])

            def four(ap):
                return ap.rearrange("p (c n) -> p c n", c=4)

            def all4(ap):
                return ap.rearrange("p (c n) -> p c n", c=1).to_broadcast([P, 4, 128])

            def mm4(B, lhs, rhs, *deps):
                for j in range(4):
                    t = p.pe(lambda e, j=j: e.matmul(B[:, 128 * j:128 * j + 128], lhs(j), rhs(j), start=True, stop=True), *deps)
                return t

            def tr4(B, src, *deps):
                for j in range(4):
                    t = p.pe(lambda e, j=j: e.transpose(B[:, 128 * j:128 * j + 128], src[:, 128 * j:128 * j + 128], ident), *deps)
                return t

            def half(ap, n, h_):
                return ap.rearrange("p (m t b) -> p t m b", t=2, b=MASKS[n])[:, h_, :, :]

            def half4(ap, n, h_):
                return ap.rearrange("p (c m t b) -> p t c m b", c=4, t=2, b=MASKS[n])[:, h_, :, :, :]

            def halfm(ap, n, h_):
                m = 64 // MASKS[n]
                v = half(ap, n, h_)
                return v.rearrange("p (c m) b -> p c m b", c=1).to_broadcast([P, 4, m, MASKS[n]])

            def mm4h(B, lhs, rhs, n, h_, *deps):
                for j in range(4):
                    r = slice(128 * j, 128 * j + 128)
                    t = p.pe(lambda e, j=j, r=r: e.matmul(half(B[:, r], n, h_), lhs(j), half(rhs[:, r], n, h_), start=True, stop=True), *deps)
                return t

            def part4(ap):
                return lambda j: ap[:, 128 * j:128 * j + 128]

            kq = lambda j: chk[q][:, 128 * (c0 + j):128 * (c0 + j) + 128]
            qq = lambda j: chq[q][:, 128 * (c0 + j):128 * (c0 + j) + 128]
            tp = mm4(B0, lambda j: bc(col("g", c0 + j), P, 128), lambda j: tri, t_gate, f["b0"])
            tk = mm4(B1, kq, kq, ready["k", h], f["b1"])
            yield
            te = p.act(lambda e: e.activation(b["Y"], B0, ACT.Exp), tp, f["Y"])
            ti2 = p.act(lambda e: e.activation(four(b["TT"]), all4(ident), ACT.Copy), f["TT"])
            for j in range(4):
                tg = p.dve(lambda e, j=j: e.scalar_tensor_tensor(out=b["gam"][:, 128 * j:128 * j + 128], in0=B0[:, 128 * j:128 * j + 128], scalar=col("gc", c0 + j), in1=mx, op0=ALU.subtract, op1=ALU.max), te, f["gam"])
            tg = p.act(lambda e: e.activation(b["gam"], b["gam"], ACT.Exp, scale=-1.0), tg)
            tq = p.pool(lambda e: e.tensor_tensor(G["qs"], chq[q][:, 128 * c0:128 * c0 + 512], b["Y"], ALU.mult), te, gf, ready["q", h])
            yield
            tpq = mm4(B0, qq, kq, te, tg)
            for j in range(4):
                ta = p.dve(lambda e, j=j: e.scalar_tensor_tensor(out=b["A"][:, 128 * j:128 * j + 128], in0=B1[:, 128 * j:128 * j + 128], scalar=col("nbeta", c0 + j), in1=b["gam"][:, 128 * j:128 * j + 128], op0=ALU.mult, op1=ALU.mult), tg, tk, f["A"])
            ta2 = p.dve(lambda e: e.tensor_tensor(b["T"], B0, b["gam"], ALU.mult), tpq, f["T"])
            yield
            tr = tr4(B1, b["A"], ta)
            tra = tr4(B0, b["T"], ta2)
            yield
            tat = p.act(lambda e: e.activation(b["AT"], B1, ACT.Copy), tr, f["AT"])
            ti = p.act(lambda e: e.activation(four(b["T"]), all4(ident), ACT.Copy), tra)
            taq = p.act(lambda e: e.activation(G["aq"], B0, ACT.Copy), tra, gf)
            mi = lambda n, tr_: mk[:, 2 * n + (tr_ ^ d), :]
            tT = p.dve(lambda e: e.copy_predicated(four(b["T"]), all4(mi(0, 0)), four(b["A"])), ti, ta, t_mk)
            tTT = p.dve(lambda e: e.copy_predicated(four(b["TT"]), all4(mi(0, 1)), four(b["AT"])), ti2, tat)
            yield
            tv = p.pool(lambda e: e.tensor_tensor(four(b["gam"]), sqv[q][:, 128 * c0:128 * c0 + 512].rearrange("p (c n) -> p c n", c=4), cols("beta"), ALU.mult), ta2, ta, ready["v", h])
            tkb = p.pool(lambda e: e.tensor_tensor(four(b["A"]), sqk[q][:, 128 * c0:128 * c0 + 512].rearrange("p (c n) -> p c n", c=4), cols("bgc"), ALU.mult), tT, tr, ready["k", h])
            yfree = tq
            b0f, b1f = [taq], [tat]
            for n in range(1, 7):
                tp = mm4h(B0, part4(b["AT"]), b["T"], n, d, tT, tat, b0f)
                yield
                ty = p.act(lambda e, n=n: e.activation(half(b["Y"], n, d), half(B0, n, d), ACT.Copy), tp, yfree)
                if n < 6:
                    tp1 = mm4h(B1, part4(b["TT"]), b["Y"], n, d, ty, tTT, b1f)
                tp0 = mm4h(B0, part4(b["Y"]), b["TT"], n, 1 - d, ty, tTT)
                yfree = tp0
                yield
                if n < 6:
                    tT = p.dve(lambda e, n=n: e.copy_predicated(half4(b["T"], n, d), halfm(mi(n, 0), n, d), half4(B1, n, d)), tp1, tp)
                    b1f = [tT]
                tTT = p.dve(lambda e, n=n: e.copy_predicated(half4(b["TT"], n, 1 - d), halfm(mi(n, 1), n, 1 - d), half4(B0, n, 1 - d)), tp0, tp1)
                b0f = [tTT]
            tu = mm4(B1, part4(b["TT"]), part4(b["gam"]), tTT, tv, b1f)
            tw = mm4(B0, part4(b["A"]), part4(b["TT"]), tkb, b0f)
            yield
            e1 = p.act(lambda e: e.activation(G["u"], B1, ACT.Copy), tu, gf)
            e0 = p.act(lambda e: e.activation(G["WT"], B0, ACT.Copy), tw, gf)
            f.update({"gam": tu, "A": tw, "AT": tp0, "T": tp, "TT": tw, "Y": tp0, "b0": e0, "b1": e1})
            gready[h, part, d] = [e0, e1, tq, taq]
            yield

        S2 = [ar[:, Sb + 256 * q:Sb + 256 * q + 256] for q in range(2)]
        V2 = ar[:, Sb + 512:Sb + 768]
        kd = [ar[:, Sb + 768 + 256 * q:Sb + 1024 + 256 * q] for q in range(2)]
        sf = {"S": p0, "v": p0, "A": p0, "O": p0, "kd": [p0, p0], "pe": p0, "n": 0}
        ofree = [p0, p0]
        odone = {}

        def pair(base, other):
            st = other - base
            return ar[:, base:base + 2 * st].rearrange("p (a b) -> p a b", a=2)[:, :, 0:128]

        def scan(h, part):
            q = h % 2
            f = sf
            B6, B7 = bank(6), bank(7)
            gr = [gready[h, part, 0], gready[h, part, 1]]
            G = Gb[part]
            if part == 0:
                f["S"] = p.pool(lambda e: e.memset(S2[f["n"] % 2], 0.0), f["S"], f["pe"])
            for n in range(4):
                So, Sn = S2[f["n"] % 2], S2[(f["n"] + 1) % 2]
                kk = kd[f["n"] % 2]
                cc = (4 * part + n, 7 - 4 * part - n)
                js = (n, 3 - n)
                sl = [slice(128 * j, 128 * j + 128) for j in js]
                for d in range(2):
                    tkd = p.pool(lambda e, d=d, kk=kk, c=cc[d]: e.tensor_scalar(kk[:, 128 * d:128 * d + 128], sqk[q][:, 128 * c:128 * c + 128], gt["dec"][:, c, d * 8 + h:d * 8 + h + 1], None, ALU.mult), f["kd"][f["n"] % 2], ready["k", h], t_gate)
                for d in range(2):
                    t1 = p.pe(lambda e, d=d, So=So, sl=sl: e.matmul(B6[:, 128 * d:128 * d + 128], G[d]["WT"][:, sl[d]], So[:, 128 * d:128 * d + 128], start=True, stop=True), f["S"], gr, f["A"])
                yield
                ub = pair(G0 + 4096 * part + 128 * js[0], G0 + 4096 * part + 2048 + 128 * js[1])
                V3 = V2.rearrange("p (a b) -> p a b", a=2)
                tv = p.dve(lambda e, ub=ub, V3=V3: e.tensor_tensor(V3, ub, B6[:, 0:256].rearrange("p (a b) -> p a b", a=2), ALU.subtract), t1, f["v"], gr)
                for d in range(2):
                    t4 = p.pe(lambda e, d=d, kk=kk: e.matmul(B6[:, 128 * d:128 * d + 128], kk[:, 128 * d:128 * d + 128], V2[:, 128 * d:128 * d + 128], start=True, stop=True), tkd, tv)
                f["kd"][f["n"] % 2] = t4
                for d in range(2):
                    r = d if part == 0 else 1 - d
                    p.quiet("tensor", lambda e, d=d, r=r, So=So, sl=sl: e.matmul(B7[:, 128 * r:128 * r + 128], G[d]["qs"][:, sl[d]], So[:, 128 * d:128 * d + 128], start=True, stop=False), f["O"])
                    t3 = p.pe(lambda e, d=d, r=r, sl=sl: e.matmul(B7[:, 128 * r:128 * r + 128], G[d]["aq"][:, sl[d]], V2[:, 128 * d:128 * d + 128], start=False, stop=True))
                yield
                for d in range(2):
                    egl = gt["egl"][:, cc[d], d * 8 + h:d * 8 + h + 1]
                    ts = p.dve(lambda e, d=d, egl=egl, So=So, Sn=Sn: e.scalar_tensor_tensor(out=Sn[:, 128 * d:128 * d + 128], in0=So[:, 128 * d:128 * d + 128], scalar=egl, in1=B6[:, 128 * d:128 * d + 128], op0=ALU.mult, op1=ALU.add), t4, f["pe"])
                lo, hi = min(cc), max(cc)
                od = pair(OC0 + 1024 * q + 128 * lo, OC0 + 1024 * q + 128 * hi)
                b3 = B7[:, 0:256].rearrange("p (a b) -> p a b", a=2)
                if part == 0:
                    to = p.act(lambda e, od=od, b3=b3: e.activation(od, b3, ACT.Copy), t3, ofree[q])
                else:
                    to = p.dve(lambda e, od=od, b3=b3: e.tensor_tensor(od, od, b3, ALU.add), t3, first[h])
                f.update({"S": ts, "v": t3, "A": ts, "O": to, "pe": t3})
                f["n"] += 1
                yield
            if part == 0:
                first[h] = to
            else:
                odone[h] = to
            gfree[part] = [[t3, tv], [t3, tv]]

        first = {}

        o_chan = [p.channel(f"o{i}") for i in range(2)]
        o_saved = []

        def finish_head(h):
            q = h % 2
            dn = odone[h]
            for c in range(8):
                ta = p.act(lambda e, c=c: e.activation(tmp[1][:, 128 * c:128 * c + 128], oc[q][:, 128 * c:128 * c + 128], ACT.Square, accum_out=sso[:, c:c + 1]), dn, tt["tmp"][1])
            t = rstd(sso[:, 0:8], 8, 1.0 / 128, ta)
            tt["tmp"][1] = ta
            o3 = oc[q].rearrange("p (c n) -> p c n", c=8)
            t = p.pool(lambda e: e.tensor_tensor(o3, o3, sso[:, 0:8].rearrange("p (c n) -> p c n", n=1).to_broadcast([P, 8, 128]), ALU.mult), t)
            yield

            def put(hf, bk, tp):
                z = zt[q][:, 512 * hf:512 * hf + 512]
                return p.dve(lambda e: e.scalar_tensor_tensor(out=z, in0=bk, scalar=vc[:, NORMA:NORMA + 1], in1=z, op0=ALU.mult, op1=ALU.mult), tp, ready["z", h])

            yield from flip(oc[q], put, t)
            ofree[q] = flip.pe
            t = p.dma("sync", o_chan[q], sc_o[h], zt[q], flip.tok)
            free_z[q] = t
            ready["fin", h] = t
            o_saved.append(t)

        def chain(*gens):
            for g in gens:
                yield from g

        interleave((chain(prep0(0), prep1(0)), 70), (gates(), 12, 0.0, 0.8))
        closing = []
        for s in range(17):
            threads = [(finish_head(g), 4, *SP[0]) for g in closing]
            closing = []
            h, part = divmod(s, 2)
            if s < 16:
                threads += [(invert(h, part, 0), 18, *SP[1]), (invert(h, part, 1), 18, *SP[2])]
            if s >= 1:
                hh, pp = divmod(s - 1, 2)
                threads.append((scan(hh, pp), 13, *SP[3]))
            if s < 14:
                threads.append((prep0(h + 1), 38, *SP[4]) if part == 0 else (prep1(h + 1), 32, *SP[4]))
            interleave(*threads)
            if s < 16:
                if part == 1:
                    last = p.now("tensor", "gpsimd")
                    free_q[h % 2] = free_k[h % 2] = free_v[h % 2] = last
            if s >= 1 and part == 0:
                free_sk[(h - 1) % 2] = p.now("tensor", "gpsimd")
                closing = [h - 1]

        for g in closing:
            for _ in finish_head(g):
                pass
        every = lambda: p.now("tensor", "vector", "scalar", "gpsimd")

        def done(src=None):
            if src is not None:
                t = p.dma("sync", ld, dbg[:, 0:src.shape[1]], src, every(), o_saved)
                p.waits("sync", [t])
            for c in p.count:
                if c not in p.names and p.count[c]:
                    p.waits("sync", [(c, p.count[c])])
            block = ctx.enter_context(nc.Block())
            p.emit(block)

        if STOP == 1:
            t = p.dma("sync", ld, A(R, 8192).rearrange("p (a n) -> p a n", a=8), sc_o.rearrange("a p n -> p a n"), every(), o_saved)
            p.waits("sync", [t])
            return done(A(R, 8192))

        p1 = every()
        o = R
        qp = [A(o + 8192 * i, 4, 1024) for i in range(2)]
        kp = [A(o + 8192 * i + 4096, 4, 1024) for i in range(2)]
        o += 16384
        Vt = A(o, 12, 512)
        o += 6144
        bias = [A(o, 4, 256), A(o + 1024, 4, 256), A(o + 2048, 4, 128)]
        o += 2560
        Lb = [A(o + 1024 * i, 1024) for i in range(2)]
        o += 2048
        PT = [A(o + 1024 * i, 1024) for i in range(2)]
        o += 2048
        Ob = [A(o + 520 * i, 520) for i in range(2)]
        o += 1040
        nm = [A(o + 4 * i, 4) for i in range(2)]
        o += 8
        oh = A(Vt_off := R + 16384, 3, 384)
        rb = A(Vt_off + 1152, 12)
        trow = [A(Vt_off + 1664 + 384 * i, 384) for i in range(2)]
        assert o <= 52640
        c_b = p.channel("bias")
        t_oh = p.dma("sync", c_b, oh, onehot, p1)
        t_oh = p.dma("sync", c_b, rb, relb, p1)
        c_t = [p.channel(f"t{i}") for i in range(2)]
        tfree = [p1, p1]
        bfree = p1
        for n in range(12):
            g = n // 4
            q = n % 2
            t = p.pe(lambda e, n=n, g=g: e.matmul(bank(7)[:, 0:384], bc(rb[0:33, n:n + 1], 33, 128), oh[0:33, g, :], start=True, stop=True), t_oh, bfree)
            t = p.act(lambda e, q=q: e.activation(trow[q], bank(7)[:, 0:384], ACT.Copy), t, tfree[q])
            bfree = t
            tfree[q] = p.dma("sync", c_t[q], sc_t[n][0:P * 384].rearrange("(a b) -> a b", a=P), trow[q], t)
        t_bias = None
        for n in range(12):
            g, hh = divmod(n, 4)
            if g < 2:
                src = sc_t[n][127:127 + 128 * 383].rearrange("(a b) -> a b", b=383)[:, 0:256]
                t_bias = p.dma("sync", c_b, bias[g][:, hh, :], src, tfree, p1)
            else:
                src = sc_t[n][191:191 + 128 * 383].rearrange("(a b) -> a b", b=383)[:, 0:128]
                t_bias = p.dma("sync", c_b, bias[2][:, hh, :], src, tfree, p1)
        bias_pe = p.now("tensor", "scalar")
        t_bias = [t_bias]

        DIL = (1, 4, 8)
        tt["bk"] = [p1, p1]
        qkfree = [p1, p1]
        qk_tok = {}

        def qk_proj(g):
            dil = DIL[g]
            L = S // dil
            for which, dstt, scale in ((0, qp[g % 2], 128.0 ** -0.5), (1, kp[g % 2], 1.0)):
                for sl in range(2):
                    place, tw = W.get()
                    wv = place[0].rearrange("p (k n) -> p k n", k=8)
                    for ct in range(2):
                        hd = 2 * sl + ct
                        for hf in range(2):
                            b, bk, fr = gbank()
                            for kt in range(8):
                                tp = p.pe(lambda e, kt=kt, hf=hf, bk=bk, ct=ct, wv=wv: e.matmul(bk, wv[:, kt, 128 * ct:128 * ct + 128], hT[:, kt, 512 * hf:512 * hf + 512], start=(kt == 0), stop=(kt == 7)), tw, fr)
                                if kt % 4 == 3:
                                    yield
                            n = 512 // dil
                            dv = dstt[:, hd, :].rearrange("p (r l) -> p l r", r=dil)[:, n * hf:n * hf + n, :]
                            sv = bk.rearrange("p (l r) -> p l r", r=dil)
                            ev = p.act(lambda e, dv=dv, sv=sv, scale=scale: e.activation(dv, sv, ACT.Copy, scale=scale), tp, qkfree[g % 2])
                            tt["bk"][b] = ev
                    W.release(place, tp)
            qk_tok[g] = ev

        vfree = [bias_pe, tfree]
        v_tok = {}

        def chunks(g):
            if g == 0:
                return [(0, 64)] + [(64 + 128 * i, 128) for i in range(7)] + [(960, 64)]
            if g == 1:
                return [(r * 256 + a, n) for r in range(4) for a, n in ((0, 64), (64, 128), (192, 64))]
            return [(128 * i, 128) for i in range(8)]

        def v_proj(g):
            dil = DIL[g]
            L = S // dil
            pl = [W.get(), W.get()]
            for i, (a, n) in enumerate(chunks(g)):
                b, bk, fr = gbank()
                for sl in range(2):
                    wv = pl[sl][0][0].rearrange("p (k n) -> p k n", k=8)
                    for kt in range(8):
                        r, l = divmod(a, L)
                        lh = hT[:, kt, r + dil * l:r + dil * l + dil * (n - 1) + 1:dil]
                        tp = p.pe(lambda e, kt=kt, bk=bk, sl=sl, wv=wv, lh=lh, n=n: e.matmul(bk[0:n, 256 * sl:256 * sl + 256], lh, wv[:, kt, :], start=(kt == 0), stop=(kt == 7)), pl[sl][1], fr)
                    yield
                ev = p.act(lambda e, bk=bk, i=i, n=n: e.activation(Vt[0:n, i, :], bk[0:n, :], ACT.Copy), tp, vfree)
                tt["bk"][b] = ev
            for sl in range(2):
                W.release(pl[sl][0], tp)
            v_tok[g] = ev

        def tiles(g):
            if g == 2:
                return [(128 * i, 128 * i, 128, 0, [(i, 0, 128)]) for i in range(8)]
            L = S // DIL[g]
            res = []
            ch = chunks(g)
            at = {a: (i, n) for i, (a, n) in enumerate(ch)}
            for r in range(DIL[g]):
                for i in range(L // 128):
                    q0 = 128 * i
                    k0, k1 = max(q0 - 64, 0), min(q0 + 192, L)
                    parts, k = [], k0
                    while k < k1:
                        ci, n = at[r * L + k]
                        parts.append((ci, k - k0, n))
                        k += n
                    res.append((r * L + q0, r * L + k0, k1 - k0, k0 - (q0 - 64), parts))
            return res

        af = {"S": p1, "T": p1, "U": p1, "L": [p1, p1], "PT": [p1, p1], "O": [p1, p1], "n": 0}
        c_ob = [p.channel(f"ob{i}") for i in range(2)]
        ob_saved = []

        def attend(g):
            dil = DIL[g]
            L = S // dil
            todo = tiles(g)
            kept = {}

            def logits(i):
                qo, ko, nk, bo, parts = todo[i]
                x_ = af["n"] % 2
                af["n"] += 1
                SP = ps[:, 1024:2048].rearrange("p (h n) -> p h n", h=4)
                for hh in range(4):
                    tp = p.pe(lambda e, hh=hh: e.matmul(SP[:, hh, 0:nk], qp[g % 2][:, hh, qo:qo + 128], kp[g % 2][:, hh, ko:ko + nk], start=True, stop=True), qk_tok[g], af["S"])
                L3 = Lb[x_].rearrange("p (h n) -> p h n", h=4)[:, :, 0:nk]
                t = p.dve(lambda e: e.tensor_tensor(L3, SP[:, :, 0:nk], bias[g][:, :, bo:bo + nk], ALU.add), tp, t_bias, af["L"][x_])
                af["S"] = t
                O = Ob[x_]
                t = p.dve(lambda e: e.tensor_reduce(O[:, 512:516], L3, AX.X, ALU.max), t, af["O"][x_])
                t = p.dve(lambda e: e.tensor_scalar(nm[x_], O[:, 512:516], -1.0, None, ALU.mult), t)
                for hh in range(4):
                    te = p.act(lambda e, hh=hh: e.activation(L3[:, hh, :], L3[:, hh, :], ACT.Exp, bias=nm[x_][:, hh:hh + 1], accum_out=O[:, 516 + hh:517 + hh]), t)
                kept[i] = (x_, L3, te)

            def values(i):
                qo, ko, nk, bo, parts = todo[i]
                x_, L3, te = kept.pop(i)
                T3 = ps[:, 2048:3072].rearrange("p (j n) -> p j n", j=8)
                np_ = len(parts)
                where = {}
                for hh in range(4):
                    for j, (ci, c0, n) in enumerate(parts):
                        where[hh, j] = 2 * hh + j if np_ <= 2 else None
                t = None
                for hh in range(4):
                    for j, (ci, c0, n) in enumerate(parts):
                        tp = p.pe(lambda e, hh=hh, j=j, c0=c0, n=n: e.transpose(T3[0:n, 2 * hh + j, :], L3[:, hh, c0:c0 + n], ident), te, af["T"])
                yield
                PT3 = PT[x_].rearrange("p (j n) -> p j n", j=8)
                t = []
                if all(n == 128 for _, _, n in parts) and np_ == 2:
                    t.append(p.act(lambda e: e.activation(PT3[:, 0:4, :], T3[:, 0:4, :], ACT.Copy), tp, af["PT"][x_]))
                    t.append(p.dve(lambda e: e.tensor_copy(PT3[:, 4:8, :], T3[:, 4:8, :]), tp, af["PT"][x_]))
                else:
                    for j, (ci, c0, n) in enumerate(parts):
                        ov = PT[x_].rearrange("p (h j n) -> p h j n", h=4, j=2)[0:n, :, j, :]
                        iv_ = ps[0:n, 2048:3072].rearrange("p (h j n) -> p h j n", h=4, j=2)[:, :, j, :]
                        if j == 0:
                            t.append(p.act(lambda e, ov=ov, iv_=iv_: e.activation(ov, iv_, ACT.Copy), tp, af["PT"][x_]))
                        else:
                            t.append(p.dve(lambda e, ov=ov, iv_=iv_: e.tensor_copy(ov, iv_), tp, t[0], af["PT"][x_]))
                af["T"] = t
                af["L"][x_] = tp
                yield
                UP = bank(6)
                for hh in range(4):
                    for j, (ci, c0, n) in enumerate(parts):
                        tp = p.pe(lambda e, hh=hh, j=j, ci=ci, n=n: e.matmul(UP[:, 128 * hh:128 * hh + 128], PT3[0:n, 2 * hh + j, :], Vt[0:n, ci, 128 * hh:128 * hh + 128], start=(j == 0), stop=(j == np_ - 1)), t, v_tok[g], af["U"])
                af["PT"][x_] = tp
                O = Ob[x_]
                t = p.act(lambda e: e.activation(O[:, 0:512], UP, ACT.Copy), tp, af["O"][x_])
                af["U"] = t
                r, l = divmod(qo, L)
                s0 = r + dil * l
                t = p.dma("sync", c_ob[x_], sc_b[g][s0:s0 + dil * 127 + 1:dil, :], O, t, te)
                af["O"][x_] = t
                ob_saved.append(t)
                yield

            logits(0)
            yield
            for i in range(len(todo)):
                if i + 1 < len(todo):
                    logits(i + 1)
                yield
                yield from values(i)
            qkfree[g % 2] = p.now("tensor")
            vfree[0] = p.now("tensor")
            vfree[1] = None

        for _ in chain(qk_proj(0), v_proj(0)):
            pass
        interleave((attend(0), 33), (qk_proj(1), 32))
        for _ in v_proj(1):
            pass
        interleave((attend(1), 33), (qk_proj(2), 32))
        for _ in v_proj(2):
            pass

        def combine_loads():
            for g in range(3):
                t = p.dma("sync", c_cb, CBt[g], sc_b[g].rearrange("(i p) n -> p i n", p=P), ob_saved, p2)
            return t

        mT = A(R + 8192, 8, 1024)
        gate_tok = {}

        def gate_a(cbs):
            for cb in cbs:
                place, tw = W.get()
                wv = place[0].rearrange("p (k n) -> p k n", k=8)
                for ct in range(2):
                    for hf in range(2):
                        b, bk, fr = gbank()
                        for kt in range(8):
                            tp = p.pe(lambda e, kt=kt, hf=hf, bk=bk, ct=ct, wv=wv: e.matmul(bk, wv[:, kt, 128 * ct:128 * ct + 128], hT[:, kt, 512 * hf:512 * hf + 512], start=(kt == 0), stop=(kt == 7)), tw, fr)
                            if kt % 4 == 3:
                                yield
                        dst = mT[:, 2 * cb + ct, 512 * hf:512 * hf + 512]
                        t = p.act(lambda e, bk=bk, dst=dst: e.activation(dst, bk, ACT.Tanh, scale=0.5), tp, qkfree[1])
                        tt["bk"][b] = t
                        gate_tok[2 * cb + ct, hf] = p.dve(lambda e, dst=dst: e.tensor_scalar(dst, dst, 0.5, 0.5, ALU.mult, ALU.add), t)
                W.release(place, tp)

        interleave((attend(2), 33), (gate_a(range(3)), 24))
        p2 = every()
        c_cb = p.channel("cb")
        c_oa = p.channel("oa")
        oT = A(R, 8, 1024)
        obT = A(R + 16384, 4, 1024)
        CB0 = R + 20480
        CBt = [A(CB0 + 4160 * i, 8, 520) for i in range(3)]
        gtmp = [A(CB0 + 12480 + 512 * i, 512) for i in range(2)]
        M4 = A(CB0 + 12480 + 1024, 8, 4)
        D4 = A(CB0 + 12480 + 1056, 8, 4)
        X4 = A(CB0 + 12480 + 1088, 8, 4)
        assert CB0 + 12480 + 1120 <= 52640
        t_oa = p.dma("sync", c_oa, oT, sc_o.rearrange("a p n -> p a n"), o_saved, p2)
        t_cb = combine_loads()
        for _ in gate_a([3]):
            pass
        obt_tok = []

        def combine():
            m = [CBt[g][:, :, 512:516] for g in range(3)]
            z = [CBt[g][:, :, 516:520] for g in range(3)]
            t = p.dve(lambda e: e.tensor_tensor(M4, m[0], m[1], ALU.max), t_cb)
            t = p.dve(lambda e: e.tensor_tensor(M4, M4, m[2], ALU.max), t)
            for g in range(3):
                t1 = p.dve(lambda e, g=g: e.tensor_tensor(m[g], m[g], M4, ALU.subtract), t)
                t1 = p.act(lambda e, g=g: e.activation(m[g], m[g], ACT.Exp), t1)
                t1 = p.dve(lambda e, g=g: e.tensor_tensor(z[g], z[g], m[g], ALU.mult), t1)
            t = p.dve(lambda e: e.tensor_tensor(D4, z[0], z[1], ALU.add), t1)
            t = p.dve(lambda e: e.tensor_tensor(D4, D4, z[2], ALU.add), t)
            t = p.dve(lambda e: e.reciprocal(D4, D4), t)
            yield
            for g in range(3):
                t1 = p.dve(lambda e, g=g: e.tensor_tensor(m[g], m[g], D4, ALU.mult), t)
            for i in range(8):
                u = [CBt[g][:, i, 0:512].rearrange("p (h n) -> p h n", h=4) for g in range(3)]
                sc = [m[g][:, i, :].rearrange("p (h n) -> p h n", n=1).to_broadcast([P, 4, 128]) for g in range(3)]
                ts = [p.dve(lambda e, g=g, u=u, sc=sc: e.tensor_tensor(u[g], u[g], sc[g], ALU.mult), t1) for g in range(2)]
                ts.append(p.pool(lambda e, u=u, sc=sc: e.tensor_tensor(u[2], u[2], sc[2], ALU.mult), t1))
                t2 = p.dve(lambda e, u=u: e.tensor_tensor(u[0], u[0], u[1], ALU.add), ts[1])
                t2 = p.dve(lambda e, u=u: e.tensor_tensor(u[0], u[0], u[2], ALU.add), t2, ts[2])
                yield
                bk = bank(7)
                for j in range(4):
                    tp = p.pe(lambda e, i=i, j=j: e.transpose(bk[:, 128 * j:128 * j + 128], CBt[0][:, i, 128 * j:128 * j + 128], ident), t2, fb[0])
                fb[0] = p.act(lambda e, i=i: e.activation(obT[:, :, 128 * i:128 * i + 128], bk.rearrange("p (j n) -> p j n", j=4), ACT.Copy), tp)
                yield
            obt_tok.append(fb[0])

        fb = [p2]
        nb = {"n": 0, "free": [(p2, tt["bk"][0]), (p2, tt["bk"][1]), p2, p2], "g": [p2, p2]}
        mt_tok = []

        def branch(second):
            src, nk, stok = (obT, 4, obt_tok) if second else (oT, 8, [t_oa])
            for cb in range(4):
                if second:
                    gw, t_gw = W.get()
                    gv = gw[0].rearrange("p (k n) -> p k n", k=8)
                bw, t_bw = W.get()
                bv = bw[0].rearrange("p (k n) -> p k n", k=8)
                for ct in range(2):
                    for hf in range(2):
                        s0, s1 = nb["n"] % 4, (nb["n"] + 1) % 4
                        nb["n"] += 2
                        x_ = (nb["n"] // 2) % 2
                        b0, b1 = bank(s0), bank(s1)
                        hs = slice(512 * hf, 512 * hf + 512)
                        if second:
                            for kt in range(8):
                                tg = p.pe(lambda e, kt=kt, b0=b0, gv=gv, ct=ct, hs=hs: e.matmul(b0, gv[:, kt, 128 * ct:128 * ct + 128], hT[:, kt, hs], start=(kt == 0), stop=(kt == 7)), t_gw, nb["free"][s0])
                            yield
                        for kt in range(nk):
                            tb = p.pe(lambda e, kt=kt, b1=b1, bv=bv, ct=ct, hs=hs: e.matmul(b1, bv[:, kt, 128 * ct:128 * ct + 128], src[:, kt, hs], start=(kt == 0), stop=(kt == nk - 1)), t_bw, nb["free"][s1], stok)
                        yield
                        g_ = gtmp[x_]
                        dst = mT[:, 2 * cb + ct, hs]
                        if second:
                            t = p.act(lambda e, b0=b0, g_=g_: e.activation(g_, b0, ACT.Tanh, scale=0.5), tg, nb["g"][x_])
                            nb["free"][s0] = t
                            t = p.dve(lambda e, g_=g_: e.tensor_scalar(g_, g_, 0.5, 0.5, ALU.mult, ALU.add), t)
                            t = p.dve(lambda e, g_=g_, b1=b1: e.tensor_tensor(g_, g_, b1, ALU.mult), t, tb)
                            nb["free"][s1] = t
                            t = nb["g"][x_] = p.dve(lambda e, g_=g_, dst=dst: e.tensor_tensor(dst, dst, g_, ALU.add), t)
                        else:
                            t = p.dve(lambda e, b1=b1, dst=dst: e.tensor_tensor(dst, dst, b1, ALU.mult), gate_tok[2 * cb + ct, hf], tb)
                            nb["free"][s1] = t
                if second:
                    W.release(gw, tg)
                W.release(bw, tb)
            mt_tok.append(t)

        interleave((branch(False), 16), (combine(), 18, 0.0, 1.0))
        if STOP == 2:
            return done(ar[:, R + 16384:R + 20480])
        for _ in branch(True):
            pass
        if STOP == 3:
            return done(ar[:, R + 8192:R + 16384])

        x1 = A(R, 8, 1024)
        YT = [A(R + 16384 + 1024 * i, 1024) for i in range(2)]
        lrow4 = A(R + 18432, 1024)
        JK4 = A(R + 19456, 1024)
        JKn = A(48704, 1024)
        p3 = every()
        W.keep = 2
        mrow = A(47680, 1024)
        c_row = p.channel("row")
        t_row = p.dma("sync", c_row, lrow4, lam["lnpost"].partition_broadcast(P), p3)
        t_x = [p.dma("sync", p.channel(f"xx{i}"), x1[:, i, :], x[0, 128 * i:128 * i + 128, :], p3) for i in range(8)]
        st4 = A(V0 + 168, 80)
        yb = {"free": [p3] * 4, "n": 0, "y": [p3, p3], "jk": p3, "jk2": p3, "tb": [p3, p3]}

        def out_rows(lhs, pl, i, deps):
            x_ = i % 2
            for cb in range(4):
                s_ = yb["n"] % 4
                yb["n"] += 1
                bk = bank(s_)
                wv = pl[cb][0][0].rearrange("p (k n) -> p k n", k=8)
                for kt in range(8):
                    tp = p.pe(lambda e, kt=kt, bk=bk, wv=wv: e.matmul(bk[:, 0:256], lhs[:, kt, 128 * i:128 * i + 128], wv[:, kt, :], start=(kt == 0), stop=(kt == 7)), pl[cb][1], deps, yb["free"][s_])
                if i == 7:
                    W.release(pl[cb][0], tp)
                ev = p.act(lambda e, cb=cb, bk=bk: e.activation(YT[x_][:, 256 * cb:256 * cb + 256], bk[:, 0:256], ACT.Copy), tp, yb["y"][x_])
                yb["free"][s_] = ev
            return ev

        def residual(i, src, tok, scol, *deps):
            st = st4[:, scol:scol + 1]
            t = p.act(lambda e: e.activation(JK4, src, ACT.Square, accum_out=st), tok, yb["jk"])
            yb["jk"] = t
            t = rstd(st, 1, 1.0 / 1024, t)
            t = p.dve(lambda e: e.scalar_tensor_tensor(out=src, in0=src, scalar=st, in1=lrow4, op0=ALU.mult, op1=ALU.mult), t, t_row)
            t = p.dve(lambda e: e.tensor_tensor(x1[:, i, :], x1[:, i, :], src, ALU.add), t, *deps)
            return t

        pl = [W.get() for _ in range(4)]
        h2 = (R_(0, 8, 1024), R_(39488, 8, 1024))
        t_mr = p.dma("sync", p.channel("mrow"), mrow, lam["lnmlp"].partition_broadcast(P), p3)
        c_sx = p.channel("sx")
        h2_tok = None
        pend = None
        t_sx = []

        def tail4(i, t):
            sl = slice(128 * i, 128 * i + 128)
            toks, yb["jk2"] = split_transposed(JKn, t, h2[0][:, :, sl], h2[1][:, :, sl], (4, 5), tuple(yb["tb"]))
            yb["tb"] = toks
            return toks[1]

        for i in range(8):
            ev = out_rows(mT, pl, i, p3)
            if pend is not None:
                h2_tok = tail4(*pend)
            t = residual(i, YT[i % 2], ev, i, t_x[i])
            yb["y"][i % 2] = t
            t_sx.append(p.dma("sync", c_sx, sc_x[0, 128 * i:128 * i + 128, :], x1[:, i, :], t))
            pend = (i, normed(x1[:, i, :], t, st4[:, 8 + i:9 + i], mrow, t_mr, JKn, yb["jk2"]))
        h2_tok = tail4(*pend)
        if STOP == 4:
            return done(ar[:, R:R + 8192])

        fT = [(R_(30720 + 4096 * i, 2, 1024), R_(32768 + 4096 * i, 2, 1024)) for i in range(2)]
        acc = A(R, 8, 1024)
        p4 = every()
        lrow = A(R + 10240, 1024)
        JK = A(R + 11264, 1024)
        t_row = p.dma("sync", c_row, lrow, lam["lnmlppost"].partition_broadcast(P), p4)
        SW = Split(p, W, [(R_(12288, SLOT), R_(14336, SLOT)), (R_(47680, SLOT), R_(49728, SLOT))], p4)
        FT = [A(26624 + 512 * i, 512) for i in range(4)]
        ftf = [p4] * 4
        bf = [p4] * 8
        ff_free = [p4, p4]
        acc_tok = {}
        f_tok = {}
        cn = {"a": 0, "b": 0}

        def ff1(c):
            q = c % 2
            hi, lo, k, tw = SW.get()
            wv = [x_.rearrange("p (k n) -> p k n", k=8) for x_ in (hi, lo)]
            for ct in range(2):
                for hf in range(2):
                    s_ = cn["a"] % 4
                    cn["a"] += 1
                    bk = bank(s_)
                    hs = slice(512 * hf, 512 * hf + 512)
                    for kt in range(8):
                        tp = mm3(bk, [w_[:, kt, 128 * ct:128 * ct + 128] for w_ in wv], [h_[:, kt, hs] for h_ in h2], kt == 0, kt == 7, tw, bf[s_], h2_tok)
                    ft = FT[s_]
                    fh, fl = fT[q][0][:, ct, hs], fT[q][1][:, ct, hs]
                    t = p.act(lambda e, bk=bk, ft=ft: e.activation(ft, bk, ACT.Relu), tp, ftf[s_])
                    bf[s_] = t
                    t = p.dve(lambda e, ft=ft: e.tensor_tensor(ft, ft, ft, ALU.mult), t)
                    t = p.act(lambda e, ft=ft, fh=fh: e.activation(fh, ft, ACT.Copy), t, ff_free[q])
                    t = p.dve(lambda e, ft=ft, fh=fh, fl=fl: e.tensor_tensor(fl, ft, fh.bitcast(F32), ALU.subtract), t, ff_free[q])
                    ftf[s_] = t
            SW.done(k, tp)
            f_tok[c] = t

        def ff2(c):
            q = c % 2
            hi, lo, k, tw = SW.get(c < 15)
            wv = [x_.rearrange("p (k n) -> p k n", k=2) for x_ in (hi, lo)]
            for i in range(8):
                for hf in range(2):
                    s_ = 4 + cn["b"] % 4
                    cn["b"] += 1
                    bk = bank(s_)
                    hs = slice(512 * hf, 512 * hf + 512)
                    for kt in range(2):
                        tp = mm3(bk, [f_[:, kt, 128 * i:128 * i + 128] for f_ in fT[q]], [w_[:, kt, hs] for w_ in wv], kt == 0, kt == 1, tw, bf[s_], f_tok[c])
                    dst = acc[:, i, hs]
                    if c == 0:
                        t = p.dve(lambda e, bk=bk, dst=dst: e.tensor_copy(dst, bk), tp, t_sx)
                    else:
                        t = p.dve(lambda e, bk=bk, dst=dst: e.tensor_tensor(dst, dst, bk, ALU.add), tp, acc_tok[i, hf])
                    bf[s_] = t
                    acc_tok[i, hf] = t
                if c == 15:
                    mlp_done(i, t)
            SW.done(k, tp)
            ff_free[q] = tp

        nrow = A(30720, 1024)
        XB = [A(31744 + 1024 * i, 1024) for i in range(2)]
        JK2 = A(33792, 1024)
        u = (R_(0, 8, 1024), R_(39488, 8, 1024))
        uTm = (R_(51776, 8, 16), R_(51904, 8, 16))
        c_xb = [p.channel(f"xb{i}") for i in range(2)]
        nx = {}
        x2_sx = []

        def start_norm():
            nx["f"] = p.now("tensor", "vector", "scalar")
            nx["row"] = p.dma("sync", p.channel("nrow"), nrow, lam["nw2"].partition_broadcast(P), nx["f"])
            nx["xbf"] = [nx["f"], nx["f"]]
            nx["jk"] = nx["f"]
            nx["tb"] = [[bf[0], bf[1]], [bf[2], bf[3]]]
            nx["x"] = {}
            for i in range(2):
                load_x1(i)

        def load_x1(i):
            nx["x"][i] = p.dma("sync", c_xb[i % 2], XB[i % 2], sc_x[0, 128 * i:128 * i + 128, :], nx["xbf"][i % 2], t_sx)

        def mlp_done(i, t):
            x_ = i % 2
            st = st4[:, 16 + i:17 + i]
            row = acc[:, i, :]
            t = p.act(lambda e: e.activation(JK, row, ACT.Square, accum_out=st), t, yb["jk"])
            yb["jk"] = t
            if i >= 2:
                split_x2(i - 2)
            t = rstd(st, 1, 1.0 / 1024, t)
            t = p.dve(lambda e: e.scalar_tensor_tensor(out=row, in0=row, scalar=st, in1=lrow, op0=ALU.mult, op1=ALU.mult), t, t_row)
            t = p.dve(lambda e: e.tensor_tensor(row, row, XB[x_], ALU.add), t, nx["x"][i])
            nx["xbf"][x_] = t
            if i + 2 < 8:
                load_x1(i + 2)
            x2_sx.append(p.dma("sync", c_sx, sc_x[1, 128 * i:128 * i + 128, :], row, t))
            nx["x2", i] = t
            if i >= 1:
                norm_x2(i - 1)

        def norm_x2(i):
            nx["n", i] = normed(acc[:, i, :], nx["x2", i], st4[:, 32 + i:33 + i], nrow, nx["row"], JK2, nx["jk"])

        def split_x2(i):
            x_ = i % 2
            sl = slice(128 * i, 128 * i + 128)
            toks, tp = split_transposed(JK2, nx["n", i], u[0][:, :, sl], u[1][:, :, sl], (2 * x_, 2 * x_ + 1), tuple(nx["tb"][x_]))
            nx["tb"][x_] = toks
            nx["jk"] = tp
            nx["tok"] = toks

        ff1(0)
        for c in range(16):
            if c < 15:
                ff1(c + 1)
            else:
                start_norm()
            ff2(c)
        split_x2(6)
        norm_x2(7)
        split_x2(7)
        if STOP == 5:
            return done(ar[:, R:R + 8192])

        p5 = every()
        Q0 = 26624
        mix = A(R, 8, 1024)
        c2 = p.channel("c2")
        mt = A(35000, 1024)
        mj = A(36024, 1024)
        t_mt = p.dma("sync", c2, mt[0:16, :], meta, p5)
        t = normed(mt[0:16, :], t_mt, st4[0:16, 24:25], nrow[0:16, :], nx["row"], mj[0:16, :], p5, n=16)
        toks, tp = split_transposed(mj[0:16, :], t, uTm[0], uTm[1], (6, 7), (p5, p5), n=16)
        t_um = toks
        t_u = nx["tok"]
        LW = 52032

        bt = {"n": 0, "free": [every()] * 8}

        def nbank(lo, n):
            s_ = lo + bt["n"] % n
            bt["n"] += 1
            return s_, bank(s_)

        def gemm_c(nslots, with_meta, each, first_ct=0):
            for sl in range(nslots):
                hi, lo, k, tw = SW.get()
                wv = [x_.rearrange("p (k n) -> p k n", k=8) for x_ in (hi, lo)]
                for ct in range(2):
                    pieces = [(u, 0, 512, 16), (u, 512, 512, 528)]
                    if with_meta:
                        pieces.insert(0, (uTm, 0, 16, 0))
                    for src, c0, n, pos in pieces:
                        s_, bk = nbank(0, 4)
                        for kt in range(8):
                            tp = mm3(bk[:, 0:n], [w_[:, kt, 128 * ct:128 * ct + 128] for w_ in wv], [x_[:, kt, c0:c0 + n] for x_ in src], kt == 0, kt == 7, tw, t_u, t_um, bt["free"][s_])
                        bt["free"][s_] = each(first_ct + 2 * sl + ct, pos, n, bk, tp)
                        yield
                SW.done(k, tp)

        T = 1040
        lwt = A(Q0 + 12544 - 1024, 8, 128)
        p6 = every()
        tz = p.pool(lambda e: e.memset(lwt, 0.0), p6)
        for g in range(2):
            for n in range(8):
                hlf = n % 2
                t_lw = p.dma("sync", c2, lwt[64 * hlf:64 * hlf + 64, 4 * g + n // 2, 64 * hlf:64 * hlf + 64], lruw[g, n], tz)
        c8 = st4[:, 40:44]
        c8b = st4[:, 44:48]
        Lc = vc[:, LRUL:LRUL + 4]
        t = p.act(lambda e: e.activation(c8b, Lc, ACT.Abs))
        t = p.act(lambda e: e.activation(c8b, c8b, ACT.Exp, scale=-1.0), t)
        t = p.act(lambda e: e.activation(c8b, c8b, ACT.Ln, bias=1.0), t)
        t = p.dve(lambda e: e.tensor_scalar(c8, Lc, -1.0, 0.0, ALU.mult, ALU.max), t)
        t = p.dve(lambda e: e.tensor_tensor(c8, c8, c8b, ALU.add), t)
        t = p.dve(lambda e: e.tensor_scalar(c8, c8, -8.0, None, ALU.mult), t)
        hb = st4[:, 48:56]
        t = p.dve(lambda e: e.tensor_scalar(hb[:, 0:4], vc[:, BR:BR + 4], -1.0, None, ALU.mult), t)
        t = p.dve(lambda e: e.tensor_scalar(hb[:, 4:8], vc[:, BI:BI + 4], 0.5, None, ALU.mult), t)
        t_c8 = t
        wc = 42
        LB = [[A(Q0 + 5220 * i + 1044 * j, 1044) for j in range(5)] for i in range(2)]
        lfree = [p6, p6]
        xl_t = {}

        def each_x(ct, pos, n, bk, tp):
            xl = LB[ct % 2][0]
            t = p.act(lambda e: e.activation(xl[:, 3 + pos:3 + pos + n], bk[:, 0:n], ACT.Copy), tp, lfree[ct % 2])
            xl_t[ct] = t
            return t

        lru_out = {}

        def lru(ct):
            xl, xc, r_, i_, a_ = LB[ct % 2]
            tz = p.pool(lambda e: e.memset(xl[:, 0:3], 0.0), lfree[ct % 2])
            cw2 = lam_cw[:, ct, :]
            t = p.dve(lambda e: e.tensor_scalar(xc[:, 0:T], xl[:, 0:T], cw2[:, 0:1], vc[:, CB + ct:CB + ct + 1], ALU.mult, ALU.add), xl_t[ct], tz, lfree[ct % 2], t_cw2)
            for j in range(1, 4):
                t = p.dve(lambda e, j=j: e.scalar_tensor_tensor(out=xc[:, 0:T], in0=xl[:, j:j + T], scalar=cw2[:, j:j + 1], in1=xc[:, 0:T], op0=ALU.mult, op1=ALU.add), t)
                yield
            ev = []
            for g, dst in ((0, r_), (1, i_)):
                for c0, n in ((0, 512), (512, 512), (1024, 16)):
                    s_ = 4 + bt["n4"] % 4
                    bt["n4"] += 1
                    bk = bank(s_)
                    tp = p.pe(lambda e, g=g, c0=c0, n=n, bk=bk: e.matmul(bk[:, 0:n], lwt[:, 4 * g + ct, :], xc[:, c0:c0 + n], start=True, stop=True), t, t_lw, bt["free"][s_])
                    tv = p.act(lambda e, g=g, c0=c0, n=n, bk=bk, dst=dst: e.activation(dst[:, c0:c0 + n], bk[:, 0:n], ACT.Exp if g == 0 else ACT.Tanh, scale=-1.0 if g == 0 else 0.5, bias=hb[:, 4 * g + ct:4 * g + ct + 1]), tp, lfree[ct % 2], t_c8)
                    bt["free"][s_] = tv
                    yield
            RR, I_, Aa, Xc, Xl = r_[:, 0:T], i_[:, 0:T], a_[:, 0:T], xc[:, 0:T], xl[:, 0:T]
            t1 = p.dve(lambda e: e.tensor_scalar(RR, RR, 1.0, None, ALU.add), tv)
            t1 = p.dve(lambda e: e.reciprocal(RR, RR), t1)
            ta = p.act(lambda e: e.activation(Aa, RR, ACT.Exp, scale=c8[:, ct:ct + 1]), t1, lfree[ct % 2])
            t1 = p.dve(lambda e: e.tensor_scalar(RR, RR, c8[:, ct:ct + 1], None, ALU.mult), ta)
            th = p.act(lambda e: e.activation(RR, RR, ACT.Tanh), t1)
            yield
            t2 = p.dve(lambda e: e.tensor_tensor(Xl, Aa, Aa, ALU.mult), ta)
            t2 = p.dve(lambda e: e.scalar_tensor_tensor(out=Xl, in0=Xl, scalar=1.0, in1=RR, op0=ALU.add, op1=ALU.mult), t2, th)
            tm_ = p.act(lambda e: e.activation(Xl, Xl, ACT.Sqrt, scale=-1.0), t2)
            yield
            t3 = p.dve(lambda e: e.tensor_scalar(I_, I_, 0.5, 0.5, ALU.mult, ALU.add), tv)
            t3 = p.dve(lambda e: e.tensor_tensor(I_, I_, Xc, ALU.mult), t3)
            t4 = p.dve(lambda e: e.memset(Xl[:, 0:1], 1.0), tm_)
            t3 = p.dve(lambda e: e.tensor_tensor(I_, I_, Xl, ALU.mult), t3, t4)
            t3 = p.dve(lambda e: e.tensor_tensor_scan(RR, Aa, I_, 0.0, ALU.mult, ALU.add), t3, th)
            yield
            while ct >= 2 and ("g", ct) not in lru_out:
                yield
            if ("g", ct) in lru_out:
                t3 = p.dve(lambda e: e.tensor_tensor(mix[:, 4 + ct, :], mix[:, 4 + ct, :], r_[:, 16:T], ALU.mult), t3, lru_out["g", ct])
            else:
                t3 = p.dve(lambda e: e.tensor_copy(mix[:, 4 + ct, :], r_[:, 16:T]), t3, p5)
            lfree[ct % 2] = t3
            lru_out[ct] = t3

        bt["n4"] = 0
        lam_cw = A(LW, 4, 4)
        t_cw2 = p.dma("sync", p.channel("cw2"), lam_cw, lam["cw2"], p6)
        GT = [A(Q0 + 12544 - 1024 - 1064 + 532 * i, 532)[:, 0:512] for i in range(2)]
        gfr = [p6, p6]

        def each_g(base):
            def f(ct, pos, n, bk, tp):
                x_ = (pos // 512) % 2
                hs = slice(pos - 16, pos - 16 + n)
                ta = p.act(lambda e: e.activation(GT[x_], bk, ACT.Tanh, scale=0.5), tp, gfr[x_])
                t = p.dve(lambda e: e.scalar_tensor_tensor(out=GT[x_], in0=GT[x_], scalar=1.0, in1=bk, op0=ALU.add, op1=ALU.mult), ta)
                dst = mix[:, base + ct, hs]
                if base == 4 and ct in lru_out:
                    t2 = p.dve(lambda e: e.scalar_tensor_tensor(out=dst, in0=GT[x_], scalar=0.5, in1=dst, op0=ALU.mult, op1=ALU.mult), t, lru_out[ct])
                else:
                    t2 = p.dve(lambda e: e.tensor_scalar(dst, GT[x_], 0.5, None, ALU.mult), t)
                    if base == 4 and pos == 528:
                        lru_out["g", ct] = t2
                gfr[x_] = t2
                return t
            return f

        def run(g):
            for _ in g:
                pass

        run(gemm_c(1, True, each_x))
        interleave((gemm_c(2, False, each_g(0)), 8), (lru(0), 12), (lru(1), 12, 0.1, 1.1))
        run(gemm_c(1, True, each_x, 2))
        interleave((gemm_c(2, False, each_g(4)), 8), (lru(2), 12), (lru(3), 12, 0.1, 1.0))
        if STOP == 6:
            return done(ar[:, R:R + 8192])

        p7 = every()
        qT = A(Q0, 4, 1024)
        kT = A(Q0 + 4096, 4, 1040)
        vO = Q0 + 8256
        cosT, sinT = A(vO, 1040), A(vO + 1040, 1040)
        rp = [A(vO + 2080 + 512 * i, 512) for i in range(2)]
        permT = A(vO + 3104, 128)
        lqk = A(vO + 3232, 256)
        c3 = p.channel("c3")
        t_r = p.dma("sync", c3, cosT, rope[0], p7)
        t_r = p.dma("sync", c3, sinT, rope[1], p7)
        t_r = p.dma("sync", c3, permT, rope[2][:, 0:128], p7)
        t_lq = p.dma("sync", p.channel("lq"), lqk, lam["lqk"].partition_broadcast(P), p7)
        lm = st4[:, 56:64]
        t = p.dve(lambda e: e.tensor_tensor(lqk[:, 0:64], lqk[:, 0:64], lqk[:, 64:128], ALU.mult), t_lq, t_r)
        t = p.dve(lambda e: e.tensor_tensor(lqk[:, 128:192], lqk[:, 128:192], lqk[:, 192:256], ALU.mult), t)
        t = p.dve(lambda e: e.tensor_reduce(lm[:, 0:1], lqk[:, 0:64], AX.X, ALU.add), t)
        t = p.dve(lambda e: e.tensor_reduce(lm[:, 1:2], lqk[:, 128:192], AX.X, ALU.add), t)
        t = p.act(lambda e: e.activation(lm[:, 0:2], lm[:, 0:2], ACT.Exp), t)
        t = p.dve(lambda e: e.tensor_tensor(lm[:, 2:3], lm[:, 1:2], lm[:, 0:1], ALU.subtract), t)
        LAM_INIT = float(0.8 - 0.6 * np.exp(0.0))
        t = p.dve(lambda e: e.tensor_scalar(lm[:, 2:3], lm[:, 2:3], LAM_INIT, None, ALU.subtract), t)
        t_lm = t
        rfree = [p7, p7]
        rk = {"n": 0}
        rt = {}

        def each_r(dst, key, shift):
            def f(ct, pos, n, bk, tp):
                x_ = rk["n"] % 2
                rk["n"] += 1
                tc = p.act(lambda e: e.activation(rp[x_][:, 0:n], bk[:, 0:n], ACT.Copy), tp, rfree[x_], p7)
                s_ = 4 + bt["n4"] % 4
                bt["n4"] += 1
                b2 = bank(s_)
                t2 = p.pe(lambda e: e.matmul(b2[:, 0:n], permT, rp[x_][:, 0:n], start=True, stop=True), tc, t_r, bt["free"][s_])
                d = dst[:, ct, pos - shift:pos - shift + n]
                t3 = p.dve(lambda e: e.tensor_tensor(d, b2[:, 0:n], sinT[:, pos:pos + n], ALU.mult), t2, p7, t_r)
                bt["free"][s_] = t3
                t4 = p.dve(lambda e: e.tensor_tensor(rp[x_][:, 0:n], rp[x_][:, 0:n], cosT[:, pos:pos + n], ALU.mult), t2)
                t5 = p.dve(lambda e: e.tensor_tensor(d, d, rp[x_][:, 0:n], ALU.add), t4)
                rfree[x_] = t5
                rt[key] = t5
                return tc
            return f

        run(gemm_c(2, True, each_r(kT, "k", 0)))
        run(gemm_c(2, False, each_r(qT, "q", 16)))
        p8 = every()
        vv = A(vO, 9, 512)
        for sl in range(2):
            hi, lo, k, tw = SW.get(sl == 0)
            wv = [x_.rearrange("p (k n) -> p k n", k=8) for x_ in (hi, lo)]
            for i in range(9):
                s_, bk = nbank(0, 4)
                n = 16 if i == 0 else 128
                for kt in range(8):
                    lh = [(m_[:, kt, :] if i == 0 else x_[:, kt, 128 * (i - 1):128 * i]) for m_, x_ in zip(uTm, u)]
                    tp = mm3(bk[0:n, 0:256], lh, [w_[:, kt, :] for w_ in wv], kt == 0, kt == 7, tw, bt["free"][s_])
                t_v = p.act(lambda e, i=i, n=n, bk=bk, sl=sl: e.activation(vv[0:n, i, 256 * sl:256 * sl + 256], bk[0:n, 0:256], ACT.Copy), tp, p8)
                bt["free"][s_] = t_v
            SW.done(k, tp)

        p9 = every()
        E0 = [A(1040 * i, 1040) for i in range(3)]
        E1 = [A(3120 + 1040 * i, 1040) for i in range(2)]
        WTb = [A(5200 + 1152 * i, 9, 128) for i in range(2)]
        o2 = [A(7504 + 128 * i, 128) for i in range(2)]
        jk2 = A(7760, 128)
        stat = [A(7888 + 8 * i, 8) for i in range(6)]
        negr = A(7936, 128)
        oner = A(8064, 64)
        tn = p.pool(lambda e: e.memset(negr[0:1, 0:64], NEG), p9)
        tn = p.pool(lambda e: e.memset(negr[0:1, 64:128], 0.0))
        tn = p.pool(lambda e: e.memset(oner[0:1, :], 1.0))
        bf = [p9] * 8
        e0f, e1f, stf, wf, of = [p9] * 3, [p9] * 2, [p9] * 6, [p9] * 2, [p9] * 2
        items = [(hh, i) for i in range(8) for hh in range(4)]
        kept = {}

        def scores(n):
            hh, i = items[n]
            nk = 16 + 128 * (i + 1)
            nb_ = 3 if i == 7 else 2
            st = stat[n % 6]
            lo = nk - 64
            for m in range(2):
                banks = range(nb_ * m, nb_ * m + nb_)
                SPm = ps[:, 512 * nb_ * m:512 * nb_ * m + nk]
                rows_ = slice(64 * m, 64 * m + 64)
                cuts = []
                for k0 in range(0, nk, 512):
                    k1 = min(k0 + 512, nk)
                    cuts += [(k0, k1)] if k1 <= lo or k0 >= lo else [(k0, lo), (lo, k1)]
                for k0, k1 in cuts:
                    last = k1 > lo
                    t = p.pe(lambda e, k0=k0, k1=k1, last=last, SPm=SPm, rows_=rows_: e.matmul(SPm[:, k0:k1], qT[rows_, hh, 128 * i:128 * i + 128], kT[rows_, hh, k0:k1], start=True, stop=not last), rt["k"], rt["q"], [bf[b_] for b_ in banks])
                    if last:
                        t = p.pe(lambda e, k0=k0, k1=k1, SPm=SPm: e.matmul(SPm[:, k0:k1], negr[0:1, :], oner[0:1, 0:k1 - k0], start=False, stop=True), tn)
                tm_ = p.dve(lambda e, m=m, SPm=SPm: e.tensor_reduce(st[:, m:m + 1], SPm, AX.X, ALU.max), t, stf[n % 6])
                tm_ = p.dve(lambda e, m=m: e.tensor_scalar(st[:, m:m + 1], st[:, m:m + 1], -0.125, None, ALU.mult), tm_)
                E = E0[n % 3] if m == 0 else E1[n % 2]
                te = p.act(lambda e, m=m, SPm=SPm, E=E: e.activation(E[:, 0:nk], SPm, ACT.Exp, scale=0.125, bias=st[:, m:m + 1], accum_out=st[:, 2 + m:3 + m]), tm_, e0f[n % 3] if m == 0 else e1f[n % 2])
                for b_ in banks:
                    bf[b_] = te
            kept[n] = te

        def weigh(n):
            hh, i = items[n]
            nk = 16 + 128 * (i + 1)
            st = stat[n % 6]
            a_, b_ = E0[n % 3][:, 0:nk], E1[n % 2][:, 0:nk]
            t = p.dve(lambda e: e.reciprocal(st[:, 4:6], st[:, 2:4]), kept[n])
            t = p.dve(lambda e: e.tensor_scalar(st[:, 5:6], st[:, 5:6], lm[:, 2:3], None, ALU.mult), t, t_lm)
            t = p.dve(lambda e: e.tensor_scalar(b_, b_, st[:, 5:6], None, ALU.mult), t)
            t = p.dve(lambda e: e.scalar_tensor_tensor(out=a_, in0=a_, scalar=st[:, 4:5], in1=b_, op0=ALU.mult, op1=ALU.add), t)
            e1f[n % 2] = t
            kept[n] = t

        o_tok = {}

        def turn_w(n):
            hh, i = items[n]
            te = kept.pop(n)
            E = E0[n % 3]
            WT_ = WTb[n % 2]
            blocks = [(0, 16, 0)] + [(16 + 128 * j, 128, j + 1) for j in range(i + 1)]
            tb = (6, 6) if i == 7 else (4, 5)
            evs = []
            for k, grp in enumerate([blocks[0:1]] + [blocks[a_:a_ + 4] for a_ in range(1, len(blocks), 4)]):
                n_ = grp[0][1]
                b_ = tb[k % 2]
                TB = bank(b_)
                for j, (c0, nn, bi) in enumerate(grp):
                    tp = p.pe(lambda e, j=j, c0=c0, nn=nn, TB=TB: e.transpose(TB[0:nn, 128 * j:128 * j + 128], E[:, c0:c0 + nn], ident), te, bf[b_])
                g_ = len(grp)
                w_ = WT_[0:n_, grp[0][2]:grp[0][2] + g_, :]
                v_ = TB[0:n_, 0:128 * g_].rearrange("p (g n) -> p g n", g=g_)
                t = p.act(lambda e, w_=w_, v_=v_: e.activation(w_, v_, ACT.Copy), tp, wf[n % 2])
                bf[b_] = t
                evs.append(t)
            e0f[n % 3] = tp
            kept["t", n] = evs

        def values(n):
            hh, i = items[n]
            blocks = [(0, 16, 0)] + [(16 + 128 * j, 128, j + 1) for j in range(i + 1)]
            WT_ = WTb[n % 2]
            evs = kept.pop(("t", n))
            ub = 7 if i == 7 else 6
            U = bank(ub)[:, 0:128]
            for j, (c0, nn, bi) in enumerate(blocks):
                tp = p.pe(lambda e, j=j, nn=nn, bi=bi: e.matmul(U, WT_[0:nn, bi, :], vv[0:nn, bi, 128 * hh:128 * hh + 128], start=(j == 0), stop=(j == len(blocks) - 1)), evs, bf[ub], t_v)
            wf[n % 2] = tp
            st = stat[n % 6]
            ot = o2[n % 2]
            t = p.act(lambda e: e.activation(ot, U, ACT.Copy), tp, of[n % 2])
            bf[ub] = t
            t1 = p.act(lambda e: e.activation(jk2, ot, ACT.Square, accum_out=st[:, 6:7]), t)
            t2 = p.dve(lambda e: e.tensor_scalar(st[:, 6:7], st[:, 6:7], 1.0 / 128, 1e-5, ALU.mult, ALU.add), t1)
            kept["o", n] = p.pool(lambda e: e.tensor_tensor(st[:, 6:7], st[:, 6:7], mh_t, ALU.pow), t2)

        def unit_o(n):
            st, ot = stat[n % 6], o2[n % 2]
            t2 = p.dve(lambda e: e.tensor_scalar(ot, ot, st[:, 6:7], 1.0 - LAM_INIT, ALU.mult, ALU.mult), kept.pop(("o", n)))
            stf[n % 6] = t2

        def turn(n):
            hh, i = items[n]
            ot = o2[n % 2]
            t2 = stf[n % 6]
            OT = bank(7)[:, 256:384]
            tp = p.pe(lambda e: e.transpose(OT, ot, ident), t2, bf[7])
            of[n % 2] = tp
            dst = mix[:, hh, 128 * i:128 * i + 128]
            bf[7] = p.dve(lambda e: e.scalar_tensor_tensor(out=dst, in0=OT, scalar=vc[:, SUB:SUB + 1], in1=dst, op0=ALU.mult, op1=ALU.mult), tp)

        N = len(items)
        scores(0)
        scores(1)
        weigh(0)
        for n in range(N):
            if n >= 2:
                unit_o(n - 2)
            if n + 2 < N:
                scores(n + 2)
            if n >= 2:
                turn(n - 2)
            if n + 1 < N:
                weigh(n + 1)
            turn_w(n)
            if n >= 1:
                values(n - 1)
        unit_o(N - 2)
        turn(N - 2)
        values(N - 1)
        unit_o(N - 1)
        turn(N - 1)
        if STOP == 7:
            return done(ar[:, R:R + 8192])

        p10 = every()
        YF = [A(12288 + 1024 * i, 1024) for i in range(2)]
        FR, JF = A(14336, 1024), A(15360, 1024)
        m2 = [[R_(b_ + 1024 * kt, 1024) for kt in range(8)] for b_ in (0, 39488)]
        FW = Split(p, W, [(R_(Q0 + 4096 * i, SLOT), R_(Q0 + 4096 * i + 2048, SLOT)) for i in range(3)] + [(R_(47680, SLOT), R_(49728, SLOT))], p10)
        XO = [A(Q0 + 12288, 512), A(51776, 512)]
        t_fr = p.dma("sync", c_row, FR, lam["fnorm"].partition_broadcast(P), p10)
        x2r = [p.dma("sync", p.channel(f"x2{i}"), YF[i], sc_x[1, 128 * i:128 * i + 128, :], p10, x2_sx) for i in range(2)]
        c_x2 = [t_[0] for t_ in x2r]
        FW.ahead()
        for kt in range(8):
            th = p.act(lambda e, kt=kt: e.activation(m2[0][kt], mix[:, kt, :], ACT.Copy), p10)
            t_m2 = p.dve(lambda e, kt=kt: e.tensor_tensor(m2[1][kt], mix[:, kt, :], m2[0][kt].bitcast(F32), ALU.subtract), th)
            if kt == 1:
                FW.ahead()
            if kt == 4:
                FW.ahead()
        FW.ahead()
        ws = [([x_.rearrange("p (k n) -> p k n", k=8) for x_ in (hi, lo)], tw) for hi, lo, k, tw in FW.ready]
        yf = [p10] * 4
        nb_ = 0
        c_out = [p.channel(f"out{i}") for i in range(2)]
        jf = None
        for i in range(8):
            x_ = i % 2
            for cb in range(4):
                s_ = nb_ % 4
                nb_ += 1
                bk = bank(s_)[:, 0:256]
                wv, tw = ws[cb]
                for kt in range(8):
                    tp = mm3(bk, [m_[kt][:, 128 * i:128 * i + 128] for m_ in m2], [w_[:, kt, :] for w_ in wv], kt == 0, kt == 7, tw, t_m2, yf[s_])
                ev = p.dve(lambda e, cb=cb, bk=bk, x_=x_: e.tensor_tensor(YF[x_][:, 256 * cb:256 * cb + 256], bk, YF[x_][:, 256 * cb:256 * cb + 256], ALU.add), tp, x2r[i])
                yf[s_] = ev
            st = st4[:, 64 + i:65 + i]
            t = p.act(lambda e, x_=x_, st=st: e.activation(JF, YF[x_], ACT.Square, accum_out=st), ev, jf)
            jf = t
            t = rstd(st, 1, 1.0 / 1024, t)
            t = p.dve(lambda e, x_=x_, st=st: e.scalar_tensor_tensor(out=YF[x_], in0=YF[x_], scalar=st, in1=FR, op0=ALU.mult, op1=ALU.mult), t, t_fr)
            t = p.dma("sync", c_out[x_], out[0, 128 * i:128 * i + 128, :], YF[x_], t)
            if i + 2 < 8:
                x2r.append(p.dma("sync", c_x2[x_], YF[x_], sc_x[1, 128 * (i + 2):128 * (i + 2) + 128, :], t))
        done()


def constants():
    f = np.float32
    i = np.arange(128)
    cst = np.zeros((128, 6, 128), f)
    cst[:, 0] = np.eye(128)
    cst[:, 1] = i[:, None] <= i[None, :]
    cst[:, 2] = i[:, None] >= i[None, :]
    cst[:, 3] = np.where(i[:, None] >= i[None, :], 0, BIG)
    cst[:, 4] = np.where(i[:, None] <= i[None, :], 0, BIG)
    cst[:, 5] = 1
    msk = np.zeros((128, 14, 128), np.float32)
    for n, b in enumerate(MASKS):
        m = (i[:, None] // (2 * b) == i[None, :] // (2 * b)) & ((i[:, None] // b) % 2 == 1) & ((i[None, :] // b) % 2 == 0)
        msk[:, 2 * n] = m
        msk[:, 2 * n + 1] = m.T
    oh = np.zeros((128, 3, 384), f)
    off = np.arange(384) - 191
    for g, dil in enumerate((1, 4, 8)):
        rel = off * dil
        n = np.abs(rel)
        large = 8 + (np.log(np.maximum(n, 1) / 8) / np.log(1024 / 8) * 8).astype(np.int32)
        bucket = (rel > 0) * 16 + np.where(n < 8, n, np.minimum(large, 15))
        ok = (np.abs(off) <= 64) if g < 2 else (off % 2 == 0) & (np.abs(off) <= 128)
        oh[bucket[ok], g, np.arange(384)[ok]] = 1
        oh[32, g, ~ok] = 1
    pos = np.arange(1040, dtype=f)
    inv = np.power(f(500000.0), -np.arange(0, 16, 2, dtype=f) / f(16)).astype(f)
    ang = pos[:, None] * inv[None, :]
    rope = np.zeros((3, 128, 1040), f)
    rope[0] = 1
    for b in range(2):
        for d in range(8):
            rope[0, 64 * b + d] = rope[0, 64 * b + 8 + d] = np.cos(ang[:, d])
            rope[1, 64 * b + d] = rope[1, 64 * b + 8 + d] = np.sin(ang[:, d])
            rope[2, 64 * b + 8 + d, 64 * b + d] = -1
            rope[2, 64 * b + d, 64 * b + 8 + d] = 1
    return cst.reshape(128, 768), msk, oh, rope


def stream(inp):
    w_in = inp["w_in"][0]

    def cols(w, *starts):
        n = 256 // len(starts)
        a = np.concatenate([w[:, s:s + n] for s in starts], axis=1)
        k = a.shape[0] // 128
        a = a.reshape(k, 128, 256).transpose(1, 0, 2).reshape(128, -1)
        if a.shape[1] < SLOT:
            a = np.concatenate([a, np.zeros((128, SLOT - a.shape[1]), a.dtype)], axis=1)
        return a

    s = []
    for h in range(8):
        s.append(cols(w_in, 128 * h, 2048 + 128 * h))
        s.append(cols(w_in, 1024 + 128 * h, 3072 + 128 * h))
    qb, kb, vb = 4128, 4128 + 1536, 4128 + 3072
    for g in range(3):
        for base in (qb, kb, vb):
            for j in range(2):
                s.append(cols(w_in, base + 512 * g + 256 * j))
    ga = vb + 1536
    gb = ga + 1024
    for j in range(4):
        s.append(cols(w_in, ga + 256 * j))
    for j in range(4):
        s.append(cols(inp["w_branch_a"][0], 256 * j))
    for j in range(4):
        s.append(cols(w_in, gb + 256 * j))
        s.append(cols(inp["w_branch_b"][0], 256 * j))
    for j in range(4):
        s.append(cols(inp["w_out"][0], 256 * j))
    w2 = inp["w_ff2"][0].reshape(16, 2, 128, 1024).transpose(0, 2, 1, 3).reshape(16, 128, 2048)
    s.append(cols(inp["w_ff1"][0], 0))
    for c in range(16):
        if c < 15:
            s.append(cols(inp["w_ff1"][0], 256 * (c + 1)))
        s.append(w2[c])
    wi = inp["w_in_2"][0]
    for c0 in (2048, 1536, 1792, 2304, 2560, 2816, 512, 768, 0, 256, 1024, 1280):
        s.append(cols(wi, c0))
    for j in range(4):
        s.append(cols(inp["w_out_2"][0], 256 * j))
    return np.ascontiguousarray(np.stack(s))


def kernel(**inputs):
    import concourse.bacc as _bacc
    from concourse.bass_utils import run_bass_kernel_spmd as _run

    inp = {k: np.asarray(v) for k, v in inputs.items()}
    nc = _bacc.Bacc("TRN2", target_bir_lowering=False, num_devices=1)
    arrays = {}

    def put(name, a):
        a = np.ascontiguousarray(a)
        arrays[name] = a
        return nc.dram_tensor(name, a.shape, mybir.dt.from_np(a.dtype), kind="ExternalInput").ap()

    def col(v):
        return v.reshape(-1, 128).T

    cst, msk, oh, rope = constants()
    w_in = inp["w_in"][0]
    wab = w_in[:, 4096:4128].reshape(8, 128, 32).transpose(1, 0, 2)
    cwt = inp["conv_w"][0].reshape(5, 24, 128).transpose(2, 1, 0)
    vecs = np.concatenate([
        col(inp["ln_mix_pre"][0]), col(inp["norm_a"][0]), col(inp["ln_mlp_pre"][0]), col(inp["norm_w_2"][0]),
        col(inp["subln_w_2"][0]), col(inp["conv_b_2"][0]), col(inp["b_rgate_2"][0]), col(inp["b_igate_2"][0]),
        col(inp["lru_L_2"][0])], axis=1)
    vecs = np.concatenate([vecs, np.zeros((128, 48 - vecs.shape[1]), vecs.dtype)], axis=1)
    gate = np.concatenate([inp["dt_bias_f"][0], inp["dt_bias_b"][0], inp["a_log_f"][0], inp["a_log_b"][0]])
    relb = np.concatenate([inp["rel_bias"], np.full((1, 12), NEG, np.float32), np.zeros((95, 12), np.float32)])
    lruw = np.stack([inp["w_rgate_2"][0], inp["w_igate_2"][0]])
    lqk = np.concatenate([inp["lambda_q1_2"][0], inp["lambda_k1_2"][0], inp["lambda_q2_2"][0], inp["lambda_k2_2"][0]])
    lam = {
        "lnpost": put("lnpost", inp["ln_mix_post"][0]), "lnmlppost": put("lnmlppost", inp["ln_mlp_post"][0]),
        "lnmlp": put("lnmlp", inp["ln_mlp_pre"][0]), "nw2": put("nw2", inp["norm_w_2"][0]),
        "fnorm": put("fnorm", inp["final_norm_w_2"]), "lqk": put("lqk", lqk),
        "cw2": put("cw2", inp["conv_w_2"][0].reshape(4, 4, 128).transpose(2, 1, 0)),
    }
    out = nc.dram_tensor("out", (1, 1024, 1024), F32, kind="ExternalOutput").ap()
    dbg = nc.dram_tensor("dbg", (128, 12288), F32, kind="ExternalOutput").ap() if STOP < 99 else None
    program(nc, put("x", inp["x"]), put("wst", stream(inp)), put("wab", wab), put("cwt", cwt), put("vecs", vecs),
            put("gate", gate), put("relb", relb), put("meta", inp["meta_tokens_2"]), lam, put("lruw", lruw),
            put("cst", cst), put("onehot", oh), put("rope", rope), put("msk", msk), out, dbg)
    r = _run(nc, [arrays], core_ids=[0])
    return r.results[0]["out"]
```
